# Optimizing a Trainium2 kernel written in Bass

```python
import jax, jax.numpy as jnp
from jax import lax
import numpy as np

D_MODEL = 1024
BATCH = 1
SEQ = 512
DEPTH = 1
DEC_BATCH = 8
DEC_SEQ = 4
PAST_LEN = 2048
PAGE_SIZE = 128

HEAD_DIM = 64
ROT_DIM = HEAD_DIM // 4
ROPE_THETA = 500000.0
H_A = 8
KV_A = 2
H_IDX = 8
D_IDX = 64
TOPK_IDX = 256
QBLK_A = 128
H_B = 8
MOBA_BLOCK = 256
TOPK_BLK = 3
QBLK_B = 32
N_GROUPS = 4
EXPERTS_PER_GROUP = 8
N_EXPERTS = N_GROUPS * EXPERTS_PER_GROUP
TOPK_EXPERT = 2
D_EXPERT = 256
MOE_BLK = 128
RMS_EPS = 1e-6
MIX_SPLIT = (H_A * HEAD_DIM, KV_A * HEAD_DIM, KV_A * HEAD_DIM, H_IDX * D_IDX, D_IDX, H_IDX,
             H_B * HEAD_DIM, H_B * HEAD_DIM, H_B * HEAD_DIM, D_MODEL, D_MODEL)
D_IN = sum(MIX_SPLIT)

kernel_name = 'dsa_moba_gated_hier_moe_step'

def rmsnorm(x, g):
    xf = x.astype(jnp.float32)
    r = lax.rsqrt(jnp.mean(xf * xf, axis=-1, keepdims=True) + RMS_EPS)
    return (xf * r).astype(x.dtype) * g

def rope_partial(x, pos):
    half = ROT_DIM // 2
    inv = ROPE_THETA ** (-jnp.arange(half, dtype=jnp.float32) / half)
    ang = pos.astype(jnp.float32)[:, None] * inv[None, :]
    cos = jnp.cos(ang)[:, None, :]
    sin = jnp.sin(ang)[:, None, :]
    xr = x[..., :ROT_DIM].astype(jnp.float32)
    x1, x2 = xr[..., :half], xr[..., half:]
    rot = jnp.concatenate([x1 * cos - x2 * sin, x2 * cos + x1 * sin], axis=-1)
    return jnp.concatenate([rot.astype(x.dtype), x[..., ROT_DIM:]], axis=-1)

def mixer_project(h, w_in, pos):
    B, T, _ = h.shape
    cuts = np.cumsum(MIX_SPLIT)[:-1].tolist()
    qa, ka, va, qi, ki, wi, qb, kb, vb, ga, gb = jnp.split(h @ w_in, cuts, axis=-1)
    qa = rope_partial(qa.reshape(B, T, H_A, HEAD_DIM), pos)
    ka = rope_partial(ka.reshape(B, T, KV_A, HEAD_DIM), pos)
    va = va.reshape(B, T, KV_A, HEAD_DIM)
    qi = rope_partial(qi.reshape(B, T, H_IDX, D_IDX), pos)
    ki = rope_partial(ki[:, :, None, :], pos)[:, :, 0]
    qb = rope_partial(qb.reshape(B, T, H_B, HEAD_DIM), pos)
    kb = rope_partial(kb.reshape(B, T, H_B, HEAD_DIM), pos)
    vb = vb.reshape(B, T, H_B, HEAD_DIM)
    return qa, ka, va, qi, ki, wi, qb, kb, vb, ga, gb

def gather_paged(pool, page_table, pos, *extra):
    b = jnp.arange(page_table.shape[0]).reshape((-1,) + (1,) * (pos.ndim - 1))
    phys = page_table[b, pos // PAGE_SIZE]
    return pool[(phys, pos % PAGE_SIZE) + extra]

def index_scores(qi, wi, ki, qpos, kpos):
    s = jax.nn.relu(jnp.einsum('bqhd,bsd->bqhs', qi, ki).astype(jnp.float32))
    w = wi.astype(jnp.float32) * (H_IDX ** -0.5 * D_IDX ** -0.5)
    score = jnp.einsum('bqhs,bqh->bqs', s, w)
    return jnp.where(kpos[None, None, :] <= qpos[None, :, None], score, -jnp.inf)

def sparse_gqa(q, k_sel, v_sel, valid):
    B, Q = q.shape[:2]
    qg = q.reshape(B, Q, KV_A, H_A // KV_A, HEAD_DIM)
    logits = jnp.einsum('bqgrd,bqkgd->bqgrk', qg, k_sel).astype(jnp.float32) * HEAD_DIM ** -0.5
    logits = jnp.where(valid[:, :, None, None, :], logits, -jnp.inf)
    p = jax.nn.softmax(logits, axis=-1).astype(v_sel.dtype)
    o = jnp.einsum('bqgrk,bqkgd->bqgrd', p, v_sel)
    return o.reshape(B, Q, H_A * HEAD_DIM)

def dsa_prompt(qa, ka, va, qi, ki, wi):
    B, T = qa.shape[:2]
    k_top = min(TOPK_IDX, T // 4)
    kpos = jnp.arange(T)
    bidx = jnp.arange(B)[:, None, None]

    def block(i):
        t0 = i * QBLK_A
        qpos = t0 + jnp.arange(QBLK_A)
        q_blk = lax.dynamic_slice_in_dim(qa, t0, QBLK_A, axis=1)
        qi_blk = lax.dynamic_slice_in_dim(qi, t0, QBLK_A, axis=1)
        wi_blk = lax.dynamic_slice_in_dim(wi, t0, QBLK_A, axis=1)
        score = index_scores(qi_blk, wi_blk, ki, qpos, kpos)
        _, idx = lax.top_k(score, k_top)
        valid = idx <= qpos[None, :, None]
        return sparse_gqa(q_blk, ka[bidx, idx], va[bidx, idx], valid)

    out = lax.map(block, jnp.arange(T // QBLK_A))
    return jnp.moveaxis(out, 0, 1).reshape(B, T, H_A * HEAD_DIM)

def dsa_sample(qa, ka_new, va_new, qi, ki_new, wi, pool_k, pool_v, pool_kidx, page_table):
    Bd, S = qa.shape[:2]
    k_top = min(TOPK_IDX, (PAST_LEN + S) // 4)
    qpos = PAST_LEN + jnp.arange(S)
    past_kidx = pool_kidx[page_table].reshape(Bd, PAST_LEN, D_IDX)
    score = jnp.concatenate([
        index_scores(qi, wi, past_kidx, qpos, jnp.arange(PAST_LEN)),
        index_scores(qi, wi, ki_new, qpos, PAST_LEN + jnp.arange(S))], axis=-1)
    _, idx = lax.top_k(score, k_top)
    valid = idx <= qpos[None, :, None]
    is_past = (idx < PAST_LEN)[..., None, None]
    past_idx = jnp.minimum(idx, PAST_LEN - 1)
    new_idx = jnp.clip(idx - PAST_LEN, 0, S - 1)
    bidx = jnp.arange(Bd)[:, None, None]
    k_sel = jnp.where(is_past, gather_paged(pool_k, page_table, past_idx), ka_new[bidx, new_idx])
    v_sel = jnp.where(is_past, gather_paged(pool_v, page_table, past_idx), va_new[bidx, new_idx])
    return sparse_gqa(qa, k_sel, v_sel, valid)

def block_attend(q, k_own, v_own, own_mask, k_sel=None, v_sel=None, sel_valid=None):
    B, Q = q.shape[:2]
    scale = HEAD_DIM ** -0.5
    s_own = jnp.einsum('bqhd,bkhd->bqhk', q, k_own).astype(jnp.float32) * scale
    s_own = jnp.where(own_mask[None, :, None, :], s_own, -jnp.inf)
    if k_sel is None:
        p = jax.nn.softmax(s_own, axis=-1).astype(v_own.dtype)
        o = jnp.einsum('bqhk,bkhd->bqhd', p, v_own)
    else:
        n_sel = k_sel.shape[3]
        n_flat = n_sel * MOBA_BLOCK
        s_sel = jnp.einsum('bqhd,bqhnkd->bqhnk', q, k_sel).astype(jnp.float32) * scale
        s_sel = jnp.where(sel_valid[..., None], s_sel, -jnp.inf).reshape(B, Q, H_B, n_flat)
        p = jax.nn.softmax(jnp.concatenate([s_sel, s_own], axis=-1), axis=-1).astype(v_own.dtype)
        p_sel = p[..., :n_flat].reshape(B, Q, H_B, n_sel, MOBA_BLOCK)
        o = (jnp.einsum('bqhk,bkhd->bqhd', p[..., n_flat:], v_own)
             + jnp.einsum('bqhnk,bqhnkd->bqhd', p_sel, v_sel))
    return o.reshape(B, Q, H_B * HEAD_DIM)

def moba_prompt(q, k, v):
    B, T = q.shape[:2]
    nb = -(-T // MOBA_BLOCK)
    pad = nb * MOBA_BLOCK - T
    kp = jnp.pad(k, ((0, 0), (0, pad), (0, 0), (0, 0)))
    vp = jnp.pad(v, ((0, 0), (0, pad), (0, 0), (0, 0)))
    n_cand = nb - 1
    n_sel = min(TOPK_BLK, n_cand)
    kmean = kp.reshape(B, nb, MOBA_BLOCK, H_B, HEAD_DIM)[:, :n_cand].astype(jnp.float32).mean(axis=2)
    bi = jnp.arange(B).reshape(B, 1, 1, 1, 1)
    hi = jnp.arange(H_B).reshape(1, 1, H_B, 1, 1)
    offs = jnp.arange(MOBA_BLOCK)

    def block(i):
        t0 = i * QBLK_B
        j = t0 // MOBA_BLOCK
        qb = lax.dynamic_slice_in_dim(q, t0, QBLK_B, axis=1)
        qpos = t0 + jnp.arange(QBLK_B)
        k_own = lax.dynamic_slice_in_dim(kp, j * MOBA_BLOCK, MOBA_BLOCK, axis=1)
        v_own = lax.dynamic_slice_in_dim(vp, j * MOBA_BLOCK, MOBA_BLOCK, axis=1)
        own_mask = (j * MOBA_BLOCK + offs)[None, :] <= qpos[:, None]
        if n_sel == 0:
            return block_attend(qb, k_own, v_own, own_mask)
        gate = jnp.einsum('bqhd,bnhd->bqhn', qb.astype(jnp.float32), kmean)
        gate = jnp.where(jnp.arange(n_cand) < j, gate, -jnp.inf)
        _, sel = lax.top_k(gate, n_sel)
        valid = sel < j
        pos_sel = sel[..., None] * MOBA_BLOCK + offs
        return block_attend(qb, k_own, v_own, own_mask, kp[bi, pos_sel, hi], vp[bi, pos_sel, hi], valid)

    out = lax.map(block, jnp.arange(T // QBLK_B))
    return jnp.moveaxis(out, 0, 1).reshape(B, T, H_B * HEAD_DIM)

def moba_sample(q, k_new, v_new, pool_k, pool_v, page_table):
    Bd, S = q.shape[:2]
    nbp = PAST_LEN // MOBA_BLOCK
    r = PAST_LEN % MOBA_BLOCK
    n_sel = min(TOPK_BLK, nbp)
    qpos = PAST_LEN + jnp.arange(S)
    qblk = qpos // MOBA_BLOCK
    if r > 0:
        tail_pos = jnp.broadcast_to(PAST_LEN - r + jnp.arange(r), (Bd, r))
        k_own = jnp.concatenate([gather_paged(pool_k, page_table, tail_pos), k_new], axis=1)
        v_own = jnp.concatenate([gather_paged(pool_v, page_table, tail_pos), v_new], axis=1)
    else:
        k_own, v_own = k_new, v_new
    own_pos = PAST_LEN - r + jnp.arange(r + S)
    own_mask = (own_pos[None, :] <= qpos[:, None]) & (own_pos[None, :] // MOBA_BLOCK == qblk[:, None])
    if n_sel == 0:
        return block_attend(q, k_own, v_own, own_mask)
    past_k = pool_k[page_table].reshape(Bd, PAST_LEN, H_B, HEAD_DIM)
    kmean = past_k[:, :nbp * MOBA_BLOCK].reshape(Bd, nbp, MOBA_BLOCK, H_B, HEAD_DIM).astype(jnp.float32).mean(axis=2)
    gate = jnp.einsum('bqhd,bnhd->bqhn', q.astype(jnp.float32), kmean)
    gate = jnp.where(jnp.arange(nbp)[None, None, None, :] < qblk[None, :, None, None], gate, -jnp.inf)
    _, sel = lax.top_k(gate, n_sel)
    valid = sel < qblk[None, :, None, None]
    pos_sel = sel[..., None] * MOBA_BLOCK + jnp.arange(MOBA_BLOCK)
    hi = jnp.arange(H_B).reshape(1, 1, H_B, 1, 1)
    k_sel = gather_paged(pool_k, page_table, pos_sel, hi)
    v_sel = gather_paged(pool_v, page_table, pos_sel, hi)
    return block_attend(q, k_own, v_own, own_mask, k_sel, v_sel, valid)

def merge_branches(o_a, o_b, ga, gb, w_br_a, w_br_b, w_out):
    u = jax.nn.sigmoid(ga) * (o_a @ w_br_a) + jax.nn.sigmoid(gb) * (o_b @ w_br_b)
    return u @ w_out

def moe_dispatch(x, idx, wts, w_gate, w_up, w_down):
    N, D = x.shape
    K = idx.shape[1]
    A = N * K
    flat_e = idx.reshape(A)
    flat_t = jnp.repeat(jnp.arange(N), K)
    flat_w = wts.reshape(A)
    order = jnp.argsort(flat_e)
    se = flat_e[order]
    counts = jnp.bincount(flat_e, length=N_EXPERTS)
    start = jnp.cumsum(counts) - counts
    padded = (counts + MOE_BLK - 1) // MOE_BLK * MOE_BLK
    pend = jnp.cumsum(padded)
    pstart = pend - padded
    dest = pstart[se] + jnp.arange(A) - start[se]
    n_blk = -(-A // MOE_BLK) + N_EXPERTS
    P = n_blk * MOE_BLK
    slot_t = jnp.full((P,), N, dtype=jnp.int32).at[dest].set(flat_t[order])
    slot_w = jnp.zeros((P,), dtype=flat_w.dtype).at[dest].set(flat_w[order])
    blk_e = jnp.minimum(jnp.searchsorted(pend, jnp.arange(n_blk) * MOE_BLK, side='right'), N_EXPERTS - 1)
    x_pad = jnp.concatenate([x, jnp.zeros((1, D), x.dtype)], axis=0)

    def run(args):
        t, e = args
        xb = x_pad[t]
        hdn = jax.nn.silu(xb @ w_gate[e]) * (xb @ w_up[e])
        return hdn @ w_down[e]

    yb = lax.map(run, (slot_t.reshape(n_blk, MOE_BLK), blk_e))
    y = jax.ops.segment_sum(yb.reshape(P, D) * slot_w[:, None], slot_t, num_segments=N + 1)[:N]
    return y.astype(x.dtype)

def hier_moe(h, w_grp, b_grp, w_exp, b_exp, w_e_gate, w_e_up, w_e_down):
    B, T, D = h.shape
    hf = h.reshape(B * T, D)
    N = hf.shape[0]
    gp = jax.nn.softmax((hf @ w_grp).astype(jnp.float32) + b_grp, axis=-1)
    gprob, gsel = lax.top_k(gp, 1)
    elog = ((hf @ w_exp).astype(jnp.float32) + b_exp).reshape(N, N_GROUPS, EXPERTS_PER_GROUP)
    elog_g = jnp.take_along_axis(elog, jnp.broadcast_to(gsel[:, :, None], (N, 1, EXPERTS_PER_GROUP)), axis=1)[:, 0]
    ep = jax.nn.softmax(elog_g, axis=-1)
    eprob, esel = lax.top_k(ep, TOPK_EXPERT)
    wts = gprob * eprob / jnp.sum(eprob, axis=-1, keepdims=True)
    idx = gsel * EXPERTS_PER_GROUP + esel
    return moe_dispatch(hf, idx, wts, w_e_gate, w_e_up, w_e_down).reshape(B, T, D)

def setup_inputs(seed: int = 0) -> dict:
    key = jax.random.key(seed)
    ks = jax.random.split(key, 24)
    n_pages = PAST_LEN // PAGE_SIZE
    n_pool = (DEC_BATCH * n_pages * 5) // 4
    nrm = jax.random.normal
    f32 = jnp.float32
    page_table = jax.random.permutation(ks[7], n_pool)[:DEC_BATCH * n_pages].reshape(DEC_BATCH, n_pages).astype(jnp.int32)
    return {
        'x_prompt': nrm(ks[0], (BATCH, SEQ, D_MODEL), f32),
        'x_sample': nrm(ks[1], (DEC_BATCH, DEC_SEQ, D_MODEL), f32),
        'cache_k_a': nrm(ks[2], (DEPTH, n_pool, PAGE_SIZE, KV_A, HEAD_DIM), f32),
        'cache_v_a': nrm(ks[3], (DEPTH, n_pool, PAGE_SIZE, KV_A, HEAD_DIM), f32),
        'cache_k_idx': nrm(ks[4], (DEPTH, n_pool, PAGE_SIZE, D_IDX), f32),
        'cache_k_b': nrm(ks[5], (DEPTH, n_pool, PAGE_SIZE, H_B, HEAD_DIM), f32),
        'cache_v_b': nrm(ks[6], (DEPTH, n_pool, PAGE_SIZE, H_B, HEAD_DIM), f32),
        'page_table': page_table,
        'w_in': nrm(ks[8], (DEPTH, D_MODEL, D_IN), f32) * D_MODEL ** -0.5,
        'w_br_a': nrm(ks[9], (DEPTH, H_A * HEAD_DIM, D_MODEL), f32) * (H_A * HEAD_DIM) ** -0.5,
        'w_br_b': nrm(ks[10], (DEPTH, H_B * HEAD_DIM, D_MODEL), f32) * (H_B * HEAD_DIM) ** -0.5,
        'w_out': nrm(ks[11], (DEPTH, D_MODEL, D_MODEL), f32) * D_MODEL ** -0.5,
        'g_mix': 1.0 + 0.01 * nrm(ks[12], (DEPTH, D_MODEL), f32),
        'g_ffn': 1.0 + 0.01 * nrm(ks[13], (DEPTH, D_MODEL), f32),
        'w_grp': nrm(ks[14], (DEPTH, D_MODEL, N_GROUPS), f32) * D_MODEL ** -0.5,
        'b_grp': 0.01 * nrm(ks[15], (DEPTH, N_GROUPS), f32),
        'w_exp': nrm(ks[16], (DEPTH, D_MODEL, N_EXPERTS), f32) * D_MODEL ** -0.5,
        'b_exp': 0.01 * nrm(ks[17], (DEPTH, N_EXPERTS), f32),
        'w_e_gate': nrm(ks[18], (DEPTH, N_EXPERTS, D_MODEL, D_EXPERT), f32) * D_MODEL ** -0.5,
        'w_e_up': nrm(ks[19], (DEPTH, N_EXPERTS, D_MODEL, D_EXPERT), f32) * D_MODEL ** -0.5,
        'w_e_down': nrm(ks[20], (DEPTH, N_EXPERTS, D_EXPERT, D_MODEL), f32) * D_EXPERT ** -0.5,
        'g_final': 1.0 + 0.01 * nrm(ks[21], (D_MODEL,), f32),
    }

def reference(x_prompt, x_sample, cache_k_a, cache_v_a, cache_k_idx, cache_k_b, cache_v_b, page_table,
              w_in, w_br_a, w_br_b, w_out, g_mix, g_ffn, w_grp, b_grp, w_exp, b_exp,
              w_e_gate, w_e_up, w_e_down, g_final):
    xp, xs = x_prompt, x_sample
    pos_p = jnp.arange(xp.shape[1])
    pos_s = PAST_LEN + jnp.arange(xs.shape[1])
    rows_p, rows_s = [], []
    for l in range(DEPTH):
        ffn_w = (w_grp[l], b_grp[l], w_exp[l], b_exp[l], w_e_gate[l], w_e_up[l], w_e_down[l])
        qa, ka, va, qi, ki, wi, qb, kb, vb, ga, gb = mixer_project(rmsnorm(xp, g_mix[l]), w_in[l], pos_p)
        o_a = dsa_prompt(qa, ka, va, qi, ki, wi)
        o_b = moba_prompt(qb, kb, vb)
        xp = xp + merge_branches(o_a, o_b, ga, gb, w_br_a[l], w_br_b[l], w_out[l])
        xp = xp + hier_moe(rmsnorm(xp, g_ffn[l]), *ffn_w)
        rows_p.append((ka, va, ki, kb, vb))
        qa, ka, va, qi, ki, wi, qb, kb, vb, ga, gb = mixer_project(rmsnorm(xs, g_mix[l]), w_in[l], pos_s)
        o_a = dsa_sample(qa, ka, va, qi, ki, wi, cache_k_a[l], cache_v_a[l], cache_k_idx[l], page_table)
        o_b = moba_sample(qb, kb, vb, cache_k_b[l], cache_v_b[l], page_table)
        xs = xs + merge_branches(o_a, o_b, ga, gb, w_br_a[l], w_br_b[l], w_out[l])
        xs = xs + hier_moe(rmsnorm(xs, g_ffn[l]), *ffn_w)
        rows_s.append((ka, va, ki, kb, vb))
    y_prompt = rmsnorm(xp, g_final)
    y_sample = rmsnorm(xs, g_final)
    k_a_p, v_a_p, k_idx_p, k_b_p, v_b_p = [jnp.stack([r[i] for r in rows_p]) for i in range(5)]
    k_a_s, v_a_s, k_idx_s, k_b_s, v_b_s = [jnp.stack([r[i] for r in rows_s]) for i in range(5)]
    return (y_prompt, y_sample, k_a_p, v_a_p, k_idx_p, k_b_p, v_b_p, k_a_s, v_a_s, k_idx_s, k_b_s, v_b_s)


_drawn_inputs = setup_inputs


def setup_inputs(seed=0):
    import zlib

    import numpy as np

    out = dict(_drawn_inputs(seed))
    spreads = {}
    factors = {'b_grp': 27.272, 'b_exp': 4.233, 'g_final': 30.141, 'g_mix': 2.82, 'g_ffn': 3.025}
    for name, (base, spread) in spreads.items():
        noise = np.random.default_rng([zlib.crc32(name.encode()), seed]).standard_normal(out[name].shape)
        drawn = base * np.exp(spread * noise) if base else spread * noise
        out[name] = __import__('jax').numpy.asarray(drawn.astype(out[name].dtype))
    for name, factor in factors.items():
        out[name] = (out[name] * factor).astype(out[name].dtype)
    return out
```

```python
from contextlib import ExitStack

import numpy as np

import concourse.bass as bass
from concourse import mybir

F32 = mybir.dt.float32
I32 = mybir.dt.int32
U32 = mybir.dt.uint32
ALU = mybir.AluOpType
ACT = mybir.ActivationFunctionType
AX = mybir.AxisListType

P = 128
D = 1024
KD = D // P
SEQ = 512
TP = SEQ // P
NB, NQ = 8, 4
SR = NB * NQ
TT = TP + 1
NTOK = SEQ + SR
PAST = 2048
PAGE = 128
NPG = PAST // PAGE
SLOT = 8
HPG = P * SLOT // PAGE
CH = 2 * SLOT
POOL = NB * NPG * 5 // 4
HD = 64
ROT = HD // 4
THETA = 500000.0
H = 8
PAIRS = H // 2
KVW = 2 * HD
QW = H * HD
TOPK_P = min(256, SEQ // 4)
TOPK_S = min(256, (PAST + NQ) // 4)
MBLK = 256
NBLK_PAST = PAST // MBLK
TOPB = 3
NG, EPG = 4, 8
NE = NG * EPG
DE = 256
EPS = 1e-6
SCALE = HD ** -0.5
IDX_SCALE = H ** -0.5 * HD ** -0.5
MASKED = -1e30
ABSENT = -3.0e38
PICKED = -3.39e38
EDGE = -3.2e38
DUMMY = 3.3e38
BLK = 64
MAXB = 2 * NTOK // BLK + NE
MAXB += MAXB % 2
TABW = 128

C_QA, C_KA, C_VA, C_QI = 0, 512, 640, 768
C_KI, C_WI, C_QB, C_KB, C_VB, C_GA = 1280, 1344, 1352, 1864, 2376, 2888
D_IN = 4936


def rows_of(t):
    return P if t < TP else SR


def const_pack():
    cols, at = [], {}

    def put(name, a):
        full = np.zeros((P, a.shape[1]), np.float32)
        full[:a.shape[0]] = a
        at[name] = (sum(c.shape[1] for c in cols), a.shape[1])
        cols.append(full)

    i = np.arange(P)
    put("ident", np.eye(P))
    put("causal", np.where(i[None, :] <= i[:, None], 0.0, MASKED))
    put("absent", np.where(i[None, :] <= i[:, None], 0.0, ABSENT))
    put("page_of", (i[:, None] // (P // HPG) == np.arange(HPG)[None, :]) * 1.0)
    put("within", (i[:, None] % (P // HPG)) * 1.0)
    row = np.arange(P)
    own = (row // 32 * NQ + row % NQ)[:, None]
    both = [(own + 4 * NQ * g == np.arange(SR)[None, :]) * 1.0 for g in range(2)]
    head = row // NQ % H
    put("gathered", np.concatenate(both, axis=1))
    put("spread", np.concatenate([x.T for x in both], axis=1))
    put("gathered_j", np.concatenate([x * (head % 4 == j)[:, None] for j in range(4) for x in both], axis=1))
    put("head_of", (head[:, None] == np.arange(H)[None, :]) * 1.0)
    put("own_b", (head[:, None] == np.arange(QW)[None, :] // HD) * 1.0)
    put("own_a", (head[:, None] // 4 == np.arange(KVW)[None, :] // HD) * 1.0)
    put("quarter", (i[:, None] // 32 == np.arange(4)[None, :]) * 1.0)
    put("before", (i[:, None] < i[None, :]) * 1.0)
    half = ROT // 2
    inv = np.float32(THETA) ** (-np.arange(half, dtype=np.float32) / np.float32(half))
    pos = np.concatenate([np.arange(SEQ), PAST + np.tile(np.arange(NQ), NB)])
    ang = (pos.astype(np.float32)[:, None] * inv.astype(np.float32)[None, :]).astype(np.float64)
    for name, f in (("cos", np.cos), ("sin", np.sin)):
        tab = np.zeros((TT * P, ROT), np.float32)
        tab[:NTOK] = np.tile(f(ang), (1, 2))
        put(name, tab.reshape(TT, P, ROT).transpose(1, 0, 2).reshape(P, TT * ROT))
    r = np.arange(SR)
    seen = (r[:, None] // NQ == r[None, :] // NQ) & (r[None, :] <= r[:, None])
    put("new_absent", np.where(seen, 0.0, ABSENT))
    for_rows = np.concatenate([np.where((x @ seen) > 0, 0.0, MASKED) for x in both], axis=1)
    put("new_masked", for_rows)
    put("blocks", np.tile(np.arange(MAXB, dtype=np.float32), (P, 1)))
    put("evens", np.tile(2.0 * np.arange(MAXB // 2, dtype=np.float32), (P, 1)))
    tok = np.arange(TT * P, dtype=np.float32).reshape(TT, P).T
    put("token", tok)
    put("real", (np.arange(TT * P).reshape(TT, P).T < NTOK) * 1.0)
    put("down", np.tile(np.arange(EPG, 0, -1, dtype=np.float32), (P, 1)))
    return np.concatenate(cols, axis=1), at


CONSTS, AT = const_pack()


class Chain:

    def __init__(self, eng, sem):
        self.eng, self.sem, self.n = eng, sem, {}
        self.turn, self.per = None, {}

    def loop(self, turn, per):
        self.turn, self.per = turn, {sem.name: k for sem, k in per}
        self.start = dict(self.n)

    def end_loop(self, turns):
        for name, k in self.per.items():
            got = self.n.get(name, 0) - self.start.get(name, 0)
            assert got == k, (name, got, k)
            self.n[name] = self.start.get(name, 0) + k * turns
        self.turn = None

    def __call__(self, ins, ready=None):
        sem = ready or self.sem
        ins.then_inc(sem, 1)
        n = self.n[sem.name] = self.n.get(sem.name, 0) + 1
        if self.turn is not None:
            assert sem.name in self.per, sem.name
            n = self.turn * self.per[sem.name] + n
        self.eng.wait_ge(sem, n)
        return ins


class State:
    pass


def const(s, name, rows=P):
    a, n = AT[name]
    return s.consts[0:rows, a:a + n]


def page_view(cache):
    return cache[0]


def build(nc, a, o):
    with ExitStack() as ctx:
        def sb(name, shape, dt=F32):
            return ctx.enter_context(nc.sbuf_tensor(name, shape, dt))

        s = State()
        s.consts = sb("consts", [P, CONSTS.shape[1]])
        s.ones = sb("ones", [P, P])
        s.rows = sb("rows", [P, 2 * NB], I32)
        s.hT = sb("hT", [P, KD, NTOK])
        s.kiT = sb("kiT", [P, NTOK])
        s.kaT = sb("kaT", [P, NTOK])
        s.qis = sb("qis", [SR, QW])
        s.va = sb("va", [P, TT, KVW])
        s.wi = sb("wi", [P, TT, H])
        s.bank = ctx.enter_context(nc.psum_tensor("bank", [P, 8, 512], F32))
        s.h2 = nc.dram_tensor("h2_rows", (NTOK, D), F32, kind="Internal").ap()
        s.slots = nc.dram_tensor("slot_table", (MAXB * BLK, TABW), I32, kind="Internal").ap()
        s.x1 = nc.dram_tensor("residual_rows", (NTOK, D), F32, kind="Internal").ap()
        s.y = nc.dram_tensor("expert_rows", (MAXB * BLK, D), F32, kind="Internal").ap()
        s.logit = sb("logit", [P, TT, NG + NE])
        with ExitStack() as attn:
            def sa(name, shape, dt=F32):
                return attn.enter_context(nc.sbuf_tensor(name, shape, dt))
            s.oaT = sa("oaT", [P, PAIRS, NTOK])
            s.obT = sa("obT", [P, PAIRS, NTOK])
            with ExitStack() as samp:
                def ss(name, shape, dt=F32):
                    return samp.enter_context(nc.sbuf_tensor(name, shape, dt))
                s.qaS, s.qbS = ss("qaS", [P, PAIRS, SR]), ss("qbS", [P, PAIRS, SR])
                s.qiS = ss("qiS", [P, PAIRS, SR])
                s.kbS, s.vbS = ss("kbS", [P, PAIRS, SR]), ss("vbS", [SR, QW])
                with ExitStack() as qkv:
                    def sq(name, shape, dt=F32):
                        return qkv.enter_context(nc.sbuf_tensor(name, shape, dt))
                    s.qaT = sq("qaT", [P, PAIRS, SEQ])
                    s.qiT = sq("qiT", [P, PAIRS, SEQ])
                    s.qbT = sq("qbT", [P, PAIRS, SEQ])
                    s.kbT = sq("kbT", [P, PAIRS, SEQ])
                    s.vb = sq("vb", [P, TP, QW])
                    with nc.cleanup_on_exit():
                        project(nc, s, a, o)
                        gather_rows(nc, s, a)
                        prompt(nc, s)
                s.newA = ss("newA", [P, NB // 4, SR])
                s.turned = ss("turned", [SR, P * SLOT])
                with nc.cleanup_on_exit():
                    sample(nc, s, a)
            with nc.cleanup_on_exit():
                merge(nc, s, a)
        s.w12 = sb("w12", [P, 2, TT])
        s.slot = sb("slot", [P, 2, TT], I32)
        s.be = sb("block_expert", [1, MAXB], I32)
        s.npair = sb("npair", [1, 1], I32)
        with nc.cleanup_on_exit():
            route(nc, s, a)
            experts(nc, s, a)
            combine(nc, s, a, o)


def project(nc, s, a, o):
    w_in = a["w_in"][0].rearrange("(k p) n -> p k n", p=P)
    GROUPS = ["kv", "qi", "qa", "kb", "qb", "vb"]
    COLS = {"kv": [(C_KA, 2 * KVW), (C_KI, HD + H)], "qi": [(C_QI, QW)], "qa": [(C_QA, QW)],
            "kb": [(C_KB, QW)], "qb": [(C_QB, QW)], "vb": [(C_VB, QW)]}
    WID = {g: sum(w for _, w in COLS[g]) for g in GROUPS}
    ITEMS = [(g, t) for g in GROUPS for t in range(TT)]
    NNAT = 3
    with ExitStack() as ctx:
        def sb(name, shape, dt=F32):
            return ctx.enter_context(nc.sbuf_tensor(name, shape, dt))

        def sem(name):
            return nc.alloc_semaphore(name)

        x = sb("x_pj", [P, TT, D])
        gmix = sb("gmix", [P, D])
        junk = sb("junk", [P, D])
        h = sb("h", [P, 2, D])
        ss = sb("ss", [P, TT])
        rr = sb("rr", [P, TT])
        w = sb("w", [P, 2, KD, 512])
        nat = sb("nat", [P, NNAT, 512])
        rt = sb("rt", [P, 2, H, ROT])
        zrow = sb("zrow", [P, 2 * TABW], I32)
        x_in = [sem(f"pj_x_in{t}") for t in range(TT)]
        c_in, g_in = sem("pj_consts_in"), sem("pj_g_in")
        w_in_s = [sem("pj_w_in0"), sem("pj_w_in1")]
        w_used = sem("pj_w_used")
        ss_ready, root_ready = sem("pj_ss_ready"), sem("pj_root_ready")
        ss_set = sem("pj_ss_set")
        h_ready, hT_done, hT_kept = sem("pj_h_ready"), sem("pj_hT_done"), sem("pj_hT_kept")
        proj_done, nat_ready = sem("pj_proj_done"), sem("pj_nat_ready")
        rot_ready, tr_done, tr_kept = sem("pj_rot_ready"), sem("pj_tr_done"), sem("pj_tr_kept")
        stored = [sem(f"pj_stored{i}") for i in range(NNAT)]
        vb_stored = sem("pj_vb_stored")
        zero_ready, zero_done = sem("pj_zero_ready"), sem("pj_zero_done")
        chain_v = sem("pj_vector_chain")
        block = ctx.enter_context(nc.Block())
        bank = s.bank
        natural = [n for n, (g, t) in enumerate(ITEMS) if g != "vb"]
        order = {n: i for i, n in enumerate(natural)}

        def nat_stores(upto, ring):
            return 16 * sum({"kv": 3, "kb": 1}.get(ITEMS[natural[i]][0], 0)
                            for i in range(ring, upto, NNAT))

        @block.sync
        def _(sp):
            sp.dma_start(s.consts[:, :], a["consts"]).then_inc(c_in, 16)
            for t in range(TP):
                sp.dma_start(x[:, t, :], a["x_prompt"][0, t * P:(t + 1) * P, :]).then_inc(x_in[t], 16)
            sp.dma_start(x[0:SR, TP, :], a["x_sample"].rearrange("b q d -> (b q) d")).then_inc(x_in[TP], 16)
            sp.dma_start(gmix[:, :], a["g_mix"].to_broadcast([P, D])).then_inc(g_in, 16)
            for gi, g in enumerate(GROUPS):
                if gi >= 2:
                    sp.wait_ge(w_used, gi - 1)
                at = 0
                for c, n in COLS[g]:
                    sp.dma_start(w[:, gi % 2, :, at:at + n], w_in[:, :, c:c + n]).then_inc(w_in_s[gi % 2], 16)
                    at += n

        def w_arrived(gi):
            return 16 * sum(len(COLS[GROUPS[k]]) for k in range(gi % 2, gi + 1, 2))

        @block.gpsimd
        def _(pool):
            nc.gpsimd.memset(s.ones[:, :], 1.0)
            nc.gpsimd.memset(zrow[:, :], 0).then_inc(zero_ready, 1)
            pool.wait_ge(zero_ready, 1)
            n = s.slots.shape[0] // P
            nz = 0
            for k in range(n):
                pool.dma_start(s.slots[k * P:(k + 1) * P, :], zrow[:, 0:TABW]).then_inc(zero_done, 16)
                nz += 1
            for n, (g, t) in enumerate(ITEMS):
                rows = rows_of(t)

                def out(name, c0, c1):
                    src = ((s.vb[:, t, :] if t < TP else s.vbS[:, :]) if g == "vb" else nat[0:rows, order[n] % NNAT, c0:c1])
                    sem_of = vb_stored if g == "vb" else stored[order[n] % NNAT]
                    if t < TP:
                        dst = o[name + "_p"][t * P:(t + 1) * P, :]
                    else:
                        dst = o[name + "_s"]
                    pool.dma_start(dst, src).then_inc(sem_of, 16)

                if g == "vb":
                    pool.wait_ge(nat_ready, n + 1)
                    out("v_b", 0, QW)
                elif g in ("kv", "kb"):
                    pool.wait_ge(rot_ready, order[n] + 1)
                    if g == "kv":
                        out("k_a", 0, KVW)
                        out("v_a", KVW, 2 * KVW)
                        out("k_idx", 2 * KVW, 2 * KVW + HD)
                    else:
                        out("k_b", 0, QW)
            pool.wait_ge(zero_done, 16 * nz)
            pool.wait_ge(vb_stored, 16 * TT)
            for i in range(NNAT):
                pool.wait_ge(stored[i], nat_stores(len(natural), i))

        @block.scalar
        def _(act):
            act.wait_ge(ss_set, 1)
            for t in range(TT):
                act.wait_ge(x_in[t], 16)
                rows = rows_of(t)
                nc.scalar.activation(junk[0:rows, :], x[0:rows, t, :], ACT.Square,
                                     accum_out=ss[0:rows, t:t + 1]).then_inc(ss_ready, 1)
                act.wait_ge(ss_ready, t + 1)
            act.wait_ge(root_ready, 1)
            nc.scalar.activation(ss[:, :], rr[:, :], ACT.Sqrt).then_inc(ss_ready, 1)

            def keep_hT(t):
                for c in range(2):
                    act.wait_ge(hT_done, 2 * t + c + 1)
                    nc.scalar.copy(s.hT[:, 4 * c:4 * c + 4, t * P:t * P + rows_of(t)],
                                   bank[:, 4 + c, :].rearrange("p (k r) -> p k r", k=4)[:, :, 0:rows_of(t)])\
                        .then_inc(hT_kept, 1)

            def keep_transposed(n):
                g, t = ITEMS[n]
                r, c = rows_of(t), slice(t * P, t * P + rows_of(t))
                act.wait_ge(tr_done, order[n] + 1)
                tb = bank[:, 4 + order[n] % 2, :].rearrange("p (k r) -> p k r", k=4)
                if g == "kv":
                    nc.scalar.copy(s.kaT[:, c], tb[:, 0, 0:r])
                    nc.scalar.copy(s.kiT[:, c], tb[:, 1, 0:r]).then_inc(tr_kept, 1)
                else:
                    dst = ({"qi": s.qiT, "qa": s.qaT, "qb": s.qbT, "kb": s.kbT}[g][:, :, c] if t < TP else
                           {"qi": s.qiS, "qa": s.qaS, "qb": s.qbS, "kb": s.kbS}[g][:, :, :])
                    nc.scalar.copy(dst, tb[:, :, 0:r]).then_inc(tr_kept, 1)

            for t in range(TT):
                keep_hT(t)
            for n, (g, t) in enumerate(ITEMS):
                rows = rows_of(t)
                act.wait_ge(proj_done, n + 1)
                if g == "vb":
                    nc.scalar.copy(s.vb[:, t, :] if t < TP else s.vbS[:, :], bank[0:rows, n % 4, :]).then_inc(nat_ready, 1)
                else:
                    i = order[n]
                    if i >= NNAT:
                        act.wait_ge(tr_done, i - NNAT + 1)
                        if nat_stores(i, i % NNAT):
                            act.wait_ge(stored[i % NNAT], nat_stores(i, i % NNAT))
                    dst, src = nat[0:rows, i % NNAT, 0:WID[g]], bank[0:rows, n % 4, 0:WID[g]]
                    if g == "qa":
                        dst = dst.rearrange("p (j a d) -> p a j d", a=2, d=HD)
                        src = src.rearrange("p (a j d) -> p a j d", a=2, d=HD)
                    nc.scalar.copy(dst, src).then_inc(nat_ready, 1)
                if n >= 1 and n - 1 in order:
                    keep_transposed(n - 1)
            if len(ITEMS) - 1 in order:
                keep_transposed(len(ITEMS) - 1)

        @block.vector
        def _(dve):
            link = Chain(dve, chain_v)
            nc.vector.memset(ss[:, :], 1.0).then_inc(ss_set, 1)
            dve.wait_ge(ss_ready, TT)
            nc.vector.tensor_scalar(rr[:, :], ss[:, :], 1.0 / D, EPS, ALU.mult, ALU.add).then_inc(root_ready, 1)
            dve.wait_ge(ss_ready, TT + 1)
            link(nc.vector.reciprocal(rr[:, :], ss[:, :]))
            dve.wait_ge(g_in, 16)
            for t in range(TT):
                rows = rows_of(t)
                if t >= 2:
                    dve.wait_ge(hT_done, 2 * (t - 1))
                nc.vector.scalar_tensor_tensor(h[0:rows, t % 2, :], x[0:rows, t, :], rr[0:rows, t:t + 1],
                                               gmix[0:rows, :], ALU.mult, ALU.mult).then_inc(h_ready, 1)
            for n in natural:
                g, t = ITEMS[n]
                rows, i = rows_of(t), order[n]
                dve.wait_ge(nat_ready, n + 1)
                b = nat[0:rows, i % NNAT, :]
                spans = [(0, H)]
                if g == "kv":
                    link(nc.vector.tensor_copy(s.va[0:rows, t, :], b[:, KVW:2 * KVW]))
                    link(nc.vector.tensor_scalar(s.wi[0:rows, t, :], b[:, 2 * KVW + HD:2 * KVW + HD + H],
                                                 IDX_SCALE, None, ALU.mult))
                    spans = [(0, 2), (2 * KVW, 1)]
                for c0, nh in spans:
                    v = b[:, c0:c0 + nh * HD].rearrange("p (h d) -> p h d", d=HD)
                    xr = v[:, :, 0:ROT]
                    cos = const(s, "cos", rows)[:, t * ROT:(t + 1) * ROT].unsqueeze(1).to_broadcast([rows, nh, ROT])
                    sin = const(s, "sin", rows)[:, t * ROT:(t + 1) * ROT].unsqueeze(1).to_broadcast([rows, nh, ROT])
                    rc, rs = rt[0:rows, 0, 0:nh, :], rt[0:rows, 1, 0:nh, :]
                    hf = ROT // 2
                    nc.vector.tensor_tensor(rc, xr, cos, ALU.mult)
                    link(nc.vector.tensor_tensor(rs, xr, sin, ALU.mult))
                    nc.vector.tensor_tensor(v[:, :, 0:hf], rc[:, :, 0:hf], rs[:, :, hf:ROT], ALU.subtract)
                    final = g != "kv" and not (g == "qi" and t == TP)
                    link(nc.vector.tensor_tensor(v[:, :, hf:ROT], rc[:, :, hf:ROT], rs[:, :, 0:hf], ALU.add),
                         rot_ready if final else None)
                if g == "qi" and t == TP:
                    link(nc.vector.tensor_copy(s.qis[:, :], b), rot_ready)
                if g == "kv":
                    src = b[:, 2 * KVW:2 * KVW + HD].unsqueeze(1).to_broadcast([rows, 2, HD])
                    link(nc.vector.tensor_copy(b[:, 384:512].rearrange("p (a d) -> p a d", a=2), src), rot_ready)

        @block.tensor
        def _(pe):
            pe.wait_ge(c_in, 16)
            ident = const(s, "ident")
            for t in range(TT):
                rows = rows_of(t)
                pe.wait_ge(h_ready, t + 1)
                for c in range(2):
                    if t >= 1:
                        pe.wait_ge(hT_kept, 2 * t + c - 1)
                    for k in range(4):
                        kk = 4 * c + k
                        last = nc.tensor.transpose(bank[:, 4 + c, k * P:k * P + rows],
                                                   h[0:rows, t % 2, kk * P:(kk + 1) * P], ident[0:rows, 0:rows])
                    last.then_inc(hT_done, 1)
            pe.wait_ge(hT_kept, 2 * TT)

            def transposes(n):
                g, t = ITEMS[n]
                rows, i = rows_of(t), order[n]
                pe.wait_ge(rot_ready, i + 1)
                if i >= 2:
                    pe.wait_ge(tr_kept, i - 1)
                b = nat[0:rows, i % NNAT, :]
                if g == "kv":
                    src = [b[:, 0:P], b[:, 384:512]]
                else:
                    src = [b[:, j * P:(j + 1) * P] for j in range(PAIRS)]
                for j, part in enumerate(src):
                    last = nc.tensor.transpose(bank[:, 4 + i % 2, j * P:j * P + rows], part, ident[0:rows, 0:rows])
                last.then_inc(tr_done, 1)

            for n, (g, t) in enumerate(ITEMS):
                gi, rows = GROUPS.index(g), rows_of(t)
                if t == 0:
                    pe.wait_ge(w_in_s[gi % 2], w_arrived(gi))
                if n >= 4:
                    pe.wait_ge(nat_ready, n - 3)
                for k in range(KD):
                    last = nc.tensor.matmul(bank[0:rows, n % 4, 0:WID[g]], s.hT[:, k, t * P:t * P + rows],
                                            w[:, gi % 2, k, 0:WID[g]], start=(k == 0), stop=(k == KD - 1))
                last.then_inc(proj_done, 1)
                if t == TT - 1:
                    pe.wait_ge(proj_done, n + 1)
                    pe.sem_inc(w_used, 1)
                if n >= 1 and n - 1 in order:
                    transposes(n - 1)
            if len(ITEMS) - 1 in order:
                transposes(len(ITEMS) - 1)


def topk_round(link, scores, best):
    link(nc_max(link, best, scores))
    link(nc_replace(link, scores, best))


def nc_max(link, best, scores):
    return link.eng.max(best, scores)


def nc_replace(link, scores, best):
    return link.eng.match_replace(scores, best, scores, PICKED)


def prompt(nc, s):
    IDX = [(t, h) for t in (1, 2, 3) for h in range(H)]
    ITEMS = [("b", t, h) for t in range(TP) for h in range(H)] + [("a", t, h) for t in range(TP) for h in range(H)]
    ROUNDS = [(t, r) for t in (1, 2, 3) for r in range(TOPK_P // 8)]
    EARLY = TP * H
    with ExitStack() as ctx:
        def sb(name, shape, dt=F32):
            return ctx.enter_context(nc.sbuf_tensor(name, shape, dt))

        def sem(name):
            return nc.alloc_semaphore(name)

        score = sb("score", [P, TP, SEQ])
        relu = sb("relu", [P, 2, SEQ])
        best = sb("best", [P, 8])
        prob = sb("prob", [P, 3, SEQ])
        probT = sb("probT", [P, 2, SEQ])
        top = sb("top", [P, 4])
        ntop = sb("ntop", [P, 4])
        total = sb("total", [P, 4])
        inv = sb("inv", [P, 4])
        idx_done, relu_done, acc_done = sem("pr_idx_done"), sem("pr_relu_done"), sem("pr_acc_done")
        qk_done, top_done, exp_done = sem("pr_qk_done"), sem("pr_top_done"), sem("pr_exp_done")
        norm_done, tr_done, tr_kept = sem("pr_norm_done"), sem("pr_tr_done"), sem("pr_tr_kept")
        pv_done, o_kept, chain_v = sem("pr_pv_done"), sem("pr_o_kept"), sem("pr_vector_chain")
        bank = s.bank
        block = ctx.enter_context(nc.Block())

        def width(t):
            return (t + 1) * P

        def place(kind, h):
            return (h // PAIRS, h % PAIRS) if kind == "a" else (h % 2, h // 2)

        @block.tensor
        def _(pe):
            ident = const(s, "ident")
            for q, (t, h) in enumerate(IDX):
                if q >= 3:
                    pe.wait_ge(relu_done, q - 2)
                r = slice(h % 2 * HD, h % 2 * HD + HD)
                nc.tensor.matmul(bank[:, q % 3, 0:width(t)], s.qiT[r, h // 2, t * P:(t + 1) * P],
                                 s.kiT[r, 0:width(t)], start=True, stop=True).then_inc(idx_done, 1)
            pe.wait_ge(relu_done, len(IDX))

            def scores(m):
                kind, t, h = ITEMS[m]
                half, pair = place(kind, h)
                r = slice(half * HD, half * HD + HD)
                if m >= 3:
                    pe.wait_ge(exp_done, m - 2)
                qT = s.qaT if kind == "a" else s.qbT
                kT = s.kaT[r, 0:width(t)] if kind == "a" else s.kbT[r, pair, 0:width(t)]
                nc.tensor.matmul(bank[:, m % 3, 0:width(t)], qT[r, pair, t * P:(t + 1) * P], kT,
                                 start=True, stop=True).then_inc(qk_done, 1)

            def turn(m):
                kind, t, h = ITEMS[m]
                pe.wait_ge(norm_done, m + 1)
                if m >= 2:
                    pe.wait_ge(tr_kept, m - 1)
                for c in range(t + 1):
                    last = nc.tensor.transpose(bank[:, 3 + m % 2, c * P:(c + 1) * P],
                                               prob[:, m % 3, c * P:(c + 1) * P], ident)
                last.then_inc(tr_done, 1)

            def weigh(m):
                kind, t, h = ITEMS[m]
                half, pair = place(kind, h)
                pe.wait_ge(tr_kept, m + 1)
                if m >= 2:
                    pe.wait_ge(o_kept, m - 1)
                for c in range(t + 1):
                    v = s.va[:, c, half * HD:(half + 1) * HD] if kind == "a" else s.vb[:, c, h * HD:(h + 1) * HD]
                    last = nc.tensor.matmul(bank[half * HD:(half + 1) * HD, 5 + m % 2, 0:P], v,
                                            probT[:, m % 2, c * P:(c + 1) * P], start=(c == 0), stop=(c == t))
                last.then_inc(pv_done, 1)

            n = len(ITEMS)
            for m in range(n + 3):
                if m < n:
                    scores(m)
                if 2 <= m < n + 2:
                    turn(m - 2)
                if m >= 3:
                    weigh(m - 3)

        @block.scalar
        def _(act):
            for q, (t, h) in enumerate(IDX):
                act.wait_ge(idx_done, q + 1)
                if q >= 2:
                    act.wait_ge(acc_done, q - 1)
                nc.scalar.activation(relu[:, q % 2, 0:width(t)], bank[:, q % 3, 0:width(t)], ACT.Relu)\
                    .then_inc(relu_done, 1)

            def exps(m):
                _, t, _ = ITEMS[m]
                act.wait_ge(top_done, m + 1)
                if m >= 3:
                    act.wait_ge(tr_done, m - 2)
                nc.scalar.activation(prob[:, m % 3, 0:width(t)], bank[:, m % 3, 0:width(t)], ACT.Exp,
                                     bias=ntop[:, m % 4:m % 4 + 1], scale=SCALE,
                                     accum_out=total[:, m % 4:m % 4 + 1]).then_inc(exp_done, 1)

            def keep_turned(m):
                _, t, _ = ITEMS[m]
                act.wait_ge(tr_done, m + 1)
                if m >= 2:
                    act.wait_ge(pv_done, m - 1)
                nc.scalar.copy(probT[:, m % 2, 0:width(t)], bank[:, 3 + m % 2, 0:width(t)]).then_inc(tr_kept, 1)

            def keep_o(m):
                kind, t, h = ITEMS[m]
                half, pair = place(kind, h)
                r = slice(half * HD, half * HD + HD)
                act.wait_ge(pv_done, m + 1)
                nc.scalar.copy((s.oaT if kind == "a" else s.obT)[r, pair, t * P:(t + 1) * P],
                               bank[r, 5 + m % 2, 0:P]).then_inc(o_kept, 1)

            n = len(ITEMS)
            for m in range(n + 3):
                if m < n:
                    exps(m)
                if 2 <= m < n + 2:
                    keep_turned(m - 2)
                if m >= 3:
                    keep_o(m - 3)

        @block.vector
        def _(dve):
            link = Chain(dve, chain_v)
            for q, (t, h) in enumerate(IDX):
                w = slice(0, width(t))
                dve.wait_ge(relu_done, q + 1)
                if h == 0:
                    link(nc.vector.tensor_scalar(score[:, t, w], relu[:, q % 2, w], s.wi[:, t, 0:1], None,
                                                 ALU.mult), acc_done)
                else:
                    link(nc.vector.scalar_tensor_tensor(score[:, t, w], relu[:, q % 2, w], s.wi[:, t, h:h + 1],
                                                        score[:, t, w], ALU.mult, ALU.add), acc_done)
                if h == H - 1:
                    d = slice(t * P, (t + 1) * P)
                    link(nc.vector.tensor_tensor(score[:, t, d], score[:, t, d], const(s, "absent"), ALU.add))

            def topk(r):
                t, k = ROUNDS[r]
                sc = score[:, t, 0:width(t)]
                topk_round(link, sc, best[:, :])
                if k == TOPK_P // 8 - 1:
                    link(nc.vector.tensor_scalar(sc, sc, EDGE, MASKED, ALU.is_gt, ALU.mult))

            def tops(m):
                kind, t, h = ITEMS[m]
                dve.wait_ge(qk_done, m + 1)
                if kind == "a" and t > 0:
                    w, bias = slice(0, width(t)), score[:, t, 0:width(t)]
                else:
                    w, bias = slice(t * P, (t + 1) * P), const(s, "causal")
                link(nc.vector.tensor_tensor(bank[:, m % 3, w], bank[:, m % 3, w], bias, ALU.add))
                link(nc.vector.reduce_max(top[:, m % 4:m % 4 + 1], bank[:, m % 3, 0:width(t)], AX.X))
                link(nc.vector.tensor_scalar(ntop[:, m % 4:m % 4 + 1], top[:, m % 4:m % 4 + 1], -SCALE, None,
                                             ALU.mult), top_done)

            def normalise(m):
                _, t, _ = ITEMS[m]
                dve.wait_ge(exp_done, m + 1)
                link(nc.vector.reciprocal(inv[:, m % 4:m % 4 + 1], total[:, m % 4:m % 4 + 1]))
                link(nc.vector.tensor_scalar(prob[:, m % 3, 0:width(t)], prob[:, m % 3, 0:width(t)],
                                             inv[:, m % 4:m % 4 + 1], None, ALU.mult), norm_done)

            n = len(ITEMS)
            for m in range(n + 1):
                if m < n:
                    tops(m)
                if m >= 1:
                    normalise(m - 1)
                if m < EARLY:
                    for r in range(m * len(ROUNDS) // EARLY, (m + 1) * len(ROUNDS) // EARLY):
                        topk(r)



def gather_rows(nc, s, a):
    with ExitStack() as ctx:
        table = ctx.enter_context(nc.sbuf_tensor("table", [P, NB * NPG], I32))
        tabf = ctx.enter_context(nc.sbuf_tensor("tabf", [P, 2 * NB, HPG], F32))
        rowf = ctx.enter_context(nc.sbuf_tensor("rowf", [P, 2 * NB], F32))
        table_in = nc.alloc_semaphore("gr_table_in")
        chain_v = nc.alloc_semaphore("gr_vector_chain")
        block = ctx.enter_context(nc.Block())

        @block.sync
        def _(sp):
            sp.dma_start(table[:, :], a["page_table"].rearrange("b g -> (b g)").unsqueeze(0)
                         .to_broadcast([P, NB * NPG])).then_inc(table_in, 16)

        @block.vector
        def _(dve):
            link = Chain(dve, chain_v)
            dve.wait_ge(table_in, 16)
            mine = const(s, "page_of")[:, 0:HPG].unsqueeze(1).to_broadcast([P, 2 * NB, HPG])
            link(nc.vector.tensor_copy(tabf[:, :, :].rearrange("p b g -> p (b g)"), table[:, :]))
            link(nc.vector.tensor_tensor(tabf[:, :, :], tabf[:, :, :], mine, ALU.mult))
            link(nc.vector.reduce_sum(rowf[:, :], tabf[:, :, :], AX.X))
            link(nc.vector.tensor_scalar(rowf[:, :], rowf[:, :], float(P // HPG), const(s, "within"),
                                         ALU.mult, ALU.add))
            link(nc.vector.tensor_copy(s.rows[:, :], rowf[:, :]))


def sample(nc, s, a):
    COLS = PAST + SR
    G = NB // 4
    HALF = P * SLOT
    QUADS = [("i", b, f, 0) for b in range(NB) for f in range(2)]
    QUADS += [("b", b, f, e) for b in range(NB) for f in range(2) for e in range(2)]
    QUADS += [("a", b, f, e) for b in range(NB) for f in range(2) for e in range(2)]
    LOTS = []
    for k, (kind, *_) in enumerate(QUADS):
        LOTS += [(k, n) for n in range(4 if kind == "b" else 1)]
    LAST = {k: n for n, (k, _) in enumerate(LOTS)}
    RES = [(k, n) for k, (kind, *_) in enumerate(QUADS) for n in range(2 if kind == "i" else 1)]
    NIDX = 2 * len([q for q in QUADS if q[0] == "i"])
    with ExitStack() as ctx:
        def sb(name, shape, dt=F32):
            return ctx.enter_context(nc.sbuf_tensor(name, shape, dt))

        def sem(name):
            return nc.alloc_semaphore(name)

        RI, RB, RA = 2, 3, 3
        ring = {"i": sb("half_i", [P, RI, SLOT * HD]), "b": sb("half_b", [P, RB, SLOT * QW]),
                "a": sb("half_a", [P, RA, SLOT * KVW])}
        kT = sb("kT_s", [P, 2, PAIRS, 4, P])
        qdup = sb("qdup", [SR, H, 2, HD])
        q_i = sb("q_i", [P, NB, 32])
        q_b = sb("q_b", [P, NB, PAIRS, 32])
        q_a = sb("q_a", [P, NB, 32])
        wrow = sb("wrow", [P, G, H])
        lg = {"i": sb("lg_i", [P, G, COLS]), "b": sb("lg_b", [P, G, COLS])}
        lg["a"] = lg["i"]
        row = sb("row", [SR, COLS])
        best = sb("best_s", [P, 8])
        gate = sb("gate", [P, 2 * NBLK_PAST])
        top = sb("top_s", [P, 4])
        ntop = sb("ntop_s", [P, 4])
        total = sb("total_s", [P, 4])
        inv = sb("inv_s", [P, 4])
        probT = sb("probT_s", [P, CH, P])
        newT = sb("newT_s", [SR, P])
        o = {"b": sb("o_b", [P, G, QW]), "a": sb("o_a", [P, G, KVW])}
        in_i = [sem(f"sm_i_in{r}") for r in range(RI)]
        in_b = [sem(f"sm_b_in{r}") for r in range(RB)]
        in_a = [sem(f"sm_a_in{r}") for r in range(RA)]
        arrived = {"i": in_i, "b": in_b, "a": in_a}
        dup_ready, dupT_done, w_done, q_ready = sem("sm_dup"), sem("sm_dupT"), sem("sm_w_done"), sem("sm_q_ready")
        tr_done, kT_kept, qk_done, res_done = sem("sm_tr_done"), sem("sm_kT_kept"), sem("sm_qk_done"), sem("sm_res_done")
        idx_read, s_kept = sem("sm_idx_read"), sem("sm_s_kept")
        new_done, row_done, row_kept = sem("sm_new_done"), sem("sm_row_done"), sem("sm_row_kept")
        bias_ready, spread_done, spread_read = sem("sm_bias_ready"), sem("sm_spread_done"), sem("sm_spread_read")
        top_done, exp_done, norm_done = sem("sm_top_done"), sem("sm_exp_done"), sem("sm_norm_done")
        pT_done, pT_kept, pv_done, o_read = sem("sm_pT_done"), sem("sm_pT_kept"), sem("sm_pv_done"), sem("sm_o_read")
        oT_done, newT_done, chain_v = sem("sm_oT_done"), sem("sm_newT_done"), sem("sm_vector_chain")
        all_read = sem("sm_all_read")
        bank = s.bank
        TB, SB, XB = (0, 1, 2), (3, 4), (5, 6)
        NEWB = 7
        block = ctx.enter_context(nc.Block())
        SOFT = [("b", 0), ("b", 1), ("a", 0), ("a", 1)]
        caches = {"i": a["cache_k_idx"][0].rearrange("g (p e) d -> (g p) (e d)", e=SLOT)}
        for k, (kk, vv) in {"b": ("cache_k_b", "cache_v_b"), "a": ("cache_k_a", "cache_v_a")}.items():
            caches[k], caches["v" + k] = (a[n][0].rearrange("g (p e) h d -> (g p) (e h d)", e=SLOT)
                                          for n in (kk, vv))

        def half_of(k):
            _, b, f, _ = QUADS[k]
            return 2 * b + f

        def rows_at(b):
            return slice(b % 4 * 32, b % 4 * 32 + 32)

        def col0(r):
            k, n = RES[r]
            kind, b, f, e = QUADS[k]
            return f * HALF + (n if kind == "i" else e) * 512

        @block.gpsimd
        def _(pool):
            def gather(kind, cache, h, seen):
                r = (seen + h) % len(arrived[kind])
                pool.indirect_dma_start(ring[kind][:, r, :], None, caches[cache],
                                        bass.IndirectOffsetOnAxis(s.rows[:, h:h + 1], 0))\
                    .then_inc(arrived[kind][r], 16)

            first = {kind: min(n for n, (k, _) in enumerate(LOTS) if QUADS[k][0] == kind) for kind in "iba"}
            per = {kind: sum(1 for k, _ in LOTS if QUADS[k][0] == kind) // (2 * NB) for kind in "iba"}
            for kind in "iba":
                n = len(arrived[kind])
                for h in range(2 * NB):
                    if h >= n:
                        pool.wait_ge(tr_done, first[kind] + per[kind] * (h - n + 1))
                    gather(kind, kind, h, 0)
            for x, kind in enumerate("ba"):
                n = len(arrived[kind])
                for h in range(2 * NB):
                    if h < n:
                        pool.wait_ge(tr_done, first[kind] + per[kind] * (2 * NB - n + h + 1))
                    else:
                        pool.wait_ge(pv_done, x * 2 * NB + h - n + 1)
                    gather(kind, "v" + kind, h, 2 * NB)

        @block.tensor
        def _(pe):
            ident = const(s, "ident")
            pe.wait_ge(dup_ready, 1)
            for h in range(H):
                last = nc.tensor.transpose(bank[:, XB[0], h * SR:(h + 1) * SR],
                                           qdup[:, h, :, :].rearrange("r a d -> r (a d)"), ident[0:SR, 0:SR])
            last.then_inc(dupT_done, 1)
            for g in range(G):
                last = nc.tensor.matmul(bank[:, XB[1], g * H:(g + 1) * H], const(s, "spread", SR)[:, g * P:(g + 1) * P],
                                        s.wi[0:SR, TP, :], start=True, stop=True)
            last.then_inc(w_done, 1)
            pe.wait_ge(q_ready, 1)
            for b in range(NB):
                out = bank[rows_at(b), NEWB, b // 4 * 96:b // 4 * 96 + 96]
                nc.tensor.matmul(out[:, 0:32], q_i[0:HD, b, :], s.kiT[0:HD, SEQ:NTOK], start=True, stop=True)
                for j in range(PAIRS):
                    nc.tensor.matmul(out[:, 32:64], q_b[:, b, j, :], s.kbS[:, j, :],
                                     start=(j == 0), stop=(j == PAIRS - 1))
                last = nc.tensor.matmul(out[:, 64:96], q_a[:, b, :], s.kaT[:, SEQ:NTOK], start=True, stop=True)
            last.then_inc(new_done, 1)

            def turn(n):
                k, i = LOTS[n]
                kind, b, f, e = QUADS[k]
                h = half_of(k)
                r = h % len(arrived[kind])
                if i == 0 and e == 0:
                    pe.wait_ge(arrived[kind][r], 16 * (h // len(arrived[kind]) + 1))
                if n >= 3:
                    pe.wait_ge(kT_kept, n - 2)
                for j in range(4):
                    at = (4 * e + i) * QW + j * P if kind == "b" else (4 * e + j) * P
                    last = nc.tensor.transpose(bank[:, TB[n % 3], j * P:(j + 1) * P],
                                               ring[kind][:, r, at:at + P], ident)
                last.then_inc(tr_done, 1)

            def scores(k):
                kind, b, f, e = QUADS[k]
                pe.wait_ge(kT_kept, LAST[k] + 1)
                for n in range(2 if kind == "i" else 1):
                    r = RES.index((k, n))
                    if 2 <= r < NIDX + 2:
                        pe.wait_ge(idx_read, r - 1)
                    elif r >= 2:
                        pe.wait_ge(s_kept, r - NIDX - 1)
                    out = bank[rows_at(b), SB[r % 2], :]
                    if kind == "i":
                        d = slice(n * HD, n * HD + HD)
                        last = nc.tensor.matmul(out, q_i[d, b, :], kT[d, k % 2, 0, :, :].rearrange("d e p -> d (e p)"),
                                                start=True, stop=True)
                    elif kind == "a":
                        last = nc.tensor.matmul(out, q_a[:, b, :], kT[:, k % 2, 0, :, :].rearrange("d e p -> d (e p)"),
                                                start=True, stop=True)
                    else:
                        for j in range(PAIRS):
                            last = nc.tensor.matmul(out, q_b[:, b, j, :],
                                                    kT[:, k % 2, j, :, :].rearrange("d e p -> d (e p)"),
                                                    start=(j == 0), stop=(j == PAIRS - 1))
                    last.then_inc(res_done, 1)
                pe.wait_ge(res_done, RES.index((k, n)) + 1)
                pe.sem_inc(qk_done, 1)

            def index_rows():
                pe.wait_ge(all_read, 1)
                for c in range(5):
                    w = 512 if c < 4 else SR
                    if c >= 2:
                        pe.wait_ge(row_kept, c - 1)
                    for g in range(G):
                        last = nc.tensor.matmul(bank[0:SR, XB[c % 2], 0:w], const(s, "gathered")[:, g * SR:(g + 1) * SR],
                                                lg["i"][:, g, c * 512:c * 512 + w], start=(g == 0), stop=(g == G - 1))
                    last.then_inc(row_done, 1)

            for n in range(len(LOTS)):
                k, i = LOTS[n]
                turn(n)
                if n == LAST[k] and k >= 1:
                    scores(k - 1)
                    if k - 1 == NIDX // 2 - 1:
                        index_rows()
            scores(len(QUADS) - 1)

            def spread(g):
                pe.wait_ge(bias_ready, 1)
                for c in range(5):
                    w = 512 if c < 4 else SR
                    n = 5 * g + c
                    if n >= 2:
                        pe.wait_ge(spread_read, n - 1)
                    nc.tensor.matmul(bank[:, XB[n % 2], 0:w], const(s, "spread", SR)[:, g * P:(g + 1) * P],
                                     row[:, c * 512:c * 512 + w], start=True, stop=True).then_inc(spread_done, 1)

            for m, (x, g) in enumerate(SOFT):
                pe.wait_ge(norm_done, m + 1)
                pe.wait_ge(s_kept, len(RES) - NIDX)
                for c in range(4):
                    n = 4 * m + c
                    if n >= 3:
                        pe.wait_ge(pT_kept, n - 2 + (n - 3) // 4)
                    for j in range(4):
                        at = (4 * c + j) * P
                        last = nc.tensor.transpose(bank[:, TB[n % 3], j * P:(j + 1) * P], lg[x][:, g, at:at + P], ident)
                    last.then_inc(pT_done, 1)
                nc.tensor.transpose(bank[0:SR, NEWB, 0:P], lg[x][:, g, PAST:COLS], ident).then_inc(newT_done, 1)
                if m + 1 < len(SOFT) and SOFT[m + 1][0] == "a":
                    spread(SOFT[m + 1][1])
                pe.wait_ge(pT_kept, 5 * (m + 1))
                for b in range(4 * g, 4 * g + 4):
                    n = (x == "a") * NB + b
                    if n >= 2:
                        pe.wait_ge(o_read, n - 1)
                    w = QW if x == "b" else KVW
                    out = bank[rows_at(b), SB[n % 2], 0:w]
                    for f in range(2):
                        h = 2 * b + f
                        v = h + 2 * NB
                        nr = len(arrived[x])
                        pe.wait_ge(arrived[x][v % nr], 16 * (v // nr + 1))
                        for e in range(SLOT):
                            last = nc.tensor.matmul(out, probT[:, f * SLOT + e, rows_at(b)],
                                                    ring[x][:, v % nr, e * w:(e + 1) * w],
                                                    start=(f == 0 and e == 0), stop=False)
                        if f == 0:
                            last.then_inc(pv_done, 1)
                    last = nc.tensor.matmul(out, newT[:, rows_at(b)], s.vbS[:, :] if x == "b" else s.va[0:SR, TP, :],
                                            start=False, stop=True)
                    last.then_inc(pv_done, 1)
            for x in "ba":
                pe.wait_ge(o_read, 2 * NB)
                for j in range(PAIRS):
                    for g in range(G):
                        lhsT = o["b"][:, g, j * P:(j + 1) * P] if x == "b" else o["a"][:, g, :]
                        pick = (const(s, "gathered")[:, g * SR:(g + 1) * SR] if x == "b" else
                                const(s, "gathered_j")[:, (j * G + g) * SR:(j * G + g + 1) * SR])
                        last = nc.tensor.matmul(bank[:, XB[x == "a"], j * SR:(j + 1) * SR], lhsT, pick,
                                                start=(g == 0), stop=(g == G - 1))
            last.then_inc(oT_done, 1)

        @block.scalar
        def _(act):
            def keep_lot(n):
                k, i = LOTS[n]
                kind = QUADS[k][0]
                act.wait_ge(tr_done, n + 1)
                if i == 0 and k >= 2:
                    act.wait_ge(qk_done, k - 1)
                src = bank[:, TB[n % 3], :].rearrange("p (j n) -> p j n", j=4)
                dst = kT[:, k % 2, :, i, :] if kind == "b" else kT[:, k % 2, 0, :, :]
                nc.scalar.copy(dst, src).then_inc(kT_kept, 1)

            def keep_scores(k):
                kind, b, f, e = QUADS[k]
                if kind == "i":
                    return
                r = RES.index((k, 0))
                act.wait_ge(res_done, r + 1)
                if kind == "a" and (b, f, e) == (0, 0, 0):
                    act.wait_ge(row_done, 5)
                nc.scalar.copy(lg[kind][rows_at(b), b // 4, col0(r):col0(r) + 512], bank[rows_at(b), SB[r % 2], :])\
                    .then_inc(s_kept, 1)

            for n in range(len(LOTS)):
                k, i = LOTS[n]
                keep_lot(n)
                if n == LAST[k] and k >= 1:
                    keep_scores(k - 1)
                    if k - 1 == NIDX // 2 - 1:
                        for c in range(4):
                            act.wait_ge(row_done, c + 1)
                            keys = row[:, 0:PAST].rearrange("r (f p j e) -> r f e j p", f=2, j=4, e=2)
                            nc.scalar.copy(keys[:, c // 2, c % 2, :, :],
                                           bank[0:SR, XB[c % 2], :].rearrange("r (j p) -> r j p", j=4))\
                                .then_inc(row_kept, 1)
            keep_scores(len(QUADS) - 1)
            for m, (x, g) in enumerate(SOFT):
                act.wait_ge(top_done, m + 1)
                nc.scalar.activation(lg[x][:, g, :], lg[x][:, g, :], ACT.Exp, bias=ntop[:, m:m + 1], scale=SCALE,
                                     accum_out=total[:, m:m + 1]).then_inc(exp_done, 1)
                for c in range(4):
                    n = 4 * m + c
                    act.wait_ge(pT_done, n + 1)
                    if c == 0 and m >= 1:
                        act.wait_ge(pv_done, 8 * m)
                    nc.scalar.copy(probT[:, 4 * c:4 * c + 4, :],
                                   bank[:, TB[n % 3], :].rearrange("p (j n) -> p j n", j=4)).then_inc(pT_kept, 1)
                act.wait_ge(newT_done, m + 1)
                nc.scalar.copy(newT[:, :], bank[0:SR, NEWB, 0:P]).then_inc(pT_kept, 1)

        def outputs(dve, link, m):
            x, g = SOFT[m]
            for b in range(4 * g, 4 * g + 4):
                n = (x == "a") * NB + b
                w = QW if x == "b" else KVW
                dve.wait_ge(pv_done, 2 * n + 2)
                link(nc.vector.tensor_tensor(o[x][rows_at(b), g, :], bank[rows_at(b), SB[n % 2], 0:w],
                                             const(s, "own_" + x)[rows_at(b), :], ALU.mult), o_read)

        @block.vector
        def _(dve):
            link = Chain(dve, chain_v)
            link(nc.vector.tensor_copy(qdup[:, :, :, :], s.qis[:, :].rearrange("r (h d) -> r h d", d=HD)
                                       .unsqueeze(2).to_broadcast([SR, H, 2, HD])), dup_ready)
            link(nc.vector.memset(q_a[:, :, :], 0.0))
            link(nc.vector.memset(q_b[:, :, :, :], 0.0))
            for half in range(2):
                r = slice(half * HD, half * HD + HD)
                link(nc.vector.tensor_copy(
                    q_a[r, :, half * 16:half * 16 + 16].rearrange("p b (j q) -> p b j q", q=NQ),
                    s.qaS[r, :, :].rearrange("p j (b q) -> p b j q", q=NQ)))
                for j in range(PAIRS):
                    c = (2 * j + half) * NQ
                    link(nc.vector.tensor_copy(q_b[r, :, j, c:c + NQ],
                                               s.qbS[r, j, :].rearrange("p (b q) -> p b q", q=NQ)))
            dve.wait_ge(w_done, 1)
            hm = const(s, "head_of").unsqueeze(1).to_broadcast([P, G, H])
            link(nc.vector.tensor_tensor(wrow[:, :, :], bank[:, XB[1], 0:G * H].rearrange("p (g h) -> p g h", h=H),
                                         hm, ALU.mult))
            link(nc.vector.reduce_sum(total[:, 0:G], wrow[:, :, :], AX.X))
            link(nc.vector.tensor_copy(top[:, 0:G], total[:, 0:G]))
            dve.wait_ge(dupT_done, 1)
            link(nc.vector.tensor_copy(q_i[:, :, :].rearrange("p b (h q) -> p b h q", q=NQ),
                                       bank[:, XB[0], 0:H * SR].rearrange("p (h b q) -> p b h q", h=H, q=NQ)), q_ready)
            dve.wait_ge(new_done, 1)
            for g in range(G):
                nb = bank[:, NEWB, 96 * g:96 * g + 96]
                link(nc.vector.tensor_scalar(lg["i"][:, g, PAST:COLS], nb[:, 0:32], 0.0, top[:, g:g + 1],
                                             ALU.max, ALU.mult))
                link(nc.vector.tensor_tensor(lg["b"][:, g, PAST:COLS], nb[:, 32:64],
                                             const(s, "new_masked")[:, g * SR:(g + 1) * SR], ALU.add))
                link(nc.vector.tensor_copy(s.newA[:, g, :], nb[:, 64:96]))
            for r in range(NIDX):
                b = QUADS[RES[r][0]][1]
                dve.wait_ge(res_done, r + 1)
                link(nc.vector.tensor_scalar(lg["i"][rows_at(b), b // 4, col0(r):col0(r) + 512],
                                             bank[rows_at(b), SB[r % 2], :], 0.0, top[rows_at(b), b // 4:b // 4 + 1],
                                             ALU.max, ALU.mult), idx_read)
            dve.sem_inc(all_read, 1)
            dve.wait_ge(row_done, 5)
            link(nc.vector.tensor_tensor(row[:, PAST:COLS], bank[0:SR, XB[0], 0:SR], const(s, "new_absent", SR), ALU.add))
            dve.wait_ge(row_kept, 4)
            for _ in range(TOPK_S // 8):
                topk_round(link, row[:, :], best[0:SR, :])
            link(nc.vector.tensor_scalar(row[:, PAST:COLS], row[:, PAST:COLS], EDGE, MASKED, ALU.is_gt, ALU.mult))
            for f in range(2):
                keys = row[:, f * HALF:(f + 1) * HALF]
                link(nc.vector.tensor_scalar(s.turned[:, :].rearrange("r (e p) -> r p e", e=SLOT),
                                             keys.rearrange("r (p e) -> r p e", e=SLOT), EDGE, MASKED,
                                             ALU.is_gt, ALU.mult))
                link(nc.vector.tensor_copy(keys, s.turned[:, :]), bias_ready if f == 1 else None)
            for m, (x, g) in enumerate(SOFT):
                L = lg[x][:, g, :]
                halves = [L[:, f * HALF:(f + 1) * HALF].rearrange("r (e n w) -> r n e w", n=4, w=32) for f in range(2)]
                if x == "b":
                    dve.wait_ge(s_kept, 4 * 4 * (g + 1))
                    for f in range(2):
                        link(nc.vector.tensor_reduce(gate[:, 4 * f:4 * f + 4], halves[f], AX.XY, ALU.add))
                    link(nc.vector.memset(gate[:, NBLK_PAST:2 * NBLK_PAST], DUMMY))
                    link(nc.vector.max(best[:, :], gate[:, 0:NBLK_PAST]))
                    link(nc.vector.memset(best[:, TOPB:8], DUMMY))
                    link(nc.vector.match_replace(gate[:, :], best[:, :], gate[:, :], PICKED))
                    link(nc.vector.tensor_scalar(gate[:, 0:NBLK_PAST], gate[:, 0:NBLK_PAST], EDGE, MASKED,
                                                 ALU.is_gt, ALU.mult))
                    for n in range(NBLK_PAST):
                        part = halves[n // 4][:, n % 4, :, :]
                        link(nc.vector.tensor_scalar(part, part, gate[:, n:n + 1], None, ALU.add))
                else:
                    dve.wait_ge(s_kept, len(RES) - NIDX)
                    link(nc.vector.tensor_tensor(L[:, PAST:COLS], s.newA[:, g, :],
                                                 const(s, "new_masked")[:, g * SR:(g + 1) * SR], ALU.add))
                    for c in range(5):
                        w = 512 if c < 4 else SR
                        n = 5 * g + c
                        dve.wait_ge(spread_done, n + 1)
                        part = L[:, c * 512:c * 512 + w]
                        link(nc.vector.tensor_tensor(part, part, bank[:, XB[n % 2], 0:w], ALU.add), spread_read)
                link(nc.vector.reduce_max(top[:, m:m + 1], L, AX.X))
                link(nc.vector.tensor_scalar(ntop[:, m:m + 1], top[:, m:m + 1], -SCALE, None, ALU.mult), top_done)
                dve.wait_ge(exp_done, m + 1)
                link(nc.vector.reciprocal(inv[:, m:m + 1], total[:, m:m + 1]))
                link(nc.vector.tensor_scalar(L, L, inv[:, m:m + 1], None, ALU.mult), norm_done)
                if m >= 1:
                    outputs(dve, link, m - 1)
            outputs(dve, link, len(SOFT) - 1)
            dve.wait_ge(oT_done, 1)
            for x, dst in (("b", s.obT), ("a", s.oaT)):
                link(nc.vector.tensor_copy(dst[:, :, SEQ:NTOK], bank[:, XB[x == "a"], 0:PAIRS * SR]
                                           .rearrange("p (j r) -> p j r", j=PAIRS)))


def merge(nc, s, a):
    w_in = a["w_in"][0].rearrange("(k p) n -> p k n", p=P)
    NCH = D // P
    PER = 1
    SAMPLE = 6
    with ExitStack() as ctx:
        def sb(name, shape, dt=F32):
            return ctx.enter_context(nc.sbuf_tensor(name, shape, dt))

        def sem(name):
            return nc.alloc_semaphore(name)

        gw = sb("gate_w", [P, 2, 2, KD, PER * P])
        wa, wb = sb("w_a", [P, PAIRS, D]), sb("w_b", [P, PAIRS, D])
        wo = sb("w_o", [P, KD, D])
        wr = sb("w_router", [P, KD, NG + NE])
        x = sb("x_mg", [P, TT, D])
        gf = sb("g_ffn", [P, D])
        sg = sb("sig", [P, 2, 2, NTOK])
        part = sb("part", [P, NTOK])
        junk = sb("junk_mg", [P, D])
        uT = sb("uT", [P, KD, NTOK])
        h2 = sb("h2", [P, 2, D])
        h2T = sb("h2T", [P, 2, D])
        ss, rr = sb("ss_mg", [P, TT]), sb("rr_mg", [P, TT])
        gate_in = [sem("mg_gate_in0"), sem("mg_gate_in1")]
        br_in, out_in, x_in, gf_in, r_in = (sem("mg_" + n) for n in ("branch_in", "out_in", "x_in", "gf_in", "r_in"))
        gate_used = sem("mg_gate_used")
        prod_done, samp_done = sem("mg_product_done"), sem("mg_sample_done")
        sig_ready, u_ready, mul_done = sem("mg_sigmoid_ready"), sem("mg_u_ready"), sem("mg_multiplied")
        out_done, x_ready = sem("mg_out_done"), sem("mg_x_ready")
        sq_ready, mean_ready, root_ready = sem("mg_square_ready"), sem("mg_mean_ready"), sem("mg_root_ready")
        h2_ready, h2T_done, h2T_kept = sem("mg_h2_ready"), sem("mg_h2T_done"), sem("mg_h2T_kept")
        log_done, log_kept = sem("mg_logits_done"), sem("mg_logits_kept")
        set_ready = sem("mg_set_ready")
        h2_stored = [sem("mg_h2_stored0"), sem("mg_h2_stored1")]
        x_stored = sem("mg_x_stored")
        chain_v = sem("mg_vector_chain")
        block = ctx.enter_context(nc.Block())
        bank = s.bank

        @block.sync
        def _(sp):
            def gates(c):
                for g in range(2):
                    c0 = C_GA + g * D + c * PER * P
                    sp.dma_start(gw[:, c % 2, g, :, :], w_in[:, :, c0:c0 + PER * P]).then_inc(gate_in[c % 2], 16)

            gates(0)
            for half in range(2):
                sp.dma_start(wa[half * HD:half * HD + HD, :, :],
                             a["w_br_a"][0, half * PAIRS * HD:(half + 1) * PAIRS * HD, :]
                             .rearrange("(j d) n -> d j n", d=HD)).then_inc(br_in, 16)
            sp.dma_start(wb[:, :, :], a["w_br_b"][0].rearrange("(j p) n -> p j n", p=P)).then_inc(br_in, 16)
            gates(1)
            sp.dma_start(wo[:, :, :], a["w_out"][0].rearrange("(k p) n -> p k n", p=P)).then_inc(out_in, 16)
            sp.dma_start(x[:, 0:TP, :], a["x_prompt"][0].rearrange("(t p) d -> p t d", p=P)).then_inc(x_in, 16)
            sp.dma_start(x[0:SR, TP, :], a["x_sample"].rearrange("b q d -> (b q) d")).then_inc(x_in, 16)
            for c in range(2, NCH // PER):
                sp.wait_ge(gate_used, (c - 1) * PER)
                gates(c)
            sp.dma_start(gf[:, :], a["g_ffn"].to_broadcast([P, D])).then_inc(gf_in, 16)
            sp.dma_start(wr[:, :, 0:NG], a["w_grp"][0].rearrange("(k p) n -> p k n", p=P)).then_inc(r_in, 16)
            sp.dma_start(wr[:, :, NG:NG + NE], a["w_exp"][0].rearrange("(k p) n -> p k n", p=P)).then_inc(r_in, 16)
            for t in range(TT):
                rows = rows_of(t)
                sp.wait_ge(x_ready, 2 * t + 2)
                sp.dma_start(s.x1[t * P:t * P + rows, :], x[0:rows, t, :]).then_inc(x_stored, 16)
                sp.wait_ge(h2_ready, t + 1)
                sp.dma_start(s.h2[t * P:t * P + rows, :], h2[0:rows, t % 2, :]).then_inc(h2_stored[t % 2], 16)
            sp.wait_ge(x_stored, 16 * TT)
            sp.wait_ge(h2_stored[0], 16 * ((TT + 1) // 2))
            sp.wait_ge(h2_stored[1], 16 * (TT // 2))

        @block.tensor
        def _(pe):
            def freed(n):
                j, i = divmod(n, 4)
                if i < 2:
                    pe.wait_ge(sig_ready, 3 * j + i + 1)
                else:
                    pe.wait_ge(mul_done, 4 * j + i - 1)

            for j in range(NCH):
                if j % PER == 0:
                    pe.wait_ge(gate_in[j // PER % 2], 32 * (j // PER // 2 + 1))
                c0 = j % PER * P
                lhs = [[gw[:, j // PER % 2, g, k, c0:c0 + P] for k in range(KD)] for g in range(2)]
                lhs += [[w[:, k, j * P:(j + 1) * P] for k in range(PAIRS)] for w in (wa, wb)]
                rhs = [s.hT, s.hT, s.oaT, s.obT]
                for i in range(4):
                    n = 4 * j + i
                    if n == 2:
                        pe.wait_ge(br_in, 48)
                    if n >= 6:
                        freed(n - 6)
                    for k, w in enumerate(lhs[i]):
                        last = nc.tensor.matmul(bank[:, n % 6, :], w, rhs[i][:, k, 0:SEQ],
                                                start=(k == 0), stop=(k == len(lhs[i]) - 1))
                    last.then_inc(prod_done, 1)
                if j >= 2:
                    pe.wait_ge(sig_ready, 3 * j - 3)
                    pe.wait_ge(mul_done, 4 * j - 4)
                for i in range(4):
                    for k, w in enumerate(lhs[i]):
                        last = nc.tensor.matmul(bank[:, SAMPLE + j % 2, i * SR:(i + 1) * SR], w,
                                                rhs[i][:, k, SEQ:NTOK],
                                                start=(k == 0), stop=(k == len(lhs[i]) - 1))
                last.then_inc(samp_done, 1)
                pe.wait_ge(samp_done, j + 1)
                pe.sem_inc(gate_used, 1)
            pe.wait_ge(out_in, 16)
            pe.wait_ge(u_ready, NCH)

            def logits(t):
                rows = rows_of(t)
                pe.wait_ge(h2_ready, t + 1)
                for c in range(2):
                    if t >= 1:
                        pe.wait_ge(h2T_kept, 2 * (t - 1) + c + 1)
                    for k in range(4):
                        kk = 4 * c + k
                        last = nc.tensor.transpose(bank[:, 4 + c, k * P:k * P + rows],
                                                   h2[0:rows, t % 2, kk * P:(kk + 1) * P],
                                                   const(s, "ident")[0:rows, 0:rows])
                    last.then_inc(h2T_done, 1)

            def route_logits(t):
                rows = rows_of(t)
                pe.wait_ge(h2T_kept, 2 * t + 2)
                if t == 0:
                    pe.wait_ge(r_in, 32)
                if t >= 2:
                    pe.wait_ge(log_kept, t - 1)
                for k in range(KD):
                    last = nc.tensor.matmul(bank[0:rows, 6 + t % 2, 0:NG + NE], h2T[:, t % 2, k * P:k * P + rows],
                                            wr[:, k, :], start=(k == 0), stop=(k == KD - 1))
                last.then_inc(log_done, 1)

            for t in range(TT):
                rows = rows_of(t)
                for half in range(2):
                    n = 2 * t + half
                    if n >= 4:
                        pe.wait_ge(x_ready, n - 3)
                    for k in range(KD):
                        last = nc.tensor.matmul(bank[0:rows, n % 4, :], uT[:, k, t * P:t * P + rows],
                                                wo[:, k, half * 512:half * 512 + 512],
                                                start=(k == 0), stop=(k == KD - 1))
                    last.then_inc(out_done, 1)
                if t >= 1:
                    logits(t - 1)
                if t >= 2:
                    route_logits(t - 2)
            logits(TT - 1)
            route_logits(TT - 2)
            route_logits(TT - 1)

        @block.scalar
        def _(act):
            for j in range(NCH):
                if j >= 2:
                    act.wait_ge(u_ready, j - 1)
                for i in range(2):
                    act.wait_ge(prod_done, 4 * j + i + 1)
                    nc.scalar.activation(sg[:, j % 2, i, 0:SEQ], bank[:, (4 * j + i) % 6, :], ACT.Sigmoid)\
                        .then_inc(sig_ready, 1)
                act.wait_ge(samp_done, j + 1)
                nc.scalar.activation(sg[:, j % 2, :, SEQ:NTOK],
                                     bank[:, SAMPLE + j % 2, 0:2 * SR].rearrange("p (i r) -> p i r", i=2),
                                     ACT.Sigmoid).then_inc(sig_ready, 1)
            act.wait_ge(set_ready, 1)

            def keep(t):
                rows = rows_of(t)
                for c in range(2):
                    act.wait_ge(h2T_done, 2 * t + c + 1)
                    if t >= 2:
                        act.wait_ge(log_done, t - 1)
                    nc.scalar.copy(h2T[:, t % 2, 512 * c:512 * c + 512].rearrange("p (k r) -> p k r", r=P)[:, :, 0:rows],
                                   bank[:, 4 + c, :].rearrange("p (k r) -> p k r", r=P)[:, :, 0:rows])\
                        .then_inc(h2T_kept, 1)

            def keep_logits(t):
                rows = rows_of(t)
                act.wait_ge(log_done, t + 1)
                nc.scalar.copy(s.logit[0:rows, t, :], bank[0:rows, 6 + t % 2, 0:NG + NE]).then_inc(log_kept, 1)

            for t in range(TT):
                rows = rows_of(t)
                act.wait_ge(x_ready, 2 * t + 2)
                if t >= 1:
                    act.wait_ge(sq_ready, t)
                nc.scalar.activation(junk[0:rows, :], x[0:rows, t, :], ACT.Square,
                                     accum_out=ss[0:rows, t:t + 1]).then_inc(sq_ready, 1)
                act.wait_ge(mean_ready, t + 1)
                nc.scalar.activation(rr[0:rows, t:t + 1], rr[0:rows, t:t + 1], ACT.Sqrt).then_inc(root_ready, 1)
                if t >= 1:
                    keep(t - 1)
                if t >= 2:
                    keep_logits(t - 2)
            keep(TT - 1)
            keep_logits(TT - 2)
            keep_logits(TT - 1)

        @block.vector
        def _(dve):
            link = Chain(dve, chain_v)
            nc.vector.memset(s.logit[:, :, :], 0.0).then_inc(set_ready, 1)
            for j in range(NCH):
                for c, c0, c1 in ((0, 0, SEQ), (1, SEQ, NTOK)):
                    if c:
                        dve.wait_ge(samp_done, j + 1)
                        pa, pb = (bank[:, SAMPLE + j % 2, i * SR:(i + 1) * SR] for i in (2, 3))
                    for i in (0, 1):
                        if not c:
                            dve.wait_ge(prod_done, 4 * j + 3 + i)
                            src = bank[:, (4 * j + 2 + i) % 6, :]
                        else:
                            src = (pa, pb)[i]
                        dve.wait_ge(sig_ready, 3 * j + (3 if c else i + 1))
                        dst = uT[:, j, c0:c1] if i == 0 else part[:, c0:c1]
                        link(nc.vector.tensor_tensor(dst, sg[:, j % 2, i, c0:c1], src, ALU.mult), mul_done)
                    link(nc.vector.tensor_tensor(uT[:, j, c0:c1], uT[:, j, c0:c1], part[:, c0:c1], ALU.add),
                         u_ready if c else None)
            dve.wait_ge(x_in, 32)
            dve.wait_ge(gf_in, 16)

            def add(t):
                rows = rows_of(t)
                for half in range(2):
                    n = 2 * t + half
                    dve.wait_ge(out_done, n + 1)
                    xs = x[0:rows, t, half * 512:half * 512 + 512]
                    link(nc.vector.tensor_tensor(xs, xs, bank[0:rows, n % 4, :], ALU.add), x_ready)

            def norm(t):
                rows = rows_of(t)
                dve.wait_ge(sq_ready, t + 1)
                link(nc.vector.tensor_scalar(rr[0:rows, t:t + 1], ss[0:rows, t:t + 1], 1.0 / D, EPS, ALU.mult, ALU.add),
                     mean_ready)
                dve.wait_ge(root_ready, t + 1)
                link(nc.vector.reciprocal(rr[0:rows, t:t + 1], rr[0:rows, t:t + 1]))
                if t >= 2:
                    dve.wait_ge(h2T_done, 2 * (t - 1))
                    dve.wait_ge(h2_stored[t % 2], 16 * (t // 2))
                nc.vector.scalar_tensor_tensor(h2[0:rows, t % 2, :], x[0:rows, t, :], rr[0:rows, t:t + 1],
                                               gf[0:rows, :], ALU.mult, ALU.mult).then_inc(h2_ready, 1)

            for t in range(TT):
                add(t)
                norm(t)


def route(nc, s, a):
    MAXK = -(-NTOK // BLK)
    with ExitStack() as ctx:
        def sb(name, shape, dt=F32):
            return ctx.enter_context(nc.sbuf_tensor(name, shape, dt))

        def sem(name):
            return nc.alloc_semaphore(name)

        bias = sb("router_bias", [P, NG + NE])
        top = sb("rt_top", [P, TT])
        place = sb("rt_place", [P, TT])
        gsum, gprob = sb("rt_gsum", [P, TT]), sb("rt_gprob", [P, TT])
        gex, geq, gone = (sb("rt_" + n, [P, TT, NG]) for n in ("gexp", "geq", "gone"))
        spread = sb("rt_spread", [P, TT, NE])
        elog, eeq = sb("rt_elog", [P, TT, EPG]), sb("rt_eeq", [P, TT, EPG])
        one = [sb(f"rt_one{k}", [P, TT, EPG]) for k in range(2)]
        m = [sb(f"rt_m{k}", [P, TT]) for k in range(2)]
        E = [sb(f"rt_E{k}", [P, TT, NE]) for k in range(2)]
        both = sb("rt_both", [P, TT, NE])
        ratio, denom = sb("rt_ratio", [P, TT]), sb("rt_denom", [P, TT])
        base = sb("rt_base", [P, TT + 1, NE])
        over = sb("rt_over", [P, NE, MAXK])
        nblk = sb("rt_nblk", [P, NE])
        cs = sb("rt_cumsum", [P, 2, NE])
        slotf = sb("rt_slotf", [P, 2, TT])
        le = sb("rt_le", [1, MAXB, NE])
        bef = sb("rt_bef", [1, MAXB])
        npf, npx = sb("rt_npf", [1, 1]), sb("rt_npx", [1, MAXB // 2])
        ids = sb("rt_ids", [P, TT, TABW], I32)
        bias_in = sem("rt_bias_in")
        gsub_ready, gexp_ready = sem("rt_group_sub_ready"), sem("rt_group_exp_ready")
        both_ready, sum_done = sem("rt_both_ready"), sem("rt_sum_done")
        slots_ready, scattered = sem("rt_slots_ready"), sem("rt_scattered")
        chain_v = sem("rt_vector_chain")
        block = ctx.enter_context(nc.Block())
        bank = s.bank

        @block.sync
        def _(sp):
            sp.dma_start(bias[:, 0:NG], a["b_grp"].to_broadcast([P, NG])).then_inc(bias_in, 16)
            sp.dma_start(bias[:, NG:], a["b_exp"].to_broadcast([P, NE])).then_inc(bias_in, 16)

        @block.scalar
        def _(act):
            act.wait_ge(gsub_ready, 1)
            nc.scalar.activation(gex[:, :, :], gex[:, :, :], ACT.Exp).then_inc(gexp_ready, 1)
            act.wait_ge(gsub_ready, 2)
            nc.scalar.activation(ratio[:, :], ratio[:, :], ACT.Exp).then_inc(gexp_ready, 1)

        @block.tensor
        def _(pe):
            pe.wait_ge(both_ready, 1)
            flat = both[:, :, :].rearrange("p t e -> p (t e)")
            nc.tensor.matmul(bank[:, 0, 0:TT * NE], const(s, "before"), flat, start=True, stop=True)
            nc.tensor.matmul(bank[:, 1, 0:TT * NE], s.ones[:, :], flat, start=True, stop=True).then_inc(sum_done, 1)

        @block.vector
        def _(dve):
            link = Chain(dve, chain_v)

            def first_of(eq, n, down, out):
                link(nc.vector.tensor_tensor(eq[:, :, :], eq[:, :, :],
                                             down.unsqueeze(1).to_broadcast([P, TT, n]), ALU.mult))
                link(nc.vector.reduce_max(place[:, :], eq[:, :, :], AX.X))
                link(nc.vector.tensor_tensor(out[:, :, :], eq[:, :, :],
                                             place[:, :].unsqueeze(2).to_broadcast([P, TT, n]), ALU.is_equal))

            def largest(v, n, down, eq, mx, out):
                link(nc.vector.reduce_max(mx[:, :], v, AX.X))
                link(nc.vector.tensor_tensor(eq[:, :, :], v, mx[:, :].unsqueeze(2).to_broadcast([P, TT, n]),
                                             ALU.is_equal))
                first_of(eq, n, down, out)

            dve.wait_ge(bias_in, 32)
            link(nc.vector.tensor_tensor(s.logit[:, :, :], s.logit[:, :, :],
                                         bias[:, :].unsqueeze(1).to_broadcast([P, TT, NG + NE]), ALU.add))
            G = s.logit[:, :, 0:NG]
            largest(G, NG, const(s, "down")[:, EPG - NG:EPG], geq, top, gone)
            link(nc.vector.tensor_tensor(gex[:, :, :], G, top[:, :].unsqueeze(2).to_broadcast([P, TT, NG]),
                                         ALU.subtract), gsub_ready)
            link(nc.vector.tensor_tensor(spread[:, :, :].rearrange("p t (g e) -> p t g e", e=EPG),
                                         s.logit[:, :, NG:].rearrange("p t (g e) -> p t g e", e=EPG),
                                         gone[:, :, :].unsqueeze(3).to_broadcast([P, TT, NG, EPG]), ALU.mult))
            link(nc.vector.reduce_sum(elog[:, :, :], spread[:, :, :].rearrange("p t (g e) -> p t e g", e=EPG), AX.X))
            for k in range(2):
                largest(elog[:, :, :], EPG, const(s, "down"), eeq, m[k], one[k])
                if k == 0:
                    link(nc.vector.scalar_tensor_tensor(elog[:, :, :], one[0][:, :, :], PICKED, elog[:, :, :],
                                                        ALU.mult, ALU.add))
                link(nc.vector.tensor_tensor(E[k][:, :, :].rearrange("p t (g e) -> p t g e", e=EPG),
                                             gone[:, :, :].unsqueeze(3).to_broadcast([P, TT, NG, EPG]),
                                             one[k][:, :, :].unsqueeze(2).to_broadcast([P, TT, NG, EPG]), ALU.mult))
                link(nc.vector.tensor_tensor(E[k][:, :, :], E[k][:, :, :],
                                             const(s, "real").unsqueeze(2).to_broadcast([P, TT, NE]), ALU.mult))
            link(nc.vector.tensor_tensor(ratio[:, :], m[1][:, :], m[0][:, :], ALU.subtract), gsub_ready)
            link(nc.vector.tensor_tensor(both[:, :, :], E[0][:, :, :], E[1][:, :, :], ALU.add), both_ready)
            dve.wait_ge(gexp_ready, 2)
            link(nc.vector.reduce_sum(gsum[:, :], gex[:, :, :], AX.X))
            link(nc.vector.scalar_tensor_tensor(denom[:, :], ratio[:, :], 1.0, gsum[:, :], ALU.add, ALU.mult))
            link(nc.vector.reciprocal(s.w12[:, 0, :], denom[:, :]))
            link(nc.vector.tensor_tensor(s.w12[:, 1, :], s.w12[:, 0, :], ratio[:, :], ALU.mult))
            dve.wait_ge(sum_done, 1)
            tot = bank[:, 1, 0:TT * NE].rearrange("p (t e) -> p t e", e=NE)
            link(nc.vector.memset(base[:, 0, :], 0.0))
            for t in range(TT):
                link(nc.vector.tensor_tensor(base[:, t + 1, :], base[:, t, :], tot[:, t, :], ALU.add))
            steps = const(s, "blocks")[:, 0:MAXK].unsqueeze(1).to_broadcast([P, NE, MAXK])
            link(nc.vector.tensor_scalar(nblk[:, :], base[:, TT, :], 1.0 / BLK, None, ALU.mult))
            link(nc.vector.tensor_tensor(over[:, :, :], nblk[:, :].unsqueeze(2).to_broadcast([P, NE, MAXK]),
                                         steps, ALU.is_gt))
            link(nc.vector.reduce_sum(nblk[:, :], over[:, :, :], AX.X))
            link(nc.vector.tensor_copy(cs[:, 0, :], nblk[:, :]))
            side, w = 0, 1
            while w < NE:
                link(nc.vector.tensor_copy(cs[:, 1 - side, 0:w], cs[:, side, 0:w]))
                link(nc.vector.tensor_tensor(cs[:, 1 - side, w:], cs[:, side, w:], cs[:, side, 0:NE - w], ALU.add))
                side, w = 1 - side, 2 * w
            ends = cs[:, side, :]
            link(nc.vector.tensor_tensor(nblk[:, :], ends, nblk[:, :], ALU.subtract))
            link(nc.vector.tensor_scalar(nblk[:, :], nblk[:, :], float(BLK), None, ALU.mult))
            link(nc.vector.tensor_tensor(both[:, :, :], bank[:, 0, 0:TT * NE].rearrange("p (t e) -> p t e", e=NE),
                                         base[:, 0:TT, :], ALU.add))
            link(nc.vector.tensor_tensor(both[:, :, :], both[:, :, :],
                                         nblk[:, :].unsqueeze(1).to_broadcast([P, TT, NE]), ALU.add))
            for k in range(2):
                link(nc.vector.tensor_tensor(spread[:, :, :], both[:, :, :], E[k][:, :, :], ALU.mult))
                link(nc.vector.reduce_sum(slotf[:, k, :], spread[:, :, :], AX.X))
            link(nc.vector.tensor_copy(s.slot[:, :, :], slotf[:, :, :]))
            link(nc.vector.tensor_copy(ids[:, :, :], const(s, "token").unsqueeze(2).to_broadcast([P, TT, TABW])),
                 slots_ready)
            link(nc.vector.tensor_tensor(le[:, :, :], ends[0:1, :].unsqueeze(1).to_broadcast([1, MAXB, NE]),
                                         const(s, "blocks", 1).unsqueeze(2).to_broadcast([1, MAXB, NE]), ALU.is_le))
            link(nc.vector.reduce_sum(bef[:, :], le[:, :, :], AX.X))
            link(nc.vector.tensor_scalar(bef[:, :], bef[:, :], float(NE - 1), None, ALU.min))
            link(nc.vector.tensor_copy(s.be[:, :], bef[:, :]))
            link(nc.vector.tensor_tensor(npx[:, :], const(s, "evens", 1), ends[0:1, NE - 1:NE]
                                         .to_broadcast([1, MAXB // 2]), ALU.is_lt))
            link(nc.vector.reduce_sum(npf[:, :], npx[:, :], AX.X))
            link(nc.vector.tensor_copy(s.npair[:, :], npf[:, :]))

        @block.gpsimd
        def _(pool):
            pool.wait_ge(slots_ready, 1)
            for k in range(2):
                for t in range(TT):
                    rows = rows_of(t)
                    pool.indirect_dma_start(s.slots, bass.IndirectOffsetOnAxis(ap=s.slot[0:rows, k, t:t + 1], axis=0),
                                            ids[0:rows, t, :], None).then_inc(scattered, 16)
            pool.wait_ge(scattered, 16 * 2 * TT)


def experts(nc, s, a):
    w_gate = a["w_e_gate"][0].rearrange("e (k p) n -> p e k n", p=P)
    w_up = a["w_e_up"][0].rearrange("e (k p) n -> p e k n", p=P)
    w_down = a["w_e_down"][0].rearrange("e (f p) n -> p e f n", p=P)
    KF = DE // P
    with ExitStack() as ctx:
        def sb(name, shape, dt=F32):
            return ctx.enter_context(nc.sbuf_tensor(name, shape, dt))

        def sem(name):
            return nc.alloc_semaphore(name)

        def sems(name):
            return [sem(f"ex_{name}{u}") for u in range(2)]

        wgu = sb("w_gate_up", [P, 2, KD, 2 * DE])
        wd = sb("w_down", [P, 2, KF, D])
        ids = sb("ids", [BLK, MAXB + 2], I32)
        id1 = sb("id1", [BLK, 2], I32)
        xg = sb("xg", [BLK, 2, D])
        xT = sb("xT", [P, 2, KD * BLK])
        sgm = sb("sgm", [BLK, 2, DE])
        hid = sb("hid", [BLK, 2, DE])
        hidT = sb("hidT", [P, 2, KF * BLK])
        y = sb("y", [BLK, 2, D])
        zeros = sb("zeros", [P, D])
        ids_in = sem("ex_ids_in")
        gu_in, wd_in, x_in, id_ready = sems("gate_up_in"), sems("down_in"), sems("x_in"), sems("id_ready")
        xT_done, xT_kept, gu_done = sems("xT_done"), sems("xT_kept"), sems("gate_up_done")
        sig_ready, hid_ready, gate_mul = sems("sigmoid_ready"), sems("hidden_ready"), sems("gated")
        hT_done, hT_kept, y_done = sems("hidT_done"), sems("hidT_kept"), sems("y_done")
        y_ready, y_kept, y_free, y_stored = sems("y_ready"), sems("y_kept"), sems("y_free"), sems("y_stored")
        zeros_ready, zeros_stored = sem("ex_zeros_ready"), sem("ex_zeros_stored")
        carry = sem("ex_carry")
        block = ctx.enter_context(nc.Block())
        bank = s.bank

        @block.sync
        def _(sp):
            with nc.allow_non_contiguous_dma(reason="one word of each row"):
                sp.dma_start(ids[:, 0:MAXB], s.slots.rearrange("(b r) w -> r b w", r=BLK)[:, :, 0:1]
                             .rearrange("r b o -> r (b o)")).then_inc(ids_in, 16)
            turns = sp.value_load(s.npair[0:1, 0:1], min_val=1, max_val=MAXB // 2)
            with sp.Fori(0, turns) as i:
                for u in range(2):
                    e = sp.value_load(s.be[0:1, bass.ds(2 * i + u, 1)], min_val=0, max_val=NE - 1)
                    sp.wait_ge(gu_done[u], i + 1)
                    sp.dma_start(wgu[:, u, :, 0:DE], w_gate[:, bass.ds(e, 1), :, :]
                                 .rearrange("p e k n -> p (e k) n")).then_inc(gu_in[u], 16)
                    sp.dma_start(wgu[:, u, :, DE:], w_up[:, bass.ds(e, 1), :, :]
                                 .rearrange("p e k n -> p (e k) n")).then_inc(gu_in[u], 16)
                for u in range(2):
                    e = sp.value_load(s.be[0:1, bass.ds(2 * i + u, 1)], min_val=0, max_val=NE - 1)
                    sp.wait_ge(y_done[u], i + 1)
                    sp.dma_start(wd[:, u, :, :], w_down[:, bass.ds(e, 1), :, :]
                                 .rearrange("p e f n -> p (e f) n")).then_inc(wd_in[u], 16)
                sp.sem_inc(zeros_stored, 16)
            sp.wait_ge(zeros_ready, 1)
            with sp.Fori(turns, MAXB // 2) as i:
                sp.dma_start(s.y[bass.ds(2 * BLK * i, 2 * BLK), :], zeros[:, :]).then_inc(zeros_stored, 16)
            sp.wait_ge(zeros_stored, MAXB // 2 * 16)

        @block.gpsimd
        def _(pool):
            nc.gpsimd.memset(ids[:, MAXB:MAXB + 2], 0).then_inc(ids_in, 16)
            pool.wait_ge(ids_in, 32)
            turns = pool.value_load(s.npair[0:1, 0:1], min_val=1, max_val=MAXB // 2)

            def gather(u, turn, column):
                nc.gpsimd.tensor_copy(id1[:, u:u + 1], column).then_inc(id_ready[u], 1)
                pool.wait_ge(id_ready[u], turn + 1)
                pool.sem_inc(carry, 1)
                pool.indirect_dma_start(xg[:, u, :], None, s.h2,
                                        bass.IndirectOffsetOnAxis(ap=id1[:, u:u + 1], axis=0)).then_inc(x_in[u], 16)

            for u in range(2):
                gather(u, 0, ids[:, u:u + 1])
            with pool.Fori(0, turns) as i:
                for u in range(2):
                    pool.wait_ge(xT_done[u], i + 1)
                    gather(u, i + 1, ids[:, bass.ds(2 * i + 2 + u, 1)])
                for u in range(2):
                    pool.wait_ge(y_ready[u], i + 1)
                    pool.dma_start(s.y[bass.ds((2 * i + u) * BLK, BLK), :], y[:, u, :]).then_inc(y_stored[u], 16)
                for u in range(2):
                    pool.wait_ge(y_stored[u], 16 * i + 16)
                    pool.sem_inc(y_free[u], 1)
            for u in range(2):
                pool.wait_ge(x_in[u], turns * 16 + 16)
            pool.sem_inc(carry, 1)

        @block.tensor
        def _(pe):
            for u in range(2):
                for done in (gu_done, y_done):
                    pe.sem_inc(done[u], 1)
            turns = pe.value_load(s.npair[0:1, 0:1], min_val=1, max_val=MAXB // 2)
            with pe.Fori(0, turns) as i:
                def turn_rows(u):
                    pe.wait_ge(x_in[u], 16 * i + 16)
                    pe.wait_ge(hT_kept[u], i + 1)
                    pe.sem_inc(carry, 1)
                    for k in range(KD):
                        last = nc.tensor.transpose(bank[:, u, k * BLK:(k + 1) * BLK], xg[:, u, k * P:(k + 1) * P],
                                                   const(s, "ident")[0:BLK, 0:BLK])
                    last.then_inc(xT_done[u], 1)

                def gate_up(u, ks):
                    for k in ks:
                        last = nc.tensor.matmul(bank[0:BLK, 2 + u, :], xT[:, u, k * BLK:(k + 1) * BLK],
                                                wgu[:, u, k, :], start=(k == 0), stop=(k == KD - 1))
                    return last

                def turn_hidden(u):
                    pe.wait_ge(hid_ready[u], i + 2)
                    pe.sem_inc(carry, 1)
                    for f in range(KF):
                        last = nc.tensor.transpose(bank[:, u, f * BLK:(f + 1) * BLK], hid[:, u, f * P:(f + 1) * P],
                                                   const(s, "ident")[0:BLK, 0:BLK])
                    last.then_inc(hT_done[u], 1)

                def down(u, half):
                    for f in range(KF):
                        last = nc.tensor.matmul(bank[0:BLK, 4 + 2 * u + half, :], hidT[:, u, f * BLK:(f + 1) * BLK],
                                                wd[:, u, f, half * 512:half * 512 + 512],
                                                start=(f == 0), stop=(f == KF - 1))
                    return last

                turn_rows(0)
                turn_rows(1)
                for u in range(2):
                    pe.wait_ge(gu_in[u], 32 * i + 32)
                    pe.wait_ge(hid_ready[u], i + 1)
                    pe.wait_ge(xT_kept[u], i + 1)
                    gate_up(u, range(0, KD // 2))
                    if u == 1:
                        turn_hidden(0)
                    gate_up(u, range(KD // 2, KD)).then_inc(gu_done[u], 1)
                for u in range(2):
                    pe.wait_ge(wd_in[u], 16 * i + 16)
                    pe.wait_ge(y_kept[u], i + 1)
                    pe.wait_ge(hT_kept[u], i + 2)
                    down(u, 0)
                    if u == 0:
                        turn_hidden(1)
                    down(u, 1).then_inc(y_done[u], 1)

        @block.scalar
        def _(act):
            for u in range(2):
                act.sem_inc(y_kept[u], 1)
                act.sem_inc(y_free[u], 1)
            turns = act.value_load(s.npair[0:1, 0:1], min_val=1, max_val=MAXB // 2)
            act.sem_inc(carry, 1)
            with act.Fori(0, turns) as i:
                for u in range(2):
                    act.wait_ge(gu_done[u], i + 2)
                    nc.scalar.activation(sgm[:, u, :], bank[0:BLK, 2 + u, 0:DE], ACT.Sigmoid).then_inc(sig_ready[u], 1)
                for u in range(2):
                    act.wait_ge(y_done[u], i + 2)
                    act.wait_ge(y_free[u], i + 1)
                    nc.scalar.copy(y[:, u, :].rearrange("p (b n) -> p b n", b=2),
                                   bank[0:BLK, 4 + 2 * u:6 + 2 * u, :]).then_inc(y_ready[u], 1)
                    act.wait_ge(y_ready[u], i + 1)
                    act.sem_inc(y_kept[u], 1)

        @block.vector
        def _(dve):
            nc.vector.memset(zeros[:, :], 0.0).then_inc(zeros_ready, 1)
            for u in range(2):
                dve.sem_inc(hT_kept[u], 1)
                dve.sem_inc(hid_ready[u], 1)
            turns = dve.value_load(s.npair[0:1, 0:1], min_val=1, max_val=MAXB // 2)
            with dve.Fori(0, turns) as i:
                for u in range(2):
                    dve.wait_ge(xT_done[u], i + 1)
                    nc.vector.tensor_copy(xT[:, u, :], bank[:, u, :]).then_inc(xT_kept[u], 1)

                def hidden(u):
                    dve.wait_ge(sig_ready[u], i + 1)
                    nc.vector.tensor_tensor(sgm[:, u, :], sgm[:, u, :], bank[0:BLK, 2 + u, 0:DE], ALU.mult)\
                        .then_inc(gate_mul[u], 1)
                    dve.wait_ge(gate_mul[u], i + 1)
                    nc.vector.tensor_tensor(hid[:, u, :], sgm[:, u, :], bank[0:BLK, 2 + u, DE:], ALU.mult)\
                        .then_inc(hid_ready[u], 1)

                def keep_hidden(u):
                    dve.wait_ge(hT_done[u], i + 1)
                    nc.vector.tensor_copy(hidT[:, u, :], bank[:, u, 0:KF * BLK]).then_inc(hT_kept[u], 1)

                hidden(0)
                keep_hidden(0)
                hidden(1)
                keep_hidden(1)


def combine(nc, s, a, o):
    with ExitStack() as ctx:
        def sb(name, shape, dt=F32):
            return ctx.enter_context(nc.sbuf_tensor(name, shape, dt))

        def sem(name):
            return nc.alloc_semaphore(name)

        x = sb("x_cb", [P, TT, D])
        y = [sb(f"y_cb{k}", [P, TT, D]) for k in range(2)]
        gl = sb("g_last", [P, D])
        junk = sb("junk_cb", [P, D])
        ss, rr = sb("ss_cb", [P, TT]), sb("rr_cb", [P, TT])
        x_in = [sem(f"cb_x_in{t}") for t in range(TT)]
        y_in = [[sem(f"cb_y_in{k}{t}") for t in range(TT)] for k in range(2)]
        g_in, stored = sem("cb_g_in"), sem("cb_stored")
        x_ready, sq_ready = sem("cb_x_ready"), sem("cb_square_ready")
        mean_ready, root_ready, y_ready = sem("cb_mean_ready"), sem("cb_root_ready"), sem("cb_y_ready")
        chain_v = sem("cb_vector_chain")
        block = ctx.enter_context(nc.Block())

        @block.gpsimd
        def _(pool):
            for t in range(TT):
                rows = rows_of(t)
                for k in range(2):
                    pool.indirect_dma_start(y[k][0:rows, t, :], None, s.y,
                                            bass.IndirectOffsetOnAxis(ap=s.slot[0:rows, k, t:t + 1], axis=0))\
                        .then_inc(y_in[k][t], 16)

        @block.sync
        def _(sp):
            for t in range(TT):
                rows = rows_of(t)
                sp.dma_start(x[0:rows, t, :], s.x1[t * P:t * P + rows, :]).then_inc(x_in[t], 16)
            sp.dma_start(gl[:, :], a["g_final"].to_broadcast([P, D])).then_inc(g_in, 16)
            for t in range(TT):
                rows = rows_of(t)
                sp.wait_ge(x_in[t], 16)
                sp.wait_ge(y_ready, t + 1)
                dst = o["y_prompt"][t * P:(t + 1) * P, :] if t < TP else o["y_sample"]
                sp.dma_start(dst, x[0:rows, t, :]).then_inc(stored, 16)
            sp.wait_ge(stored, 16 * TT)

        @block.scalar
        def _(act):
            for t in range(TT):
                rows = rows_of(t)
                act.wait_ge(x_ready, t + 1)
                if t >= 1:
                    act.wait_ge(sq_ready, t)
                nc.scalar.activation(junk[0:rows, :], x[0:rows, t, :], ACT.Square,
                                     accum_out=ss[0:rows, t:t + 1]).then_inc(sq_ready, 1)
                act.wait_ge(mean_ready, t + 1)
                nc.scalar.activation(rr[0:rows, t:t + 1], rr[0:rows, t:t + 1], ACT.Sqrt).then_inc(root_ready, 1)

        @block.vector
        def _(dve):
            link = Chain(dve, chain_v)
            dve.wait_ge(g_in, 16)
            for t in range(TT):
                rows = rows_of(t)
                xs = x[0:rows, t, :]
                dve.wait_ge(x_in[t], 16)
                for k in range(2):
                    dve.wait_ge(y_in[k][t], 16)
                    link(nc.vector.scalar_tensor_tensor(xs, y[k][0:rows, t, :], s.w12[0:rows, k, t:t + 1], xs,
                                                        ALU.mult, ALU.add), x_ready if k else None)
                dve.wait_ge(sq_ready, t + 1)
                link(nc.vector.tensor_scalar(rr[0:rows, t:t + 1], ss[0:rows, t:t + 1], 1.0 / D, EPS, ALU.mult, ALU.add),
                     mean_ready)
                dve.wait_ge(root_ready, t + 1)
                link(nc.vector.reciprocal(rr[0:rows, t:t + 1], rr[0:rows, t:t + 1]))
                nc.vector.scalar_tensor_tensor(xs, xs, rr[0:rows, t:t + 1], gl[0:rows, :], ALU.mult, ALU.mult)\
                    .then_inc(y_ready, 1)


CACHES = ["cache_k_a", "cache_v_a", "cache_k_idx", "cache_k_b", "cache_v_b"]
INPUTS = ["x_prompt", "x_sample", *CACHES, "page_table", "w_in", "w_br_a", "w_br_b", "w_out", "g_mix",
          "g_ffn", "w_grp", "b_grp", "w_exp", "b_exp", "w_e_gate", "w_e_up", "w_e_down", "g_final"]
ROWS = {"k_a": (2, HD), "v_a": (2, HD), "k_idx": (HD,), "k_b": (H, HD), "v_b": (H, HD)}
OUTPUTS = [("y_prompt", (1, SEQ, D)), ("y_sample", (NB, NQ, D))]
OUTPUTS += [(n + "_p", (1, 1, SEQ, *r)) for n, r in ROWS.items()]
OUTPUTS += [(n + "_s", (1, NB, NQ, *r)) for n, r in ROWS.items()]


def kernel(**inputs):
    import concourse.bacc as bacc
    from concourse.bass_utils import run_bass_kernel_spmd

    nc = bacc.Bacc("TRN2", target_bir_lowering=False, num_devices=1)
    arrays, args, outs = {}, {}, {}
    for name in INPUTS:
        v = np.ascontiguousarray(inputs[name])
        arrays["in_" + name] = v
        args[name] = nc.dram_tensor("in_" + name, v.shape, mybir.dt.from_np(v.dtype), kind="ExternalInput").ap()
    arrays["in_consts"] = CONSTS
    args["consts"] = nc.dram_tensor("in_consts", CONSTS.shape, F32, kind="ExternalInput").ap()
    args["g_final"] = args["g_final"].unsqueeze(0)
    for i, (name, shape) in enumerate(OUTPUTS):
        ap = nc.dram_tensor(f"out_{i}", shape, F32, kind="ExternalOutput").ap()
        if name.startswith("y_"):
            outs[name] = ap.rearrange("a b d -> (a b) d")
        elif len(shape) == 5:
            outs[name] = ap.rearrange("a b t h d -> (a b t) (h d)")
        else:
            outs[name] = ap.rearrange("a b t d -> (a b t) d")
    build(nc, args, outs)
    r = run_bass_kernel_spmd(nc, [arrays], core_ids=[0])
    return tuple(r.results[0][f"out_{i}"] for i in range(len(OUTPUTS)))
```

```python
from contextlib import ExitStack

import numpy as np

import concourse.bass as bass
from concourse import mybir

F32 = mybir.dt.float32
F32R = mybir.dt.float32r
I32 = mybir.dt.int32
ALU = mybir.AluOpType
ACT = mybir.ActivationFunctionType
AX = mybir.AxisListType

P = 128
D = 1024
KD = D // P
SEQ = 512
TP = SEQ // P
NB, NQ = 8, 4
SR = NB * NQ
TT = TP + 1
NTOK = SEQ + SR
PAST = 2048
PAGE = 128
NPG = PAST // PAGE
SLOT = 8
HPG = P * SLOT // PAGE
CH = 2 * SLOT
POOL = NB * NPG * 5 // 4
HD = 64
ROT = HD // 4
THETA = 500000.0
H = 8
PAIRS = H // 2
KVW = 2 * HD
QW = H * HD
TOPK_P = min(256, SEQ // 4)
TOPK_S = min(256, (PAST + NQ) // 4)
MBLK = 256
NBLK_PAST = PAST // MBLK
TOPB = 3
NG, EPG = 4, 8
NE = NG * EPG
DE = 256
EPS = 1e-6
SCALE = HD ** -0.5
IDX_SCALE = H ** -0.5 * HD ** -0.5
MASKED = -1e30
ABSENT = -3.0e38
PICKED = -3.39e38
EDGE = -3.2e38
DUMMY = 3.3e38
BLK = 64
MAXB = 2 * NTOK // BLK + NE
MAXB += MAXB % 2
TABW = 128

C_QA, C_KA, C_VA, C_QI = 0, 512, 640, 768
C_KI, C_WI, C_QB, C_KB, C_VB, C_GA = 1280, 1344, 1352, 1864, 2376, 2888
D_IN = 4936


def rows_of(t):
    return P if t < TP else SR


def const_pack():
    cols, at = [], {}

    def put(name, a):
        full = np.zeros((P, a.shape[1]), np.float32)
        full[:a.shape[0]] = a
        at[name] = (sum(c.shape[1] for c in cols), a.shape[1])
        cols.append(full)

    i = np.arange(P)
    put("ident", np.eye(P))
    put("causal", np.where(i[None, :] <= i[:, None], 0.0, MASKED))
    put("absent", np.where(i[None, :] <= i[:, None], 0.0, ABSENT))
    put("page_of", (i[:, None] // (P // HPG) == np.arange(HPG)[None, :]) * 1.0)
    put("within", (i[:, None] % (P // HPG)) * 1.0)
    row = np.arange(P)
    own = (row // 32 * NQ + row % NQ)[:, None]
    both = [(own + 4 * NQ * g == np.arange(SR)[None, :]) * 1.0 for g in range(2)]
    head = row // NQ % H
    put("gathered", np.concatenate(both, axis=1))
    put("spread", np.concatenate([x.T for x in both], axis=1))
    put("gathered_j", np.concatenate([x * (head % 4 == j)[:, None] for j in range(4) for x in both], axis=1))
    put("head_of", (head[:, None] == np.arange(H)[None, :]) * 1.0)
    put("own_b", (head[:, None] == np.arange(QW)[None, :] // HD) * 1.0)
    put("own_a", (head[:, None] // 4 == np.arange(KVW)[None, :] // HD) * 1.0)
    put("before", (i[:, None] < i[None, :]) * 1.0)
    half = ROT // 2
    inv = np.float32(THETA) ** (-np.arange(half, dtype=np.float32) / np.float32(half))
    pos = np.concatenate([np.arange(SEQ), PAST + np.tile(np.arange(NQ), NB)])
    ang = (pos.astype(np.float32)[:, None] * inv.astype(np.float32)[None, :]).astype(np.float64)
    for name, f in (("cos", np.cos), ("sin", np.sin)):
        tab = np.zeros((TT * P, ROT), np.float32)
        tab[:NTOK] = np.tile(f(ang), (1, 2))
        put(name, tab.reshape(TT, P, ROT).transpose(1, 0, 2).reshape(P, TT * ROT))
    r = np.arange(SR)
    seen = (r[:, None] // NQ == r[None, :] // NQ) & (r[None, :] <= r[:, None])
    put("new_absent", np.where(seen, 0.0, ABSENT))
    for_rows = np.concatenate([np.where((x @ seen) > 0, 0.0, MASKED) for x in both], axis=1)
    put("new_masked", for_rows)
    put("blocks", np.tile(np.arange(MAXB, dtype=np.float32), (P, 1)))
    put("evens", np.tile(2.0 * np.arange(MAXB // 2, dtype=np.float32), (P, 1)))
    tok = np.arange(TT * P, dtype=np.float32).reshape(TT, P).T
    put("token", tok)
    put("real", (np.arange(TT * P).reshape(TT, P).T < NTOK) * 1.0)
    put("down", np.tile(np.arange(EPG, 0, -1, dtype=np.float32), (P, 1)))
    return np.concatenate(cols, axis=1), at


CONSTS, AT = const_pack()


class Chain:

    def __init__(self, eng, sem):
        self.eng, self.sem, self.n = eng, sem, {}
        self.turn, self.per = None, {}

    def loop(self, turn, per):
        self.turn, self.per = turn, {sem.name: k for sem, k in per}
        self.start = dict(self.n)

    def end_loop(self, turns):
        for name, k in self.per.items():
            got = self.n.get(name, 0) - self.start.get(name, 0)
            assert got == k, (name, got, k)
            self.n[name] = self.start.get(name, 0) + k * turns
        self.turn = None

    def __call__(self, ins, ready=None):
        sem = ready or self.sem
        ins.then_inc(sem, 1)
        n = self.n[sem.name] = self.n.get(sem.name, 0) + 1
        if self.turn is not None:
            assert sem.name in self.per, sem.name
            n = self.turn * self.per[sem.name] + n
        self.eng.wait_ge(sem, n)
        return ins


class State:
    pass


def const(s, name, rows=P):
    a, n = AT[name]
    return s.consts[0:rows, a:a + n]


def build(nc, a, o):
    with ExitStack() as ctx:
        def sb(name, shape, dt=F32):
            return ctx.enter_context(nc.sbuf_tensor(name, shape, dt))

        s = State()
        s.consts = sb("consts", [P, CONSTS.shape[1]])
        s.ones = sb("ones", [P, P])
        s.rows = sb("rows", [P, 2 * NB], I32)
        s.hT = sb("hT", [P, KD, NTOK])
        s.kiT = sb("kiT", [P, NTOK])
        s.kaT = sb("kaT", [P, NTOK])
        s.qis = sb("qis", [SR, QW])
        s.va = sb("va", [P, TT, KVW])
        s.wi = sb("wi", [P, TT, H])
        s.bank = ctx.enter_context(nc.psum_tensor("bank", [P, 8, 512], F32))
        s.h2 = nc.dram_tensor("h2_rows", (NTOK, D), F32, kind="Internal").ap()
        s.slots = nc.dram_tensor("slot_table", (MAXB * BLK, TABW), I32, kind="Internal").ap()
        s.x1 = nc.dram_tensor("residual_rows", (NTOK, D), F32, kind="Internal").ap()
        s.y = nc.dram_tensor("expert_rows", (MAXB * BLK, D), F32, kind="Internal").ap()
        s.logit = sb("logit", [P, TT, NG + NE])
        with ExitStack() as attn:
            def sa(name, shape, dt=F32):
                return attn.enter_context(nc.sbuf_tensor(name, shape, dt))
            s.oaT = sa("oaT", [P, PAIRS, NTOK])
            s.obT = sa("obT", [P, PAIRS, NTOK])
            with ExitStack() as samp:
                def ss(name, shape, dt=F32):
                    return samp.enter_context(nc.sbuf_tensor(name, shape, dt))
                s.qaS, s.qbS = ss("qaS", [P, PAIRS, SR]), ss("qbS", [P, PAIRS, SR])
                s.qiS = ss("qiS", [P, PAIRS, SR])
                s.kbS, s.vbS = ss("kbS", [P, PAIRS, SR]), ss("vbS", [SR, QW])
                with ExitStack() as qkv:
                    def sq(name, shape, dt=F32):
                        return qkv.enter_context(nc.sbuf_tensor(name, shape, dt))
                    s.qaT = sq("qaT", [P, PAIRS, SEQ])
                    s.qiT = sq("qiT", [P, PAIRS, SEQ])
                    s.qbT = sq("qbT", [P, PAIRS, SEQ])
                    s.kbT = sq("kbT", [P, PAIRS, SEQ])
                    s.vb = sq("vb", [P, TP, QW])
                    with nc.cleanup_on_exit():
                        project(nc, s, a, o)
                        gather_rows(nc, s, a)
                        prompt(nc, s)
                s.newA = ss("newA", [P, NB // 4, SR])
                s.turned = ss("turned", [SR, P * SLOT])
                with nc.cleanup_on_exit():
                    sample(nc, s, a)
            with nc.cleanup_on_exit():
                merge(nc, s, a)
        s.w12 = sb("w12", [P, 2, TT])
        s.slot = sb("slot", [P, 2, TT], I32)
        s.be = sb("block_expert", [1, MAXB], I32)
        s.npair = sb("npair", [1, 1], I32)
        with nc.cleanup_on_exit():
            route(nc, s, a)
            experts(nc, s, a)
            combine(nc, s, a, o)


def project(nc, s, a, o):
    w_in = a["w_in"][0].rearrange("(k p) n -> p k n", p=P)
    GROUPS = ["kv", "qi", "qa", "kb", "qb", "vb"]
    COLS = {"kv": [(C_KA, 2 * KVW), (C_KI, HD + H)], "qi": [(C_QI, QW)], "qa": [(C_QA, QW)],
            "kb": [(C_KB, QW)], "qb": [(C_QB, QW)], "vb": [(C_VB, QW)]}
    WID = {g: sum(w for _, w in COLS[g]) for g in GROUPS}
    ITEMS = [(g, t) for g in GROUPS for t in range(TT)]
    NNAT = 3
    with ExitStack() as ctx:
        def sb(name, shape, dt=F32):
            return ctx.enter_context(nc.sbuf_tensor(name, shape, dt))

        def sem(name):
            return nc.alloc_semaphore(name)

        x = sb("x_pj", [P, TT, D])
        gmix = sb("gmix", [P, D])
        junk = sb("junk", [P, D])
        h = sb("h", [P, 2, D])
        ss = sb("ss", [P, TT])
        rr = sb("rr", [P, TT])
        w = sb("w", [P, 2, KD, 512])
        nat = sb("nat", [P, NNAT, 512])
        rt = sb("rt", [P, 2, H, ROT])
        zrow = sb("zrow", [P, 2 * TABW], I32)
        x_in = [sem(f"pj_x_in{t}") for t in range(TT)]
        c_in, g_in = sem("pj_consts_in"), sem("pj_g_in")
        w_in_s = [sem("pj_w_in0"), sem("pj_w_in1")]
        w_used = sem("pj_w_used")
        ss_ready, root_ready = sem("pj_ss_ready"), sem("pj_root_ready")
        ss_set = sem("pj_ss_set")
        h_ready, hT_done, hT_kept = sem("pj_h_ready"), sem("pj_hT_done"), sem("pj_hT_kept")
        proj_done, nat_ready = sem("pj_proj_done"), sem("pj_nat_ready")
        rot_ready, tr_done, tr_kept = sem("pj_rot_ready"), sem("pj_tr_done"), sem("pj_tr_kept")
        stored = [sem(f"pj_stored{i}") for i in range(NNAT)]
        vb_stored = sem("pj_vb_stored")
        zero_ready, zero_done = sem("pj_zero_ready"), sem("pj_zero_done")
        chain_v = sem("pj_vector_chain")
        block = ctx.enter_context(nc.Block())
        bank = s.bank
        natural = [n for n, (g, t) in enumerate(ITEMS) if g != "vb"]
        order = {n: i for i, n in enumerate(natural)}

        def nat_stores(upto, ring):
            return 16 * sum({"kv": 3, "kb": 1}.get(ITEMS[natural[i]][0], 0)
                            for i in range(ring, upto, NNAT))

        @block.sync
        def _(sp):
            sp.dma_start(s.consts[:, :], a["consts"]).then_inc(c_in, 16)
            for t in range(TP):
                sp.dma_start(x[:, t, :], a["x_prompt"][0, t * P:(t + 1) * P, :]).then_inc(x_in[t], 16)
            sp.dma_start(x[0:SR, TP, :], a["x_sample"].rearrange("b q d -> (b q) d")).then_inc(x_in[TP], 16)
            sp.dma_start(gmix[:, :], a["g_mix"].to_broadcast([P, D])).then_inc(g_in, 16)
            for gi, g in enumerate(GROUPS):
                if gi >= 2:
                    sp.wait_ge(w_used, gi - 1)
                at = 0
                for c, n in COLS[g]:
                    sp.dma_start(w[:, gi % 2, :, at:at + n], w_in[:, :, c:c + n]).then_inc(w_in_s[gi % 2], 16)
                    at += n

        def w_arrived(gi):
            return 16 * sum(len(COLS[GROUPS[k]]) for k in range(gi % 2, gi + 1, 2))

        @block.gpsimd
        def _(pool):
            nc.gpsimd.memset(s.ones[:, :], 1.0)
            nc.gpsimd.memset(zrow[:, :], 0).then_inc(zero_ready, 1)
            pool.wait_ge(zero_ready, 1)
            n = s.slots.shape[0] // P
            nz = 0
            for k in range(n):
                pool.dma_start(s.slots[k * P:(k + 1) * P, :], zrow[:, 0:TABW]).then_inc(zero_done, 16)
                nz += 1
            for n, (g, t) in enumerate(ITEMS):
                rows = rows_of(t)

                def out(name, c0, c1):
                    src = ((s.vb[:, t, :] if t < TP else s.vbS[:, :]) if g == "vb" else nat[0:rows, order[n] % NNAT, c0:c1])
                    sem_of = vb_stored if g == "vb" else stored[order[n] % NNAT]
                    if t < TP:
                        dst = o[name + "_p"][t * P:(t + 1) * P, :]
                    else:
                        dst = o[name + "_s"]
                    pool.dma_start(dst, src).then_inc(sem_of, 16)

                if g == "vb":
                    pool.wait_ge(nat_ready, n + 1)
                    out("v_b", 0, QW)
                elif g in ("kv", "kb"):
                    pool.wait_ge(rot_ready, order[n] + 1)
                    if g == "kv":
                        out("k_a", 0, KVW)
                        out("v_a", KVW, 2 * KVW)
                        out("k_idx", 2 * KVW, 2 * KVW + HD)
                    else:
                        out("k_b", 0, QW)
            pool.wait_ge(zero_done, 16 * nz)
            pool.wait_ge(vb_stored, 16 * TT)
            for i in range(NNAT):
                pool.wait_ge(stored[i], nat_stores(len(natural), i))

        @block.scalar
        def _(act):
            act.wait_ge(ss_set, 1)
            for t in range(TT):
                act.wait_ge(x_in[t], 16)
                rows = rows_of(t)
                nc.scalar.activation(junk[0:rows, :], x[0:rows, t, :], ACT.Square,
                                     accum_out=ss[0:rows, t:t + 1]).then_inc(ss_ready, 1)
                act.wait_ge(ss_ready, t + 1)
            act.wait_ge(root_ready, 1)
            nc.scalar.activation(ss[:, :], rr[:, :], ACT.Sqrt).then_inc(ss_ready, 1)

            def keep_hT(t):
                for c in range(2):
                    act.wait_ge(hT_done, 2 * t + c + 1)
                    nc.scalar.copy(s.hT[:, 4 * c:4 * c + 4, t * P:t * P + rows_of(t)],
                                   bank[:, 4 + c, :].rearrange("p (k r) -> p k r", k=4)[:, :, 0:rows_of(t)])\
                        .then_inc(hT_kept, 1)

            def keep_transposed(n):
                g, t = ITEMS[n]
                r, c = rows_of(t), slice(t * P, t * P + rows_of(t))
                act.wait_ge(tr_done, order[n] + 1)
                tb = bank[:, 4 + order[n] % 2, :].rearrange("p (k r) -> p k r", k=4)
                if g == "kv":
                    nc.scalar.copy(s.kaT[:, c], tb[:, 0, 0:r])
                    nc.scalar.copy(s.kiT[:, c], tb[:, 1, 0:r]).then_inc(tr_kept, 1)
                else:
                    dst = ({"qi": s.qiT, "qa": s.qaT, "qb": s.qbT, "kb": s.kbT}[g][:, :, c] if t < TP else
                           {"qi": s.qiS, "qa": s.qaS, "qb": s.qbS, "kb": s.kbS}[g][:, :, :])
                    nc.scalar.copy(dst, tb[:, :, 0:r]).then_inc(tr_kept, 1)

            for t in range(TT):
                keep_hT(t)
            for n, (g, t) in enumerate(ITEMS):
                rows = rows_of(t)
                act.wait_ge(proj_done, n + 1)
                if g == "vb":
                    nc.scalar.copy(s.vb[:, t, :] if t < TP else s.vbS[:, :], bank[0:rows, n % 4, :]).then_inc(nat_ready, 1)
                else:
                    i = order[n]
                    if i >= NNAT:
                        act.wait_ge(tr_done, i - NNAT + 1)
                        if nat_stores(i, i % NNAT):
                            act.wait_ge(stored[i % NNAT], nat_stores(i, i % NNAT))
                    dst, src = nat[0:rows, i % NNAT, 0:WID[g]], bank[0:rows, n % 4, 0:WID[g]]
                    if g == "qa":
                        dst = dst.rearrange("p (j a d) -> p a j d", a=2, d=HD)
                        src = src.rearrange("p (a j d) -> p a j d", a=2, d=HD)
                    nc.scalar.copy(dst, src).then_inc(nat_ready, 1)
                if n >= 1 and n - 1 in order:
                    keep_transposed(n - 1)
            if len(ITEMS) - 1 in order:
                keep_transposed(len(ITEMS) - 1)

        @block.vector
        def _(dve):
            link = Chain(dve, chain_v)
            nc.vector.memset(ss[:, :], 1.0).then_inc(ss_set, 1)
            dve.wait_ge(ss_ready, TT)
            nc.vector.tensor_scalar(rr[:, :], ss[:, :], 1.0 / D, EPS, ALU.mult, ALU.add).then_inc(root_ready, 1)
            dve.wait_ge(ss_ready, TT + 1)
            link(nc.vector.reciprocal(rr[:, :], ss[:, :]))
            dve.wait_ge(g_in, 16)
            for t in range(TT):
                rows = rows_of(t)
                if t >= 2:
                    dve.wait_ge(hT_done, 2 * (t - 1))
                nc.vector.scalar_tensor_tensor(h[0:rows, t % 2, :], x[0:rows, t, :], rr[0:rows, t:t + 1],
                                               gmix[0:rows, :], ALU.mult, ALU.mult).then_inc(h_ready, 1)
            for n in natural:
                g, t = ITEMS[n]
                rows, i = rows_of(t), order[n]
                dve.wait_ge(nat_ready, n + 1)
                b = nat[0:rows, i % NNAT, :]
                spans = [(0, H)]
                if g == "kv":
                    link(nc.vector.tensor_copy(s.va[0:rows, t, :], b[:, KVW:2 * KVW]))
                    link(nc.vector.tensor_scalar(s.wi[0:rows, t, :], b[:, 2 * KVW + HD:2 * KVW + HD + H],
                                                 IDX_SCALE, None, ALU.mult))
                    spans = [(0, 2), (2 * KVW, 1)]
                for c0, nh in spans:
                    v = b[:, c0:c0 + nh * HD].rearrange("p (h d) -> p h d", d=HD)
                    xr = v[:, :, 0:ROT]
                    cos = const(s, "cos", rows)[:, t * ROT:(t + 1) * ROT].unsqueeze(1).to_broadcast([rows, nh, ROT])
                    sin = const(s, "sin", rows)[:, t * ROT:(t + 1) * ROT].unsqueeze(1).to_broadcast([rows, nh, ROT])
                    rc, rs = rt[0:rows, 0, 0:nh, :], rt[0:rows, 1, 0:nh, :]
                    hf = ROT // 2
                    nc.vector.tensor_tensor(rc, xr, cos, ALU.mult)
                    link(nc.vector.tensor_tensor(rs, xr, sin, ALU.mult))
                    nc.vector.tensor_tensor(v[:, :, 0:hf], rc[:, :, 0:hf], rs[:, :, hf:ROT], ALU.subtract)
                    final = g != "kv" and not (g == "qi" and t == TP)
                    link(nc.vector.tensor_tensor(v[:, :, hf:ROT], rc[:, :, hf:ROT], rs[:, :, 0:hf], ALU.add),
                         rot_ready if final else None)
                if g == "qi" and t == TP:
                    link(nc.vector.tensor_copy(s.qis[:, :], b), rot_ready)
                if g == "kv":
                    src = b[:, 2 * KVW:2 * KVW + HD].unsqueeze(1).to_broadcast([rows, 2, HD])
                    link(nc.vector.tensor_copy(b[:, 384:512].rearrange("p (a d) -> p a d", a=2), src), rot_ready)

        @block.tensor
        def _(pe):
            pe.wait_ge(c_in, 16)
            ident = const(s, "ident")
            for t in range(TT):
                rows = rows_of(t)
                pe.wait_ge(h_ready, t + 1)
                for c in range(2):
                    if t >= 1:
                        pe.wait_ge(hT_kept, 2 * t + c - 1)
                    for k in range(4):
                        kk = 4 * c + k
                        last = nc.tensor.transpose(bank[:, 4 + c, k * P:k * P + rows],
                                                   h[0:rows, t % 2, kk * P:(kk + 1) * P], ident[0:rows, 0:rows])
                    last.then_inc(hT_done, 1)
            pe.wait_ge(hT_kept, 2 * TT)

            def transposes(n):
                g, t = ITEMS[n]
                rows, i = rows_of(t), order[n]
                pe.wait_ge(rot_ready, i + 1)
                if i >= 2:
                    pe.wait_ge(tr_kept, i - 1)
                b = nat[0:rows, i % NNAT, :]
                if g == "kv":
                    src = [b[:, 0:P], b[:, 384:512]]
                else:
                    src = [b[:, j * P:(j + 1) * P] for j in range(PAIRS)]
                for j, part in enumerate(src):
                    last = nc.tensor.transpose(bank[:, 4 + i % 2, j * P:j * P + rows], part, ident[0:rows, 0:rows])
                last.then_inc(tr_done, 1)

            for n, (g, t) in enumerate(ITEMS):
                gi, rows = GROUPS.index(g), rows_of(t)
                if t == 0:
                    pe.wait_ge(w_in_s[gi % 2], w_arrived(gi))
                if n >= 4:
                    pe.wait_ge(nat_ready, n - 3)
                for k in range(KD):
                    last = nc.tensor.matmul(bank[0:rows, n % 4, 0:WID[g]], s.hT[:, k, t * P:t * P + rows],
                                            w[:, gi % 2, k, 0:WID[g]], start=(k == 0), stop=(k == KD - 1))
                last.then_inc(proj_done, 1)
                if t == TT - 1:
                    pe.wait_ge(proj_done, n + 1)
                    pe.sem_inc(w_used, 1)
                if n >= 1 and n - 1 in order:
                    transposes(n - 1)
            if len(ITEMS) - 1 in order:
                transposes(len(ITEMS) - 1)


def topk_round(link, scores, best):
    link(nc_max(link, best, scores))
    link(nc_replace(link, scores, best))


def nc_max(link, best, scores):
    return link.eng.max(best, scores)


def nc_replace(link, scores, best):
    return link.eng.match_replace(scores, best, scores, PICKED)


def prompt(nc, s):
    IDX = [(t, h) for t in (1, 2, 3) for h in range(H)]
    ITEMS = [("b", t, h) for t in range(TP) for h in range(H)] + [("a", t, h) for t in range(TP) for h in range(H)]
    ROUNDS = [(t, r) for t in (1, 2, 3) for r in range(TOPK_P // 8)]
    EARLY = TP * H + (TP - 1) * H
    with ExitStack() as ctx:
        def sb(name, shape, dt=F32):
            return ctx.enter_context(nc.sbuf_tensor(name, shape, dt))

        def sem(name):
            return nc.alloc_semaphore(name)

        score = sb("score", [P, TP, SEQ])
        relu = sb("relu", [P, 2, SEQ])
        best = sb("best", [P, 8])
        prob = sb("prob", [P, 4, SEQ])
        probT = sb("probT", [P, 2, SEQ])
        top = sb("top", [P, 4])
        ntop = sb("ntop", [P, 4])
        total = sb("total", [P, 4])
        inv = sb("inv", [P, 4])
        zeros = sb("zeros", [P, D])
        idx_done, relu_done, acc_done = sem("pr_idx_done"), sem("pr_relu_done"), sem("pr_acc_done")
        qk_done, top_done, exp_done = sem("pr_qk_done"), sem("pr_top_done"), sem("pr_exp_done")
        norm_done, tr_done, tr_kept = sem("pr_norm_done"), sem("pr_tr_done"), sem("pr_tr_kept")
        pv_done, o_kept, chain_v = sem("pr_pv_done"), sem("pr_o_kept"), sem("pr_vector_chain")
        inv_ready = sem("pr_inv_ready")
        zeros_ready, zeros_stored = sem("pr_zeros_ready"), sem("pr_zeros_stored")
        bank = s.bank
        block = ctx.enter_context(nc.Block())

        def width(t):
            return (t + 1) * P

        def place(kind, h):
            return (h // PAIRS, h % PAIRS) if kind == "a" else (h % 2, h // 2)

        @block.sync
        def _(sp):
            sp.wait_ge(zeros_ready, 1)
            first = -(-2 * NTOK // BLK) * BLK // P * P
            for r in range(first, MAXB * BLK, P):
                sp.dma_start(s.y[r:r + P, :], zeros[:, :]).then_inc(zeros_stored, 16)
            sp.wait_ge(zeros_stored, 16 * ((MAXB * BLK - first) // P))

        @block.gpsimd
        def _(pool):
            for m, (_, t, _) in enumerate(ITEMS):
                pool.wait_ge(inv_ready, m + 1)
                p = prob[:, m % 4, 0:width(t)]
                nc.gpsimd.tensor_scalar(p, p, inv[:, m % 4:m % 4 + 1], None, ALU.mult).then_inc(norm_done, 1)

        @block.tensor
        def _(pe):
            ident = const(s, "ident")
            for q, (t, h) in enumerate(IDX):
                if q >= 3:
                    pe.wait_ge(relu_done, q - 2)
                r = slice(h % 2 * HD, h % 2 * HD + HD)
                nc.tensor.matmul(bank[:, q % 3, 0:width(t)], s.qiT[r, h // 2, t * P:(t + 1) * P],
                                 s.kiT[r, 0:width(t)], start=True, stop=True).then_inc(idx_done, 1)
            pe.wait_ge(relu_done, len(IDX))

            def scores(m):
                kind, t, h = ITEMS[m]
                half, pair = place(kind, h)
                r = slice(half * HD, half * HD + HD)
                if m >= 4:
                    pe.wait_ge(exp_done, m - 3)
                qT = s.qaT if kind == "a" else s.qbT
                kT = s.kaT[r, 0:width(t)] if kind == "a" else s.kbT[r, pair, 0:width(t)]
                nc.tensor.matmul(bank[:, m % 4, 0:width(t)], qT[r, pair, t * P:(t + 1) * P], kT,
                                 start=True, stop=True).then_inc(qk_done, 1)

            def turn(m):
                kind, t, h = ITEMS[m]
                pe.wait_ge(norm_done, m + 1)
                if m >= 2:
                    pe.wait_ge(tr_kept, m - 1)
                for c in range(t + 1):
                    last = nc.tensor.transpose(bank[:, 4 + m % 2, c * P:(c + 1) * P],
                                               prob[:, m % 4, c * P:(c + 1) * P], ident)
                last.then_inc(tr_done, 1)

            def weigh(m):
                kind, t, h = ITEMS[m]
                half, pair = place(kind, h)
                pe.wait_ge(tr_kept, m + 1)
                if m >= 2:
                    pe.wait_ge(o_kept, m - 1)
                for c in range(t + 1):
                    v = s.va[:, c, half * HD:(half + 1) * HD] if kind == "a" else s.vb[:, c, h * HD:(h + 1) * HD]
                    last = nc.tensor.matmul(bank[half * HD:(half + 1) * HD, 6 + m % 2, 0:P], v,
                                            probT[:, m % 2, c * P:(c + 1) * P], start=(c == 0), stop=(c == t))
                last.then_inc(pv_done, 1)

            n = len(ITEMS)
            for m in range(n + 4):
                if m < n:
                    scores(m)
                if 3 <= m < n + 3:
                    turn(m - 3)
                if m >= 4:
                    weigh(m - 4)

        @block.scalar
        def _(act):
            for q, (t, h) in enumerate(IDX):
                act.wait_ge(idx_done, q + 1)
                if q >= 2:
                    act.wait_ge(acc_done, q - 1)
                nc.scalar.activation(relu[:, q % 2, 0:width(t)], bank[:, q % 3, 0:width(t)], ACT.Relu)\
                    .then_inc(relu_done, 1)

            def exps(m):
                _, t, _ = ITEMS[m]
                act.wait_ge(top_done, m + 1)
                if m >= 4:
                    act.wait_ge(inv_ready, m - 3)
                if m >= 4:
                    act.wait_ge(tr_done, m - 3)
                nc.scalar.activation(prob[:, m % 4, 0:width(t)], bank[:, m % 4, 0:width(t)], ACT.Exp,
                                     bias=ntop[:, m % 4:m % 4 + 1], scale=SCALE,
                                     accum_out=total[:, m % 4:m % 4 + 1]).then_inc(exp_done, 1)

            def keep_turned(m):
                _, t, _ = ITEMS[m]
                act.wait_ge(tr_done, m + 1)
                if m >= 2:
                    act.wait_ge(pv_done, m - 1)
                nc.scalar.copy(probT[:, m % 2, 0:width(t)], bank[:, 4 + m % 2, 0:width(t)]).then_inc(tr_kept, 1)

            def keep_o(m):
                kind, t, h = ITEMS[m]
                half, pair = place(kind, h)
                r = slice(half * HD, half * HD + HD)
                act.wait_ge(pv_done, m + 1)
                nc.scalar.copy((s.oaT if kind == "a" else s.obT)[r, pair, t * P:(t + 1) * P],
                               bank[r, 6 + m % 2, 0:P]).then_inc(o_kept, 1)

            n = len(ITEMS)
            for m in range(n + 4):
                if m < n:
                    exps(m)
                if 3 <= m < n + 3:
                    keep_turned(m - 3)
                if m >= 4:
                    keep_o(m - 4)

        @block.vector
        def _(dve):
            nc.vector.memset(zeros[:, :], 0.0).then_inc(zeros_ready, 1)
            link = Chain(dve, chain_v)
            for q, (t, h) in enumerate(IDX):
                w = slice(0, width(t))
                dve.wait_ge(relu_done, q + 1)
                if h == 0:
                    link(nc.vector.tensor_scalar(score[:, t, w], relu[:, q % 2, w], s.wi[:, t, 0:1], None,
                                                 ALU.mult), acc_done)
                else:
                    link(nc.vector.scalar_tensor_tensor(score[:, t, w], relu[:, q % 2, w], s.wi[:, t, h:h + 1],
                                                        score[:, t, w], ALU.mult, ALU.add), acc_done)
                if h == H - 1:
                    d = slice(t * P, (t + 1) * P)
                    link(nc.vector.tensor_tensor(score[:, t, d], score[:, t, d], const(s, "absent"), ALU.add))

            def topk(r):
                t, k = ROUNDS[r]
                sc = score[:, t, 0:width(t)]
                topk_round(link, sc, best[:, :])
                if k == TOPK_P // 8 - 1:
                    link(nc.vector.tensor_scalar(sc, sc, EDGE, MASKED, ALU.is_gt, ALU.mult))

            def tops(m):
                kind, t, h = ITEMS[m]
                dve.wait_ge(qk_done, m + 1)
                if kind == "a" and t > 0:
                    w, bias = slice(0, width(t)), score[:, t, 0:width(t)]
                else:
                    w, bias = slice(t * P, (t + 1) * P), const(s, "causal")
                link(nc.vector.tensor_tensor(bank[:, m % 4, w], bank[:, m % 4, w], bias, ALU.add))
                link(nc.vector.reduce_max(top[:, m % 4:m % 4 + 1], bank[:, m % 4, 0:width(t)], AX.X))
                link(nc.vector.tensor_scalar(ntop[:, m % 4:m % 4 + 1], top[:, m % 4:m % 4 + 1], -SCALE, None,
                                             ALU.mult), top_done)

            n = len(ITEMS)
            for m in range(n + 1):
                if m < n:
                    tops(m)
                if m >= 1:
                    dve.wait_ge(exp_done, m)
                    if m >= 5:
                        dve.wait_ge(norm_done, m - 4)
                    k = (m - 1) % 4
                    link(nc.vector.reciprocal(inv[:, k:k + 1], total[:, k:k + 1]), inv_ready)
                if m < EARLY:
                    for r in range(m * len(ROUNDS) // EARLY, (m + 1) * len(ROUNDS) // EARLY):
                        topk(r)



def gather_rows(nc, s, a):
    with ExitStack() as ctx:
        table = ctx.enter_context(nc.sbuf_tensor("table", [P, NB * NPG], I32))
        tabf = ctx.enter_context(nc.sbuf_tensor("tabf", [P, 2 * NB, HPG], F32))
        rowf = ctx.enter_context(nc.sbuf_tensor("rowf", [P, 2 * NB], F32))
        table_in = nc.alloc_semaphore("gr_table_in")
        chain_v = nc.alloc_semaphore("gr_vector_chain")
        block = ctx.enter_context(nc.Block())

        @block.sync
        def _(sp):
            sp.dma_start(table[:, :], a["page_table"].rearrange("b g -> (b g)").unsqueeze(0)
                         .to_broadcast([P, NB * NPG])).then_inc(table_in, 16)

        @block.vector
        def _(dve):
            link = Chain(dve, chain_v)
            dve.wait_ge(table_in, 16)
            mine = const(s, "page_of")[:, 0:HPG].unsqueeze(1).to_broadcast([P, 2 * NB, HPG])
            link(nc.vector.tensor_copy(tabf[:, :, :].rearrange("p b g -> p (b g)"), table[:, :]))
            link(nc.vector.tensor_tensor(tabf[:, :, :], tabf[:, :, :], mine, ALU.mult))
            link(nc.vector.reduce_sum(rowf[:, :], tabf[:, :, :], AX.X))
            link(nc.vector.tensor_scalar(rowf[:, :], rowf[:, :], float(P // HPG), const(s, "within"),
                                         ALU.mult, ALU.add))
            link(nc.vector.tensor_copy(s.rows[:, :], rowf[:, :]))


def sample(nc, s, a):
    COLS = PAST + SR
    G = NB // 4
    HALF = P * SLOT
    QUADS = [("i", b, f, 0) for b in range(NB) for f in range(2)]
    QUADS += [("b", b, f, e) for b in range(NB) for f in range(2) for e in range(2)]
    QUADS += [("a", b, f, e) for b in range(NB) for f in range(2) for e in range(2)]
    LOTS = []
    for k, (kind, *_) in enumerate(QUADS):
        LOTS += [(k, n) for n in range(4 if kind == "b" else 1)]
    LAST = {k: n for n, (k, _) in enumerate(LOTS)}
    RES = [(k, n) for k, (kind, *_) in enumerate(QUADS) for n in range(2 if kind == "i" else 1)]
    NIDX = 2 * len([q for q in QUADS if q[0] == "i"])
    with ExitStack() as ctx:
        def sb(name, shape, dt=F32):
            return ctx.enter_context(nc.sbuf_tensor(name, shape, dt))

        def sem(name):
            return nc.alloc_semaphore(name)

        RI, RB, RA = 3, 3, 3
        ring = {"i": sb("half_i", [P, RI, SLOT * HD]), "b": sb("half_b", [P, RB, SLOT * QW]),
                "a": sb("half_a", [P, RA, SLOT * KVW])}
        kT = sb("kT_s", [P, 2, PAIRS, 4, P])
        qdup = sb("qdup", [SR, H, 2, HD])
        q_i = sb("q_i", [P, NB, 32])
        q_b = sb("q_b", [P, NB, PAIRS, 32])
        q_a = sb("q_a", [P, NB, 32])
        wrow = sb("wrow", [P, G, H])
        lg = {"i": sb("lg_i", [P, G, COLS]), "b": sb("lg_b", [P, G, COLS])}
        lg["a"] = lg["i"]
        row = sb("row", [SR, COLS])
        best, best8 = sb("best_s", [P, 8]), sb("best8_s", [SR, 8])
        gate = sb("gate", [P, 2 * NBLK_PAST])
        top = sb("top_s", [P, 4])
        ntop = sb("ntop_s", [P, 4])
        total = sb("total_s", [P, 4])
        inv = sb("inv_s", [P, 4])
        probT = [kT[:, r].rearrange("p j e n -> p (j e) n") for r in range(2)]
        newT = sb("newT_s", [SR, 2, P])
        o = {"b": sb("o_b", [P, G, QW]), "a": sb("o_a", [P, G, KVW])}
        in_i = [sem(f"sm_i_in{r}") for r in range(RI)]
        in_b = [sem(f"sm_b_in{r}") for r in range(RB)]
        in_a = [sem(f"sm_a_in{r}") for r in range(RA)]
        arrived = {"i": in_i, "b": in_b, "a": in_a}
        dup_ready, dupT_done, w_done, q_ready = sem("sm_dup"), sem("sm_dupT"), sem("sm_w_done"), sem("sm_q_ready")
        tr_done, kT_kept, qk_done, res_done = sem("sm_tr_done"), sem("sm_kT_kept"), sem("sm_qk_done"), sem("sm_res_done")
        idx_read, s_kept = sem("sm_idx_read"), sem("sm_s_kept")
        new_done, row_done, row_kept = sem("sm_new_done"), sem("sm_row_done"), sem("sm_row_kept")
        bias_ready, spread_done, spread_read = sem("sm_bias_ready"), sem("sm_spread_done"), sem("sm_spread_read")
        top_done, exp_done, norm_done = sem("sm_top_done"), sem("sm_exp_done"), sem("sm_norm_done")
        pT_done, pT_kept, pv_done, o_read = sem("sm_pT_done"), sem("sm_pT_kept"), sem("sm_pv_done"), sem("sm_o_read")
        oT_done, newT_done, chain_v = sem("sm_oT_done"), sem("sm_newT_done"), sem("sm_vector_chain")
        all_read = sem("sm_all_read")
        bank = s.bank
        TB, SB, XB = (0, 1, 2), (3, 4), (5, 6)
        NEWB = 7
        block = ctx.enter_context(nc.Block())
        SOFT = [("b", 0), ("b", 1), ("a", 0), ("a", 1)]
        caches = {"i": a["cache_k_idx"][0].rearrange("g (p e) d -> (g p) (e d)", e=SLOT)}
        for k, (kk, vv) in {"b": ("cache_k_b", "cache_v_b"), "a": ("cache_k_a", "cache_v_a")}.items():
            caches[k], caches["v" + k] = (a[n][0].rearrange("g (p e) h d -> (g p) (e h d)", e=SLOT)
                                          for n in (kk, vv))

        def half_of(k):
            _, b, f, _ = QUADS[k]
            return 2 * b + f

        def rows_at(b):
            return slice(b % 4 * 32, b % 4 * 32 + 32)

        def col0(r):
            k, n = RES[r]
            kind, b, f, e = QUADS[k]
            return f * HALF + (n if kind == "i" else e) * 512

        @block.gpsimd
        def _(pool):
            def gather(kind, cache, h, seen):
                r = (seen + h) % len(arrived[kind])
                pool.indirect_dma_start(ring[kind][:, r, :], None, caches[cache],
                                        bass.IndirectOffsetOnAxis(s.rows[:, h:h + 1], 0))\
                    .then_inc(arrived[kind][r], 16)

            first = {kind: min(n for n, (k, _) in enumerate(LOTS) if QUADS[k][0] == kind) for kind in "iba"}
            per = {kind: sum(1 for k, _ in LOTS if QUADS[k][0] == kind) // (2 * NB) for kind in "iba"}
            for kind in "iba":
                n = len(arrived[kind])
                for h in range(2 * NB):
                    if h >= n:
                        pool.wait_ge(tr_done, first[kind] + per[kind] * (h - n + 1))
                    gather(kind, kind, h, 0)
            for x, kind in enumerate("ba"):
                n = len(arrived[kind])
                for h in range(2 * NB):
                    if h < n:
                        pool.wait_ge(tr_done, first[kind] + per[kind] * (2 * NB - n + h + 1))
                    else:
                        pool.wait_ge(pv_done, x * 2 * NB + h - n + 1)
                    gather(kind, "v" + kind, h, 2 * NB)

        @block.tensor
        def _(pe):
            ident = const(s, "ident")
            pe.wait_ge(dup_ready, 1)
            for h in range(H):
                last = nc.tensor.transpose(bank[:, XB[0], h * SR:(h + 1) * SR],
                                           qdup[:, h, :, :].rearrange("r a d -> r (a d)"), ident[0:SR, 0:SR])
            last.then_inc(dupT_done, 1)
            for g in range(G):
                last = nc.tensor.matmul(bank[:, XB[1], g * H:(g + 1) * H], const(s, "spread", SR)[:, g * P:(g + 1) * P],
                                        s.wi[0:SR, TP, :], start=True, stop=True)
            last.then_inc(w_done, 1)
            pe.wait_ge(q_ready, 1)
            for b in range(NB):
                out = bank[rows_at(b), NEWB, b // 4 * 96:b // 4 * 96 + 96]
                nc.tensor.matmul(out[:, 0:32], q_i[0:HD, b, :], s.kiT[0:HD, SEQ:NTOK], start=True, stop=True)
                for j in range(PAIRS):
                    nc.tensor.matmul(out[:, 32:64], q_b[:, b, j, :], s.kbS[:, j, :],
                                     start=(j == 0), stop=(j == PAIRS - 1))
                last = nc.tensor.matmul(out[:, 64:96], q_a[:, b, :], s.kaT[:, SEQ:NTOK], start=True, stop=True)
            last.then_inc(new_done, 1)

            def turn(n):
                k, i = LOTS[n]
                kind, b, f, e = QUADS[k]
                h = half_of(k)
                r = h % len(arrived[kind])
                if i == 0 and e == 0:
                    pe.wait_ge(arrived[kind][r], 16 * (h // len(arrived[kind]) + 1))
                if n >= 3:
                    pe.wait_ge(kT_kept, n - 2)
                for j in range(4):
                    at = (4 * e + i) * QW + j * P if kind == "b" else (4 * e + j) * P
                    last = nc.tensor.transpose(bank[:, TB[n % 3], j * P:(j + 1) * P],
                                               ring[kind][:, r, at:at + P], ident)
                last.then_inc(tr_done, 1)

            def scores(k):
                kind, b, f, e = QUADS[k]
                pe.wait_ge(kT_kept, LAST[k] + 1)
                for n in range(2 if kind == "i" else 1):
                    r = RES.index((k, n))
                    if 2 <= r < NIDX + 2:
                        pe.wait_ge(idx_read, r - 1)
                    elif r >= 2:
                        pe.wait_ge(s_kept, r - NIDX - 1)
                    out = bank[rows_at(b), SB[r % 2], :]
                    if kind == "i":
                        d = slice(n * HD, n * HD + HD)
                        last = nc.tensor.matmul(out, q_i[d, b, :], kT[d, k % 2, 0, :, :].rearrange("d e p -> d (e p)"),
                                                start=True, stop=True)
                    elif kind == "a":
                        last = nc.tensor.matmul(out, q_a[:, b, :], kT[:, k % 2, 0, :, :].rearrange("d e p -> d (e p)"),
                                                start=True, stop=True)
                    else:
                        for j in range(PAIRS):
                            last = nc.tensor.matmul(out, q_b[:, b, j, :],
                                                    kT[:, k % 2, j, :, :].rearrange("d e p -> d (e p)"),
                                                    start=(j == 0), stop=(j == PAIRS - 1))
                    last.then_inc(res_done, 1)
                pe.wait_ge(res_done, RES.index((k, n)) + 1)
                pe.sem_inc(qk_done, 1)

            def index_rows():
                pe.wait_ge(all_read, 1)
                for c in range(5):
                    w = 512 if c < 4 else SR
                    if c >= 2:
                        pe.wait_ge(row_kept, c - 1)
                    for g in range(G):
                        last = nc.tensor.matmul(bank[0:SR, XB[c % 2], 0:w], const(s, "gathered")[:, g * SR:(g + 1) * SR],
                                                lg["i"][:, g, c * 512:c * 512 + w], start=(g == 0), stop=(g == G - 1))
                    last.then_inc(row_done, 1)

            for n in range(len(LOTS)):
                k, i = LOTS[n]
                turn(n)
                if n == LAST[k] and k >= 1:
                    scores(k - 1)
                    if k - 1 == NIDX // 2 - 1:
                        index_rows()
            scores(len(QUADS) - 1)

            def spread(g):
                pe.wait_ge(bias_ready, 1)
                for c in range(5):
                    w = 512 if c < 4 else SR
                    n = 5 * g + c
                    if n >= 2:
                        pe.wait_ge(spread_read, n - 1)
                    nc.tensor.matmul(bank[:, XB[n % 2], 0:w], const(s, "spread", SR)[:, g * P:(g + 1) * P],
                                     row[:, c * 512:c * 512 + w], start=True, stop=True).then_inc(spread_done, 1)

            def turn_rows(m):
                x, g = SOFT[m]
                pe.wait_ge(norm_done, m + 1)
                pe.wait_ge(s_kept, len(RES) - NIDX)
                for c in range(4):
                    n = 4 * m + c
                    if n >= 3:
                        pe.wait_ge(pT_kept, n - 2 + (n - 3) // 4)
                    for j in range(4):
                        at = (4 * c + j) * P
                        last = nc.tensor.transpose(bank[:, TB[n % 3], j * P:(j + 1) * P], lg[x][:, g, at:at + P], ident)
                    last.then_inc(pT_done, 1)
                if m >= 1:
                    pe.wait_ge(pT_kept, 5 * m)
                nc.tensor.transpose(bank[0:SR, NEWB, 0:P], lg[x][:, g, PAST:COLS], ident).then_inc(newT_done, 1)

            def weigh(m, samples):
                x, g = SOFT[m]
                pe.wait_ge(pT_kept, 5 * (m + 1))
                for b in samples:
                    n = (x == "a") * NB + b
                    if n >= 2:
                        pe.wait_ge(o_read, n - 1)
                    w = QW if x == "b" else KVW
                    out = bank[rows_at(b), SB[n % 2], 0:w]
                    for f in range(2):
                        h = 2 * b + f
                        v = h + 2 * NB
                        nr = len(arrived[x])
                        pe.wait_ge(arrived[x][v % nr], 16 * (v // nr + 1))
                        for e in range(SLOT):
                            last = nc.tensor.matmul(out, probT[m % 2][:, f * SLOT + e, rows_at(b)],
                                                    ring[x][:, v % nr, e * w:(e + 1) * w],
                                                    start=(f == 0 and e == 0), stop=False)
                        if f == 0:
                            last.then_inc(pv_done, 1)
                    last = nc.tensor.matmul(out, newT[:, m % 2, rows_at(b)], s.vbS[:, :] if x == "b" else s.va[0:SR, TP, :],
                                            start=False, stop=True)
                    last.then_inc(pv_done, 1)

            turn_rows(0)
            weigh(0, range(0, 2))
            turn_rows(1)
            weigh(0, range(2, 4))
            spread(0)
            weigh(1, range(4, 6))
            turn_rows(2)
            weigh(1, range(6, 8))
            spread(1)
            weigh(2, range(0, 2))
            turn_rows(3)
            weigh(2, range(2, 4))
            weigh(3, range(4, 8))
            for x in "ba":
                pe.wait_ge(o_read, 2 * NB)
                for j in range(PAIRS):
                    for g in range(G):
                        lhsT = o["b"][:, g, j * P:(j + 1) * P] if x == "b" else o["a"][:, g, :]
                        pick = (const(s, "gathered")[:, g * SR:(g + 1) * SR] if x == "b" else
                                const(s, "gathered_j")[:, (j * G + g) * SR:(j * G + g + 1) * SR])
                        last = nc.tensor.matmul(bank[:, XB[x == "a"], j * SR:(j + 1) * SR], lhsT, pick,
                                                start=(g == 0), stop=(g == G - 1))
            last.then_inc(oT_done, 1)

        @block.scalar
        def _(act):
            def keep_lot(n):
                k, i = LOTS[n]
                kind = QUADS[k][0]
                act.wait_ge(tr_done, n + 1)
                if i == 0 and k >= 2:
                    act.wait_ge(qk_done, k - 1)
                src = bank[:, TB[n % 3], :].rearrange("p (j n) -> p j n", j=4)
                dst = kT[:, k % 2, :, i, :] if kind == "b" else kT[:, k % 2, 0, :, :]
                nc.scalar.copy(dst, src).then_inc(kT_kept, 1)

            def keep_scores(k):
                kind, b, f, e = QUADS[k]
                if kind == "i":
                    return
                r = RES.index((k, 0))
                act.wait_ge(res_done, r + 1)
                if kind == "a" and (b, f, e) == (0, 0, 0):
                    act.wait_ge(row_done, 5)
                nc.scalar.copy(lg[kind][rows_at(b), b // 4, col0(r):col0(r) + 512], bank[rows_at(b), SB[r % 2], :])\
                    .then_inc(s_kept, 1)

            for n in range(len(LOTS)):
                k, i = LOTS[n]
                keep_lot(n)
                if n == LAST[k] and k >= 1:
                    keep_scores(k - 1)
                    if k - 1 == NIDX // 2 - 1:
                        for c in range(4):
                            act.wait_ge(row_done, c + 1)
                            keys = row[:, 0:PAST].rearrange("r (f p j e) -> r f e j p", f=2, j=4, e=2)
                            nc.scalar.copy(keys[:, c // 2, c % 2, :, :],
                                           bank[0:SR, XB[c % 2], :].rearrange("r (j p) -> r j p", j=4))\
                                .then_inc(row_kept, 1)
            keep_scores(len(QUADS) - 1)
            for m, (x, g) in enumerate(SOFT):
                act.wait_ge(top_done, m + 1)
                nc.scalar.activation(lg[x][:, g, :], lg[x][:, g, :], ACT.Exp, bias=ntop[:, m:m + 1], scale=SCALE,
                                     accum_out=total[:, m:m + 1]).then_inc(exp_done, 1)
                for c in range(4):
                    n = 4 * m + c
                    act.wait_ge(pT_done, n + 1)
                    if c == 0 and m >= 2:
                        act.wait_ge(pv_done, 8 * (m - 1))
                    nc.scalar.copy(probT[m % 2][:, 4 * c:4 * c + 4, :],
                                   bank[:, TB[n % 3], :].rearrange("p (j n) -> p j n", j=4)).then_inc(pT_kept, 1)
                act.wait_ge(newT_done, m + 1)
                nc.scalar.copy(newT[:, m % 2, :], bank[0:SR, NEWB, 0:P]).then_inc(pT_kept, 1)

        def outputs(dve, link, m, between=None):
            x, g = SOFT[m]
            for b in range(4 * g, 4 * g + 4):
                n = (x == "a") * NB + b
                w = QW if x == "b" else KVW
                dve.wait_ge(pv_done, 2 * n + 2)
                link(nc.vector.tensor_tensor(o[x][rows_at(b), g, :], bank[rows_at(b), SB[n % 2], 0:w],
                                             const(s, "own_" + x)[rows_at(b), :], ALU.mult), o_read)
                if between:
                    between()

        @block.vector
        def _(dve):
            link = Chain(dve, chain_v)
            link(nc.vector.tensor_copy(qdup[:, :, :, :], s.qis[:, :].rearrange("r (h d) -> r h d", d=HD)
                                       .unsqueeze(2).to_broadcast([SR, H, 2, HD])), dup_ready)
            link(nc.vector.memset(q_a[:, :, :], 0.0))
            link(nc.vector.memset(q_b[:, :, :, :], 0.0))
            for half in range(2):
                r = slice(half * HD, half * HD + HD)
                link(nc.vector.tensor_copy(
                    q_a[r, :, half * 16:half * 16 + 16].rearrange("p b (j q) -> p b j q", q=NQ),
                    s.qaS[r, :, :].rearrange("p j (b q) -> p b j q", q=NQ)))
                for j in range(PAIRS):
                    c = (2 * j + half) * NQ
                    link(nc.vector.tensor_copy(q_b[r, :, j, c:c + NQ],
                                               s.qbS[r, j, :].rearrange("p (b q) -> p b q", q=NQ)))
            dve.wait_ge(w_done, 1)
            hm = const(s, "head_of").unsqueeze(1).to_broadcast([P, G, H])
            link(nc.vector.tensor_tensor(wrow[:, :, :], bank[:, XB[1], 0:G * H].rearrange("p (g h) -> p g h", h=H),
                                         hm, ALU.mult))
            link(nc.vector.reduce_sum(total[:, 0:G], wrow[:, :, :], AX.X))
            link(nc.vector.tensor_copy(top[:, 0:G], total[:, 0:G]))
            dve.wait_ge(dupT_done, 1)
            link(nc.vector.tensor_copy(q_i[:, :, :].rearrange("p b (h q) -> p b h q", q=NQ),
                                       bank[:, XB[0], 0:H * SR].rearrange("p (h b q) -> p b h q", h=H, q=NQ)), q_ready)
            dve.wait_ge(new_done, 1)
            for g in range(G):
                nb = bank[:, NEWB, 96 * g:96 * g + 96]
                link(nc.vector.tensor_scalar(lg["i"][:, g, PAST:COLS], nb[:, 0:32], 0.0, top[:, g:g + 1],
                                             ALU.max, ALU.mult))
                link(nc.vector.tensor_tensor(lg["b"][:, g, PAST:COLS], nb[:, 32:64],
                                             const(s, "new_masked")[:, g * SR:(g + 1) * SR], ALU.add))
                link(nc.vector.tensor_copy(s.newA[:, g, :], nb[:, 64:96]))
            for r in range(NIDX):
                b = QUADS[RES[r][0]][1]
                dve.wait_ge(res_done, r + 1)
                link(nc.vector.tensor_scalar(lg["i"][rows_at(b), b // 4, col0(r):col0(r) + 512],
                                             bank[rows_at(b), SB[r % 2], :], 0.0, top[rows_at(b), b // 4:b // 4 + 1],
                                             ALU.max, ALU.mult), idx_read)
            dve.sem_inc(all_read, 1)
            dve.wait_ge(row_done, 5)
            link(nc.vector.tensor_tensor(row[:, PAST:COLS], bank[0:SR, XB[0], 0:SR], const(s, "new_absent", SR), ALU.add))
            dve.wait_ge(row_kept, 4)
            def rounds(n):
                for _ in range(n):
                    topk_round(link, row[:, :], best8[:, :])

            def bias_of_choice():
                link(nc.vector.tensor_scalar(row[:, PAST:COLS], row[:, PAST:COLS], EDGE, MASKED, ALU.is_gt, ALU.mult))
                for f in range(2):
                    keys = row[:, f * HALF:(f + 1) * HALF]
                    link(nc.vector.tensor_scalar(s.turned[:, :].rearrange("r (e p) -> r p e", e=SLOT),
                                                 keys.rearrange("r (p e) -> r p e", e=SLOT), EDGE, MASKED,
                                                 ALU.is_gt, ALU.mult))
                    link(nc.vector.tensor_copy(keys, s.turned[:, :]), bias_ready if f == 1 else None)

            def mask(m):
                x, g = SOFT[m]
                L = lg[x][:, g, :]
                halves = [L[:, f * HALF:(f + 1) * HALF].rearrange("r (e n w) -> r n e w", n=4, w=32) for f in range(2)]
                if x == "b":
                    dve.wait_ge(s_kept, 4 * 4 * (g + 1))
                    for f in range(2):
                        link(nc.vector.tensor_reduce(gate[:, 4 * f:4 * f + 4], halves[f], AX.XY, ALU.add))
                    link(nc.vector.memset(gate[:, NBLK_PAST:2 * NBLK_PAST], DUMMY))
                    link(nc.vector.max(best[:, :], gate[:, 0:NBLK_PAST]))
                    link(nc.vector.memset(best[:, TOPB:8], DUMMY))
                    link(nc.vector.match_replace(gate[:, :], best[:, :], gate[:, :], PICKED))
                    link(nc.vector.tensor_scalar(gate[:, 0:NBLK_PAST], gate[:, 0:NBLK_PAST], EDGE, MASKED,
                                                 ALU.is_gt, ALU.mult))
                    for n in range(NBLK_PAST):
                        part = halves[n // 4][:, n % 4, :, :]
                        link(nc.vector.tensor_scalar(part, part, gate[:, n:n + 1], None, ALU.add))
                else:
                    dve.wait_ge(s_kept, len(RES) - NIDX)
                    link(nc.vector.tensor_tensor(L[:, PAST:COLS], s.newA[:, g, :],
                                                 const(s, "new_masked")[:, g * SR:(g + 1) * SR], ALU.add))
                    for c in range(5):
                        w = 512 if c < 4 else SR
                        n = 5 * g + c
                        dve.wait_ge(spread_done, n + 1)
                        part = L[:, c * 512:c * 512 + w]
                        link(nc.vector.tensor_tensor(part, part, bank[:, XB[n % 2], 0:w], ALU.add), spread_read)
                link(nc.vector.reduce_max(top[:, m:m + 1], L, AX.X))
                link(nc.vector.tensor_scalar(ntop[:, m:m + 1], top[:, m:m + 1], -SCALE, None, ALU.mult), top_done)

            def normalise(m):
                x, g = SOFT[m]
                dve.wait_ge(exp_done, m + 1)
                link(nc.vector.reciprocal(inv[:, m:m + 1], total[:, m:m + 1]))
                link(nc.vector.tensor_scalar(lg[x][:, g, :], lg[x][:, g, :], inv[:, m:m + 1], None, ALU.mult), norm_done)

            ROUNDS = TOPK_S // 8
            LATE = 4
            rounds(ROUNDS * 5 // 8)
            mask(0)
            mask(1)
            rounds(ROUNDS - ROUNDS * 5 // 8 - LATE)
            normalise(0)
            normalise(1)
            outputs(dve, link, 0, lambda: rounds(LATE // 4))
            bias_of_choice()
            for m in (2, 3):
                mask(m)
                normalise(m)
                outputs(dve, link, m - 1)
            outputs(dve, link, len(SOFT) - 1)
            dve.wait_ge(oT_done, 1)
            for x, dst in (("b", s.obT), ("a", s.oaT)):
                link(nc.vector.tensor_copy(dst[:, :, SEQ:NTOK], bank[:, XB[x == "a"], 0:PAIRS * SR]
                                           .rearrange("p (j r) -> p j r", j=PAIRS)))


def merge(nc, s, a):
    w_in = a["w_in"][0].rearrange("(k p) n -> p k n", p=P)
    NCH = D // P
    HALF = NTOK // 2
    with ExitStack() as ctx:
        def sb(name, shape, dt=F32):
            return ctx.enter_context(nc.sbuf_tensor(name, shape, dt))

        def sem(name):
            return nc.alloc_semaphore(name)

        gw = sb("gate_w", [P, 2, KD, P])
        gh, gl = sb("gate_w_hi", [P, 2, 2, KD, P]), sb("gate_w_lo", [P, 2, 2, KD, P])
        bw = sb("branch_w", [P, 2, 2, PAIRS, P])
        hTh, hTl = sb("hT_hi", [P, KD, NTOK]), sb("hT_lo", [P, KD, NTOK])
        wo = sb("w_o", [P, KD, D])
        wr = sb("w_router", [P, KD, NG + NE])
        xp = s.hT[:, :, :].rearrange("p k r -> p (k r)")[:, 0:TP * D].rearrange("p (t d) -> p t d", d=D)
        xs = sb("x_sample_mg", [SR, D])
        gf = sb("g_ffn", [P, D])
        sig = sb("sig", [P, 4 * NTOK])
        sg = sig[:, :].rearrange("p (a b r) -> p a b r", a=2, b=2)
        part = sb("part", [P, NTOK])
        junk = sb("junk_mg", [P, D])
        uT = sb("uT", [P, KD, NTOK])
        h2 = bw[:, :, :, :, :].rearrange("p a b k n -> p a (b k n)")
        h2T = sig[:, 0:2 * D].rearrange("p (a d) -> p a d", a=2)
        ss, rr = sb("ss_mg", [P, TT]), sb("rr_mg", [P, TT])
        gate_in = sem("mg_gate_in")
        br_in = [sem("mg_branch_in0"), sem("mg_branch_in1")]
        out_in, x_in, gf_in, r_in = (sem("mg_" + n) for n in ("out_in", "x_in", "gf_in", "r_in"))
        hT_split, gate_split = sem("mg_hT_split"), sem("mg_gate_split")
        prod_done = sem("mg_product_done")
        sig_ready, u_ready, mul_done = sem("mg_sigmoid_ready"), sem("mg_u_ready"), sem("mg_multiplied")
        out_done, x_ready = sem("mg_out_done"), sem("mg_x_ready")
        sq_ready, mean_ready, root_ready = sem("mg_square_ready"), sem("mg_mean_ready"), sem("mg_root_ready")
        h2_ready, h2T_done, h2T_kept = sem("mg_h2_ready"), sem("mg_h2T_done"), sem("mg_h2T_kept")
        log_done, log_kept = sem("mg_logits_done"), sem("mg_logits_kept")
        set_ready = sem("mg_set_ready")
        h2_stored = [sem("mg_h2_stored0"), sem("mg_h2_stored1")]
        x_stored = sem("mg_x_stored")
        chain_v = sem("mg_vector_chain")
        block = ctx.enter_context(nc.Block())
        bank = s.bank

        def row_of(t):
            return xp[:, t, :] if t < TP else xs[:, :]

        @block.sync
        def _(sp):
            def gates(c):
                if c >= 1:
                    sp.wait_ge(gate_split, 2 * c)
                for g in range(2):
                    c0 = C_GA + g * D + c * P
                    sp.dma_start(gw[:, g, :, :], w_in[:, :, c0:c0 + P]).then_inc(gate_in, 16)

            def branches(c):
                cols = slice(c * P, (c + 1) * P)
                for half in range(2):
                    sp.dma_start(bw[half * HD:half * HD + HD, c % 2, 0, :, :],
                                 a["w_br_a"][0, half * PAIRS * HD:(half + 1) * PAIRS * HD, cols]
                                 .rearrange("(j d) n -> d j n", d=HD)).then_inc(br_in[c % 2], 16)
                sp.dma_start(bw[:, c % 2, 1, :, :], a["w_br_b"][0, :, cols].rearrange("(j p) n -> p j n", p=P))\
                    .then_inc(br_in[c % 2], 16)

            gates(0)
            branches(0)
            branches(1)
            gates(1)
            sp.dma_start(wo[:, :, :], a["w_out"][0].rearrange("(k p) n -> p k n", p=P)).then_inc(out_in, 16)
            sp.wait_ge(hT_split, KD)
            sp.dma_start(xp, a["x_prompt"][0].rearrange("(t p) d -> p t d", p=P)).then_inc(x_in, 16)
            sp.dma_start(xs[:, :], a["x_sample"].rearrange("b q d -> (b q) d")).then_inc(x_in, 16)
            for c in range(2, NCH):
                gates(c)
                sp.wait_ge(prod_done, 4 * (c - 1))
                branches(c)
            sp.dma_start(gf[:, :], a["g_ffn"].to_broadcast([P, D])).then_inc(gf_in, 16)
            sp.dma_start(wr[:, :, 0:NG], a["w_grp"][0].rearrange("(k p) n -> p k n", p=P)).then_inc(r_in, 16)
            sp.dma_start(wr[:, :, NG:NG + NE], a["w_exp"][0].rearrange("(k p) n -> p k n", p=P)).then_inc(r_in, 16)
            for t in range(TT):
                rows = rows_of(t)
                sp.wait_ge(x_ready, 2 * t + 2)
                sp.dma_start(s.x1[t * P:t * P + rows, :], row_of(t)).then_inc(x_stored, 16)
                sp.wait_ge(h2_ready, t + 1)
                sp.dma_start(s.h2[t * P:t * P + rows, :], h2[0:rows, t % 2, :]).then_inc(h2_stored[t % 2], 16)
            sp.wait_ge(x_stored, 16 * TT)
            sp.wait_ge(h2_stored[0], 16 * ((TT + 1) // 2))
            sp.wait_ge(h2_stored[1], 16 * (TT // 2))

        @block.tensor
        def _(pe):
            for j in range(NCH):
                for i in range(4):
                    if i < 2:
                        pe.wait_ge(gate_split, 2 * j + i + 1)
                    elif i == 2:
                        pe.wait_ge(br_in[j % 2], 48 * (j // 2 + 1))
                    if j >= 1:
                        if i < 2:
                            pe.wait_ge(sig_ready, 2 * (j - 1) + i + 1)
                        else:
                            pe.wait_ge(mul_done, 2 * (j - 1) + i - 1)
                    for half in range(2):
                        rows = slice(half * HALF, (half + 1) * HALF)
                        out = bank[:, 2 * i + half, 0:HALF]
                        for k in range(KD if i < 2 else PAIRS):
                            if i >= 2:
                                last = nc.tensor.matmul(out, bw[:, j % 2, i - 2, k, :],
                                                        (s.oaT, s.obT)[i - 2][:, k, rows],
                                                        start=(k == 0), stop=(k == PAIRS - 1))
                                continue
                            if j == 0 and i == 0 and half == 0:
                                pe.wait_ge(hT_split, k + 1)
                            w_hi, w_lo = (v[:, j % 2, i, k, :].bitcast(F32R) for v in (gh, gl))
                            hi, lo = (v[:, k, rows].bitcast(F32R) for v in (hTh, hTl))
                            for c, (l, m) in enumerate(((w_hi, hi), (w_hi, lo), (w_lo, hi))):
                                last = nc.tensor.matmul(out, l, m, start=(k == 0 and c == 0),
                                                        stop=(k == KD - 1 and c == 2))
                    last.then_inc(prod_done, 1)
            pe.wait_ge(out_in, 16)
            pe.wait_ge(u_ready, NCH)

            def logits(t):
                rows = rows_of(t)
                pe.wait_ge(h2_ready, t + 1)
                for c in range(2):
                    if t >= 1:
                        pe.wait_ge(h2T_kept, 2 * (t - 1) + c + 1)
                    for k in range(4):
                        kk = 4 * c + k
                        last = nc.tensor.transpose(bank[:, 4 + c, k * P:k * P + rows],
                                                   h2[0:rows, t % 2, kk * P:(kk + 1) * P],
                                                   const(s, "ident")[0:rows, 0:rows])
                    last.then_inc(h2T_done, 1)

            def route_logits(t):
                rows = rows_of(t)
                pe.wait_ge(h2T_kept, 2 * t + 2)
                if t == 0:
                    pe.wait_ge(r_in, 32)
                if t >= 2:
                    pe.wait_ge(log_kept, t - 1)
                for k in range(KD):
                    last = nc.tensor.matmul(bank[0:rows, 6 + t % 2, 0:NG + NE], h2T[:, t % 2, k * P:k * P + rows],
                                            wr[:, k, :], start=(k == 0), stop=(k == KD - 1))
                last.then_inc(log_done, 1)

            for t in range(TT):
                rows = rows_of(t)
                for half in range(2):
                    n = 2 * t + half
                    if n >= 4:
                        pe.wait_ge(x_ready, n - 3)
                    for k in range(KD):
                        last = nc.tensor.matmul(bank[0:rows, n % 4, :], uT[:, k, t * P:t * P + rows],
                                                wo[:, k, half * 512:half * 512 + 512],
                                                start=(k == 0), stop=(k == KD - 1))
                    last.then_inc(out_done, 1)
                if t >= 1:
                    logits(t - 1)
                if t >= 2:
                    route_logits(t - 2)
            logits(TT - 1)
            route_logits(TT - 2)
            route_logits(TT - 1)

        @block.scalar
        def _(act):
            for j in range(NCH):
                if j >= 2:
                    act.wait_ge(u_ready, j - 1)
                for i in range(2):
                    act.wait_ge(prod_done, 4 * j + i + 1)
                    nc.scalar.activation(sg[:, j % 2, i, :].rearrange("p (b r) -> p b r", b=2),
                                         bank[:, 2 * i:2 * i + 2, 0:HALF], ACT.Sigmoid).then_inc(sig_ready, 1)
            act.wait_ge(set_ready, 1)

            def keep(t):
                rows = rows_of(t)
                for c in range(2):
                    act.wait_ge(h2T_done, 2 * t + c + 1)
                    if t >= 2:
                        act.wait_ge(log_done, t - 1)
                    nc.scalar.copy(h2T[:, t % 2, 512 * c:512 * c + 512].rearrange("p (k r) -> p k r", r=P)[:, :, 0:rows],
                                   bank[:, 4 + c, :].rearrange("p (k r) -> p k r", r=P)[:, :, 0:rows])\
                        .then_inc(h2T_kept, 1)

            def keep_logits(t):
                rows = rows_of(t)
                act.wait_ge(log_done, t + 1)
                nc.scalar.copy(s.logit[0:rows, t, :], bank[0:rows, 6 + t % 2, 0:NG + NE]).then_inc(log_kept, 1)

            for t in range(TT):
                rows = rows_of(t)
                act.wait_ge(x_ready, 2 * t + 2)
                if t >= 1:
                    act.wait_ge(sq_ready, t)
                nc.scalar.activation(junk[0:rows, :], row_of(t), ACT.Square,
                                     accum_out=ss[0:rows, t:t + 1]).then_inc(sq_ready, 1)
                act.wait_ge(mean_ready, t + 1)
                nc.scalar.activation(rr[0:rows, t:t + 1], rr[0:rows, t:t + 1], ACT.Sqrt).then_inc(root_ready, 1)
                if t >= 1:
                    keep(t - 1)
                if t >= 2:
                    keep_logits(t - 2)
            keep(TT - 1)
            keep_logits(TT - 2)
            keep_logits(TT - 1)

        @block.vector
        def _(dve):
            link = Chain(dve, chain_v)
            nc.vector.memset(s.logit[:, :, :], 0.0).then_inc(set_ready, 1)

            def split(hi, lo, v, ready):
                link(nc.vector.tensor_copy(hi.bitcast(F32R), v))
                link(nc.vector.tensor_tensor(lo.bitcast(F32R), v, hi, ALU.subtract), ready)

            def split_gates(j):
                dve.wait_ge(gate_in, 32 * (j + 1))
                for g in range(2):
                    split(gh[:, j % 2, g, :, :], gl[:, j % 2, g, :, :], gw[:, g, :, :], gate_split)

            for k in range(KD):
                split(hTh[:, k, :], hTl[:, k, :], s.hT[:, k, :], hT_split)
            split_gates(0)
            for j in range(NCH):
                if j + 1 < NCH:
                    split_gates(j + 1)
                for i in (0, 1):
                    dve.wait_ge(prod_done, 4 * j + 3 + i)
                    dve.wait_ge(sig_ready, 2 * j + i + 1)
                    dst = (uT[:, j, :] if i == 0 else part[:, :]).rearrange("p (b r) -> p b r", b=2)
                    link(nc.vector.tensor_tensor(dst, sg[:, j % 2, i, :].rearrange("p (b r) -> p b r", b=2),
                                                 bank[:, 4 + 2 * i:6 + 2 * i, 0:HALF], ALU.mult), mul_done)
                link(nc.vector.tensor_tensor(uT[:, j, :], uT[:, j, :], part[:, :], ALU.add), u_ready)
            dve.wait_ge(x_in, 32)
            dve.wait_ge(gf_in, 16)

            def add(t):
                rows = rows_of(t)
                for half in range(2):
                    n = 2 * t + half
                    dve.wait_ge(out_done, n + 1)
                    part_x = row_of(t)[:, half * 512:half * 512 + 512]
                    link(nc.vector.tensor_tensor(part_x, part_x, bank[0:rows, n % 4, :], ALU.add), x_ready)

            def norm(t):
                rows = rows_of(t)
                dve.wait_ge(sq_ready, t + 1)
                link(nc.vector.tensor_scalar(rr[0:rows, t:t + 1], ss[0:rows, t:t + 1], 1.0 / D, EPS, ALU.mult, ALU.add),
                     mean_ready)
                dve.wait_ge(root_ready, t + 1)
                link(nc.vector.reciprocal(rr[0:rows, t:t + 1], rr[0:rows, t:t + 1]))
                if t >= 2:
                    dve.wait_ge(h2T_done, 2 * (t - 1))
                    dve.wait_ge(h2_stored[t % 2], 16 * (t // 2))
                nc.vector.scalar_tensor_tensor(h2[0:rows, t % 2, :], row_of(t), rr[0:rows, t:t + 1],
                                               gf[0:rows, :], ALU.mult, ALU.mult).then_inc(h2_ready, 1)

            for t in range(TT):
                add(t)
                norm(t)


def route(nc, s, a):
    MAXK = -(-NTOK // BLK)
    with ExitStack() as ctx:
        def sb(name, shape, dt=F32):
            return ctx.enter_context(nc.sbuf_tensor(name, shape, dt))

        def sem(name):
            return nc.alloc_semaphore(name)

        bias = sb("router_bias", [P, NG + NE])
        top = sb("rt_top", [P, TT])
        place = sb("rt_place", [P, TT])
        gsum, gprob = sb("rt_gsum", [P, TT]), sb("rt_gprob", [P, TT])
        gex, geq, gone = (sb("rt_" + n, [P, TT, NG]) for n in ("gexp", "geq", "gone"))
        spread = sb("rt_spread", [P, TT, NE])
        elog, eeq = sb("rt_elog", [P, TT, EPG]), sb("rt_eeq", [P, TT, EPG])
        one = [sb(f"rt_one{k}", [P, TT, EPG]) for k in range(2)]
        m = [sb(f"rt_m{k}", [P, TT]) for k in range(2)]
        E = [sb(f"rt_E{k}", [P, TT, NE]) for k in range(2)]
        both = sb("rt_both", [P, TT, NE])
        ratio, denom = sb("rt_ratio", [P, TT]), sb("rt_denom", [P, TT])
        base = sb("rt_base", [P, TT + 1, NE])
        over = sb("rt_over", [P, NE, MAXK])
        nblk = sb("rt_nblk", [P, NE])
        cs = sb("rt_cumsum", [P, 2, NE])
        slotf = sb("rt_slotf", [P, 2, TT])
        le = sb("rt_le", [1, MAXB, NE])
        bef = sb("rt_bef", [1, MAXB])
        npf, npx = sb("rt_npf", [1, 1]), sb("rt_npx", [1, MAXB // 2])
        ids = sb("rt_ids", [P, TT, TABW], I32)
        bias_in = sem("rt_bias_in")
        gsub_ready, gexp_ready = sem("rt_group_sub_ready"), sem("rt_group_exp_ready")
        both_ready, sum_done = sem("rt_both_ready"), sem("rt_sum_done")
        slots_ready, scattered = sem("rt_slots_ready"), sem("rt_scattered")
        chain_v = sem("rt_vector_chain")
        block = ctx.enter_context(nc.Block())
        bank = s.bank

        @block.sync
        def _(sp):
            sp.dma_start(bias[:, 0:NG], a["b_grp"].to_broadcast([P, NG])).then_inc(bias_in, 16)
            sp.dma_start(bias[:, NG:], a["b_exp"].to_broadcast([P, NE])).then_inc(bias_in, 16)

        @block.scalar
        def _(act):
            act.wait_ge(gsub_ready, 1)
            nc.scalar.activation(gex[:, :, :], gex[:, :, :], ACT.Exp).then_inc(gexp_ready, 1)
            act.wait_ge(gsub_ready, 2)
            nc.scalar.activation(ratio[:, :], ratio[:, :], ACT.Exp).then_inc(gexp_ready, 1)

        @block.tensor
        def _(pe):
            pe.wait_ge(both_ready, 1)
            flat = both[:, :, :].rearrange("p t e -> p (t e)")
            nc.tensor.matmul(bank[:, 0, 0:TT * NE], const(s, "before"), flat, start=True, stop=True)
            nc.tensor.matmul(bank[:, 1, 0:TT * NE], s.ones[:, :], flat, start=True, stop=True).then_inc(sum_done, 1)

        @block.vector
        def _(dve):
            link = Chain(dve, chain_v)

            def first_of(eq, n, down, out):
                link(nc.vector.tensor_tensor(eq[:, :, :], eq[:, :, :],
                                             down.unsqueeze(1).to_broadcast([P, TT, n]), ALU.mult))
                link(nc.vector.reduce_max(place[:, :], eq[:, :, :], AX.X))
                link(nc.vector.tensor_tensor(out[:, :, :], eq[:, :, :],
                                             place[:, :].unsqueeze(2).to_broadcast([P, TT, n]), ALU.is_equal))

            def largest(v, n, down, eq, mx, out):
                link(nc.vector.reduce_max(mx[:, :], v, AX.X))
                link(nc.vector.tensor_tensor(eq[:, :, :], v, mx[:, :].unsqueeze(2).to_broadcast([P, TT, n]),
                                             ALU.is_equal))
                first_of(eq, n, down, out)

            dve.wait_ge(bias_in, 32)
            link(nc.vector.tensor_tensor(s.logit[:, :, :], s.logit[:, :, :],
                                         bias[:, :].unsqueeze(1).to_broadcast([P, TT, NG + NE]), ALU.add))
            G = s.logit[:, :, 0:NG]
            largest(G, NG, const(s, "down")[:, EPG - NG:EPG], geq, top, gone)
            link(nc.vector.tensor_tensor(gex[:, :, :], G, top[:, :].unsqueeze(2).to_broadcast([P, TT, NG]),
                                         ALU.subtract), gsub_ready)
            link(nc.vector.tensor_tensor(spread[:, :, :].rearrange("p t (g e) -> p t g e", e=EPG),
                                         s.logit[:, :, NG:].rearrange("p t (g e) -> p t g e", e=EPG),
                                         gone[:, :, :].unsqueeze(3).to_broadcast([P, TT, NG, EPG]), ALU.mult))
            link(nc.vector.reduce_sum(elog[:, :, :], spread[:, :, :].rearrange("p t (g e) -> p t e g", e=EPG), AX.X))
            for k in range(2):
                largest(elog[:, :, :], EPG, const(s, "down"), eeq, m[k], one[k])
                if k == 0:
                    link(nc.vector.scalar_tensor_tensor(elog[:, :, :], one[0][:, :, :], PICKED, elog[:, :, :],
                                                        ALU.mult, ALU.add))
                link(nc.vector.tensor_tensor(E[k][:, :, :].rearrange("p t (g e) -> p t g e", e=EPG),
                                             gone[:, :, :].unsqueeze(3).to_broadcast([P, TT, NG, EPG]),
                                             one[k][:, :, :].unsqueeze(2).to_broadcast([P, TT, NG, EPG]), ALU.mult))
                link(nc.vector.tensor_tensor(E[k][:, :, :], E[k][:, :, :],
                                             const(s, "real").unsqueeze(2).to_broadcast([P, TT, NE]), ALU.mult))
            link(nc.vector.tensor_tensor(ratio[:, :], m[1][:, :], m[0][:, :], ALU.subtract), gsub_ready)
            link(nc.vector.tensor_tensor(both[:, :, :], E[0][:, :, :], E[1][:, :, :], ALU.add), both_ready)
            dve.wait_ge(gexp_ready, 2)
            link(nc.vector.reduce_sum(gsum[:, :], gex[:, :, :], AX.X))
            link(nc.vector.scalar_tensor_tensor(denom[:, :], ratio[:, :], 1.0, gsum[:, :], ALU.add, ALU.mult))
            link(nc.vector.reciprocal(s.w12[:, 0, :], denom[:, :]))
            link(nc.vector.tensor_tensor(s.w12[:, 1, :], s.w12[:, 0, :], ratio[:, :], ALU.mult))
            dve.wait_ge(sum_done, 1)
            tot = bank[:, 1, 0:TT * NE].rearrange("p (t e) -> p t e", e=NE)
            link(nc.vector.memset(base[:, 0, :], 0.0))
            for t in range(TT):
                link(nc.vector.tensor_tensor(base[:, t + 1, :], base[:, t, :], tot[:, t, :], ALU.add))
            steps = const(s, "blocks")[:, 0:MAXK].unsqueeze(1).to_broadcast([P, NE, MAXK])
            link(nc.vector.tensor_scalar(nblk[:, :], base[:, TT, :], 1.0 / BLK, None, ALU.mult))
            link(nc.vector.tensor_tensor(over[:, :, :], nblk[:, :].unsqueeze(2).to_broadcast([P, NE, MAXK]),
                                         steps, ALU.is_gt))
            link(nc.vector.reduce_sum(nblk[:, :], over[:, :, :], AX.X))
            link(nc.vector.tensor_copy(cs[:, 0, :], nblk[:, :]))
            side, w = 0, 1
            while w < NE:
                link(nc.vector.tensor_copy(cs[:, 1 - side, 0:w], cs[:, side, 0:w]))
                link(nc.vector.tensor_tensor(cs[:, 1 - side, w:], cs[:, side, w:], cs[:, side, 0:NE - w], ALU.add))
                side, w = 1 - side, 2 * w
            ends = cs[:, side, :]
            link(nc.vector.tensor_tensor(nblk[:, :], ends, nblk[:, :], ALU.subtract))
            link(nc.vector.tensor_scalar(nblk[:, :], nblk[:, :], float(BLK), None, ALU.mult))
            link(nc.vector.tensor_tensor(both[:, :, :], bank[:, 0, 0:TT * NE].rearrange("p (t e) -> p t e", e=NE),
                                         base[:, 0:TT, :], ALU.add))
            link(nc.vector.tensor_tensor(both[:, :, :], both[:, :, :],
                                         nblk[:, :].unsqueeze(1).to_broadcast([P, TT, NE]), ALU.add))
            for k in range(2):
                link(nc.vector.tensor_tensor(spread[:, :, :], both[:, :, :], E[k][:, :, :], ALU.mult))
                link(nc.vector.reduce_sum(slotf[:, k, :], spread[:, :, :], AX.X))
            link(nc.vector.tensor_copy(s.slot[:, :, :], slotf[:, :, :]))
            link(nc.vector.tensor_copy(ids[:, :, :], const(s, "token").unsqueeze(2).to_broadcast([P, TT, TABW])),
                 slots_ready)
            link(nc.vector.tensor_tensor(le[:, :, :], ends[0:1, :].unsqueeze(1).to_broadcast([1, MAXB, NE]),
                                         const(s, "blocks", 1).unsqueeze(2).to_broadcast([1, MAXB, NE]), ALU.is_le))
            link(nc.vector.reduce_sum(bef[:, :], le[:, :, :], AX.X))
            link(nc.vector.tensor_scalar(bef[:, :], bef[:, :], float(NE - 1), None, ALU.min))
            link(nc.vector.tensor_copy(s.be[:, :], bef[:, :]))
            link(nc.vector.tensor_tensor(npx[:, :], const(s, "evens", 1), ends[0:1, NE - 1:NE]
                                         .to_broadcast([1, MAXB // 2]), ALU.is_lt))
            link(nc.vector.reduce_sum(npf[:, :], npx[:, :], AX.X))
            link(nc.vector.tensor_copy(s.npair[:, :], npf[:, :]))

        @block.gpsimd
        def _(pool):
            pool.wait_ge(slots_ready, 1)
            for k in range(2):
                for t in range(TT):
                    rows = rows_of(t)
                    pool.indirect_dma_start(s.slots, bass.IndirectOffsetOnAxis(ap=s.slot[0:rows, k, t:t + 1], axis=0),
                                            ids[0:rows, t, :], None).then_inc(scattered, 16)
            pool.wait_ge(scattered, 16 * 2 * TT)


def experts(nc, s, a):
    w_gate = a["w_e_gate"][0].rearrange("e (k p) n -> p e k n", p=P)
    w_up = a["w_e_up"][0].rearrange("e (k p) n -> p e k n", p=P)
    w_down = a["w_e_down"][0].rearrange("e (f p) n -> p e f n", p=P)
    KF = DE // P
    KH = KD // 2
    PAIR = 2 * BLK
    MAXP = MAXB // 2
    with ExitStack() as ctx:
        def sb(name, shape, dt=F32):
            return ctx.enter_context(nc.sbuf_tensor(name, shape, dt))

        def sem(name):
            return nc.alloc_semaphore(name)

        wgu = sb("w_gate_up", [P, 2, 2, KH, 2 * DE])
        wd = sb("w_down", [P, 2, KF, D])
        ids = sb("ids", [PAIR, MAXP + 1], I32)
        id1 = sb("id1", [PAIR, 1], I32)
        xg = sb("xg", [PAIR, D])
        xT = sb("xT", [P, KD, PAIR])
        sgm, hid = sb("sgm", [PAIR, DE]), sb("hid", [PAIR, DE])
        hidT = sb("hidT", [P, KF, PAIR])
        y = sb("y", [PAIR, D])
        ids_in, id_ready, x_in = sem("ex_ids_in"), sem("ex_id_ready"), sem("ex_x_in")
        part_in = [sem("ex_first_part_in"), sem("ex_last_part_in")]
        part_done = [sem("ex_first_part_done"), sem("ex_last_part_done")]
        down_in, y_done = sem("ex_down_in"), sem("ex_y_done")
        xT_done, xT_kept = sem("ex_xT_done"), sem("ex_xT_kept")
        sig_ready, gated, hid_ready = sem("ex_sigmoid_ready"), sem("ex_gated"), sem("ex_hidden_ready")
        hT_done, hT_kept = sem("ex_hidT_done"), sem("ex_hidT_kept")
        y_ready, y_kept, y_free, y_stored = sem("ex_y_ready"), sem("ex_y_kept"), sem("ex_y_free"), sem("ex_y_stored")
        carry = sem("ex_carry")
        block = ctx.enter_context(nc.Block())
        bank = s.bank

        @block.sync
        def _(sp):
            with nc.allow_non_contiguous_dma(reason="one word of each row"):
                sp.dma_start(ids[:, 0:MAXP], s.slots.rearrange("(b r) w -> r b w", r=PAIR)[:, :, 0:1]
                             .rearrange("r b o -> r (b o)")).then_inc(ids_in, 16)
            turns = sp.value_load(s.npair[0:1, 0:1], min_val=1, max_val=MAXP)
            with sp.Fori(0, turns) as i:
                e = [sp.value_load(s.be[0:1, bass.ds(2 * i + u, 1)], min_val=0, max_val=NE - 1) for u in range(2)]
                for part in range(2):
                    ks = slice(part * KH, (part + 1) * KH)
                    sp.wait_ge(part_done[part], i + 1)
                    for u in range(2):
                        for w, c in ((w_gate, 0), (w_up, DE)):
                            sp.dma_start(wgu[:, u, part, :, c:c + DE], w[:, bass.ds(e[u], 1), ks, :]
                                         .rearrange("p e k n -> p (e k) n")).then_inc(part_in[part], 16)
                sp.wait_ge(y_done, i + 1)
                for u in range(2):
                    sp.dma_start(wd[:, u, :, :], w_down[:, bass.ds(e[u], 1), :, :]
                                 .rearrange("p e f n -> p (e f) n")).then_inc(down_in, 16)

        @block.gpsimd
        def _(pool):
            nc.gpsimd.memset(ids[:, MAXP:MAXP + 1], 0).then_inc(ids_in, 16)
            pool.wait_ge(ids_in, 32)
            turns = pool.value_load(s.npair[0:1, 0:1], min_val=1, max_val=MAXP)

            def gather(turn, column):
                nc.gpsimd.tensor_copy(id1[:, :], column).then_inc(id_ready, 1)
                pool.wait_ge(id_ready, turn + 1)
                pool.sem_inc(carry, 1)
                pool.indirect_dma_start(xg[:, :], None, s.h2,
                                        bass.IndirectOffsetOnAxis(ap=id1[:, 0:1], axis=0)).then_inc(x_in, 16)

            gather(0, ids[:, 0:1])
            with pool.Fori(0, turns) as i:
                pool.wait_ge(xT_done, i + 1)
                gather(i + 1, ids[:, bass.ds(i + 1, 1)])
                pool.wait_ge(y_ready, i + 1)
                pool.dma_start(s.y[bass.ds(i * PAIR, PAIR), :], y[:, :]).then_inc(y_stored, 16)
                pool.wait_ge(y_stored, 16 * i + 16)
                pool.sem_inc(y_free, 1)
            pool.wait_ge(x_in, turns * 16 + 16)
            pool.sem_inc(carry, 1)

        @block.tensor
        def _(pe):
            for done in (*part_done, y_done):
                pe.sem_inc(done, 1)
            turns = pe.value_load(s.npair[0:1, 0:1], min_val=1, max_val=MAXP)
            with pe.Fori(0, turns) as i:
                pe.wait_ge(x_in, 16 * i + 16)
                pe.sem_inc(carry, 1)
                for k in range(KD):
                    last = nc.tensor.transpose(bank[:, k // 4, k % 4 * PAIR:(k % 4 + 1) * PAIR],
                                               xg[:, k * P:(k + 1) * P], const(s, "ident"))
                last.then_inc(xT_done, 1)
                pe.wait_ge(xT_kept, i + 1)
                for part in range(2):
                    pe.wait_ge(part_in[part], 64 * i + 64)
                    for k in range(KH):
                        kk = part * KH + k
                        for u in range(2):
                            r = slice(u * BLK, (u + 1) * BLK)
                            last = nc.tensor.matmul(bank[r, 2, :], xT[:, kk, r], wgu[:, u, part, k, :],
                                                    start=(kk == 0), stop=(kk == KD - 1))
                    last.then_inc(part_done[part], 1)
                pe.wait_ge(hid_ready, i + 1)
                pe.sem_inc(carry, 1)
                for f in range(KF):
                    last = nc.tensor.transpose(bank[:, 3, f * PAIR:(f + 1) * PAIR], hid[:, f * P:(f + 1) * P],
                                               const(s, "ident"))
                last.then_inc(hT_done, 1)
                pe.wait_ge(down_in, 32 * i + 32)
                pe.wait_ge(y_kept, i + 1)
                pe.wait_ge(hT_kept, i + 1)
                for half in range(2):
                    for f in range(KF):
                        for u in range(2):
                            r = slice(u * BLK, (u + 1) * BLK)
                            last = nc.tensor.matmul(bank[r, 4 + half, :], hidT[:, f, r],
                                                    wd[:, u, f, half * 512:half * 512 + 512],
                                                    start=(f == 0), stop=(f == KF - 1))
                last.then_inc(y_done, 1)

        @block.scalar
        def _(act):
            act.sem_inc(y_kept, 1)
            act.sem_inc(y_free, 1)
            turns = act.value_load(s.npair[0:1, 0:1], min_val=1, max_val=MAXP)
            act.sem_inc(carry, 1)
            with act.Fori(0, turns) as i:
                act.wait_ge(part_done[1], i + 2)
                nc.scalar.activation(sgm[:, :], bank[:, 2, 0:DE], ACT.Sigmoid).then_inc(sig_ready, 1)
                act.wait_ge(y_done, i + 2)
                act.wait_ge(y_free, i + 1)
                nc.scalar.copy(y[:, :].rearrange("p (b n) -> p b n", b=2), bank[:, 4:6, :]).then_inc(y_ready, 1)
                act.wait_ge(y_ready, i + 1)
                act.sem_inc(y_kept, 1)

        @block.vector
        def _(dve):
            turns = dve.value_load(s.npair[0:1, 0:1], min_val=1, max_val=MAXP)
            with dve.Fori(0, turns) as i:
                dve.wait_ge(xT_done, i + 1)
                nc.vector.tensor_copy(xT[:, :, :].rearrange("p (b k) r -> p b (k r)", b=2), bank[:, 0:2, :])\
                    .then_inc(xT_kept, 1)
                dve.wait_ge(sig_ready, i + 1)
                nc.vector.tensor_tensor(sgm[:, :], sgm[:, :], bank[:, 2, 0:DE], ALU.mult).then_inc(gated, 1)
                dve.wait_ge(gated, i + 1)
                nc.vector.tensor_tensor(hid[:, :], sgm[:, :], bank[:, 2, DE:], ALU.mult).then_inc(hid_ready, 1)
                dve.wait_ge(hT_done, i + 1)
                nc.vector.tensor_copy(hidT[:, :, :].rearrange("p f r -> p (f r)"), bank[:, 3, 0:KF * PAIR])\
                    .then_inc(hT_kept, 1)


def combine(nc, s, a, o):
    with ExitStack() as ctx:
        def sb(name, shape, dt=F32):
            return ctx.enter_context(nc.sbuf_tensor(name, shape, dt))

        def sem(name):
            return nc.alloc_semaphore(name)

        x = sb("x_cb", [P, TT, D])
        y = [sb(f"y_cb{k}", [P, TT, D]) for k in range(2)]
        gl = sb("g_last", [P, D])
        junk = sb("junk_cb", [P, D])
        ss, rr = sb("ss_cb", [P, TT]), sb("rr_cb", [P, TT])
        x_in = [sem(f"cb_x_in{t}") for t in range(TT)]
        y_in = [[sem(f"cb_y_in{k}{t}") for t in range(TT)] for k in range(2)]
        g_in, stored = sem("cb_g_in"), sem("cb_stored")
        x_ready, sq_ready = sem("cb_x_ready"), sem("cb_square_ready")
        mean_ready, root_ready, y_ready = sem("cb_mean_ready"), sem("cb_root_ready"), sem("cb_y_ready")
        chain_v = sem("cb_vector_chain")
        block = ctx.enter_context(nc.Block())

        @block.gpsimd
        def _(pool):
            for t in range(TT):
                rows = rows_of(t)
                for k in range(2):
                    pool.indirect_dma_start(y[k][0:rows, t, :], None, s.y,
                                            bass.IndirectOffsetOnAxis(ap=s.slot[0:rows, k, t:t + 1], axis=0))\
                        .then_inc(y_in[k][t], 16)

        @block.sync
        def _(sp):
            for t in range(TT):
                rows = rows_of(t)
                sp.dma_start(x[0:rows, t, :], s.x1[t * P:t * P + rows, :]).then_inc(x_in[t], 16)
            sp.dma_start(gl[:, :], a["g_final"].to_broadcast([P, D])).then_inc(g_in, 16)
            for t in range(TT):
                rows = rows_of(t)
                sp.wait_ge(x_in[t], 16)
                sp.wait_ge(y_ready, t + 1)
                dst = o["y_prompt"][t * P:(t + 1) * P, :] if t < TP else o["y_sample"]
                sp.dma_start(dst, x[0:rows, t, :]).then_inc(stored, 16)
            sp.wait_ge(stored, 16 * TT)

        @block.scalar
        def _(act):
            for t in range(TT):
                rows = rows_of(t)
                act.wait_ge(x_ready, t + 1)
                if t >= 1:
                    act.wait_ge(sq_ready, t)
                nc.scalar.activation(junk[0:rows, :], x[0:rows, t, :], ACT.Square,
                                     accum_out=ss[0:rows, t:t + 1]).then_inc(sq_ready, 1)
                act.wait_ge(mean_ready, t + 1)
                nc.scalar.activation(rr[0:rows, t:t + 1], rr[0:rows, t:t + 1], ACT.Sqrt).then_inc(root_ready, 1)

        @block.vector
        def _(dve):
            link = Chain(dve, chain_v)
            dve.wait_ge(g_in, 16)
            for t in range(TT):
                rows = rows_of(t)
                xs = x[0:rows, t, :]
                dve.wait_ge(x_in[t], 16)
                for k in range(2):
                    dve.wait_ge(y_in[k][t], 16)
                    link(nc.vector.scalar_tensor_tensor(xs, y[k][0:rows, t, :], s.w12[0:rows, k, t:t + 1], xs,
                                                        ALU.mult, ALU.add), x_ready if k else None)
                dve.wait_ge(sq_ready, t + 1)
                link(nc.vector.tensor_scalar(rr[0:rows, t:t + 1], ss[0:rows, t:t + 1], 1.0 / D, EPS, ALU.mult, ALU.add),
                     mean_ready)
                dve.wait_ge(root_ready, t + 1)
                link(nc.vector.reciprocal(rr[0:rows, t:t + 1], rr[0:rows, t:t + 1]))
                nc.vector.scalar_tensor_tensor(xs, xs, rr[0:rows, t:t + 1], gl[0:rows, :], ALU.mult, ALU.mult)\
                    .then_inc(y_ready, 1)


CACHES = ["cache_k_a", "cache_v_a", "cache_k_idx", "cache_k_b", "cache_v_b"]
INPUTS = ["x_prompt", "x_sample", *CACHES, "page_table", "w_in", "w_br_a", "w_br_b", "w_out", "g_mix",
          "g_ffn", "w_grp", "b_grp", "w_exp", "b_exp", "w_e_gate", "w_e_up", "w_e_down", "g_final"]
ROWS = {"k_a": (2, HD), "v_a": (2, HD), "k_idx": (HD,), "k_b": (H, HD), "v_b": (H, HD)}
OUTPUTS = [("y_prompt", (1, SEQ, D)), ("y_sample", (NB, NQ, D))]
OUTPUTS += [(n + "_p", (1, 1, SEQ, *r)) for n, r in ROWS.items()]
OUTPUTS += [(n + "_s", (1, NB, NQ, *r)) for n, r in ROWS.items()]


def kernel(**inputs):
    import concourse.bacc as bacc
    from concourse.bass_utils import run_bass_kernel_spmd

    nc = bacc.Bacc("TRN2", target_bir_lowering=False, num_devices=1)
    arrays, args, outs = {}, {}, {}
    for name in INPUTS:
        v = np.ascontiguousarray(inputs[name])
        arrays["in_" + name] = v
        args[name] = nc.dram_tensor("in_" + name, v.shape, mybir.dt.from_np(v.dtype), kind="ExternalInput").ap()
    arrays["in_consts"] = CONSTS
    args["consts"] = nc.dram_tensor("in_consts", CONSTS.shape, F32, kind="ExternalInput").ap()
    args["g_final"] = args["g_final"].unsqueeze(0)
    for i, (name, shape) in enumerate(OUTPUTS):
        ap = nc.dram_tensor(f"out_{i}", shape, F32, kind="ExternalOutput").ap()
        if name.startswith("y_"):
            outs[name] = ap.rearrange("a b d -> (a b) d")
        elif len(shape) == 5:
            outs[name] = ap.rearrange("a b t h d -> (a b t) (h d)")
        else:
            outs[name] = ap.rearrange("a b t d -> (a b t) d")
    build(nc, args, outs)
    r = run_bass_kernel_spmd(nc, [arrays], core_ids=[0])
    return tuple(r.results[0][f"out_{i}"] for i in range(len(OUTPUTS)))
```
